# Optimizing a Trainium2 kernel written in Bass

```python
import math
import jax, jax.numpy as jnp
from jax import lax
import numpy as np
import jax
import jax.numpy as jnp

D_MODEL = 1024
BATCH = 1
SEQ = 512
DEPTH = 1

CHUNK = 64
Q_BLOCK = 128
N_MEM = 256
MIX_WIDTH = D_MODEL
FOX_WIDTH = MIX_WIDTH // 2
HGRN_WIDTH = MIX_WIDTH - FOX_WIDTH
FOX_HEAD_DIM = 64
FOX_HEADS = FOX_WIDTH // FOX_HEAD_DIM
HGRN_KEY_DIM = 128
HGRN_HEADS = HGRN_WIDTH // HGRN_KEY_DIM
HGRN_VAL_DIM = HGRN_WIDTH // HGRN_HEADS
X_HEADS = 4
X_HEAD_DIM = D_MODEL // X_HEADS
D_FF = 4 * D_MODEL
EPS = 1e-6
SPLITS = (FOX_WIDTH, FOX_WIDTH, FOX_WIDTH, FOX_HEADS, HGRN_WIDTH, HGRN_WIDTH, HGRN_WIDTH, HGRN_WIDTH)
IN_COLS = sum(SPLITS)


def rmsnorm(x, g):
    xf = x.astype(jnp.float32)
    y = xf * lax.rsqrt(jnp.mean(xf * xf, axis=-1, keepdims=True) + EPS)
    return (y * g.astype(jnp.float32)).astype(x.dtype)

def fox_attention(q, k, v, log_f):
    b_, h_, s_, d_ = q.shape
    nb = s_ // Q_BLOCK
    scale = 1.0 / math.sqrt(d_)
    F = jnp.cumsum(log_f, axis=-1)
    qb = q.reshape(b_, h_, nb, Q_BLOCK, d_).transpose(2, 0, 1, 3, 4)
    Fb = F.reshape(b_, h_, nb, Q_BLOCK).transpose(2, 0, 1, 3)
    pos = jnp.arange(s_, dtype=jnp.int32).reshape(nb, Q_BLOCK)
    key_pos = jnp.arange(s_, dtype=jnp.int32)

    def block(args):
        qi, Fi, pi = args
        s = jnp.einsum('bhqd,bhkd->bhqk', qi, k).astype(jnp.float32) * scale
        s = s + Fi[..., None] - F[:, :, None, :]
        mask = pi[:, None] >= key_pos[None, :]
        s = jnp.where(mask, s, -jnp.inf)
        p = jax.nn.softmax(s, axis=-1)
        return jnp.einsum('bhqk,bhkd->bhqd', p.astype(v.dtype), v)

    out = lax.map(block, (qb, Fb, pos))
    return out.transpose(1, 2, 0, 3, 4).reshape(b_, h_, s_, d_)

def hgrn2_chunkwise(q, f_logit, i, lb):
    b_, s_, _ = q.shape
    n_c = s_ // CHUNK

    def heads(t, d):
        return t.astype(jnp.float32).reshape(b_, n_c, CHUNK, HGRN_HEADS, d).transpose(1, 0, 3, 2, 4)

    lbh = lb.astype(jnp.float32).reshape(HGRN_HEADS, 1, HGRN_KEY_DIM)
    f = lbh + (1.0 - lbh) * jax.nn.sigmoid(heads(f_logit, HGRN_KEY_DIM))
    kk = 1.0 - f
    g = jnp.log(f)
    qq = jax.nn.silu(heads(q, HGRN_KEY_DIM))
    ii = heads(i, HGRN_VAL_DIM)
    causal = jnp.tril(jnp.ones((CHUNK, CHUNK), dtype=bool))

    def step(state, inp):
        qc, kc, ic, gc = inp
        bcum = jnp.cumsum(gc, axis=2)
        diff = bcum[:, :, :, None, :] - bcum[:, :, None, :, :]
        decay = jnp.exp(jnp.where(causal[:, :, None], diff, -jnp.inf))
        attn = jnp.einsum('bhtd,bhsd,bhtsd->bhts', qc, kc, decay)
        intra = jnp.einsum('bhts,bhsv->bhtv', attn, ic)
        inter = jnp.einsum('bhtd,bhdv->bhtv', qc * jnp.exp(bcum), state)
        b_last = bcum[:, :, -1]
        k_dec = kc * jnp.exp(b_last[:, :, None, :] - bcum)
        new_state = jnp.exp(b_last)[..., None] * state + jnp.einsum('bhsd,bhsv->bhdv', k_dec, ic)
        return new_state, intra + inter

    s0 = jnp.zeros((b_, HGRN_HEADS, HGRN_KEY_DIM, HGRN_VAL_DIM), jnp.float32)
    _, outs = lax.scan(step, s0, (qq, kk, ii, g))
    return outs.transpose(1, 0, 3, 2, 4).reshape(b_, s_, HGRN_HEADS, HGRN_VAL_DIM)

def memory_cross_attention(h, mem_n, w_q, w_kv, w_o):
    b_, s_, _ = h.shape
    m_ = mem_n.shape[1]
    q = (h @ w_q).reshape(b_, s_, X_HEADS, X_HEAD_DIM)
    kv = mem_n @ w_kv
    k, v = jnp.split(kv, 2, axis=-1)
    k = k.reshape(b_, m_, X_HEADS, X_HEAD_DIM)
    v = v.reshape(b_, m_, X_HEADS, X_HEAD_DIM)
    s = jnp.einsum('bshd,bmhd->bhsm', q, k).astype(jnp.float32) / math.sqrt(X_HEAD_DIM)
    p = jax.nn.softmax(s, axis=-1)
    o = jnp.einsum('bhsm,bmhd->bshd', p.astype(v.dtype), v).reshape(b_, s_, D_MODEL)
    return o @ w_o

def first_inputs(seed: int = 0) -> dict:
    key = jax.random.key(seed)
    ks = jax.random.split(key, 20)
    nrm = lambda k, shape, s: jax.random.normal(k, shape, jnp.float32) * s
    gain = lambda k, shape: 1.0 + 0.02 * jax.random.normal(k, shape, jnp.float32)
    return {
        "x": nrm(ks[0], (BATCH, SEQ, D_MODEL), 1.0),
        "mem": nrm(ks[1], (BATCH, N_MEM, D_MODEL), 1.0),
        "norm_mix_g": gain(ks[2], (DEPTH, D_MODEL)),
        "w_in": nrm(ks[3], (DEPTH, D_MODEL, IN_COLS), D_MODEL ** -0.5),
        "fox_f_bias": 1.0 + 0.1 * jax.random.normal(ks[4], (DEPTH, FOX_HEADS), jnp.float32),
        "hgrn_lb_logits": nrm(ks[5], (DEPTH + 1, HGRN_WIDTH), 0.1),
        "hgrn_norm_g": gain(ks[6], (DEPTH, HGRN_VAL_DIM)),
        "w_out": nrm(ks[7], (DEPTH, MIX_WIDTH, D_MODEL), MIX_WIDTH ** -0.5),
        "norm_x_g": gain(ks[8], (DEPTH, D_MODEL)),
        "norm_mem_g": gain(ks[9], (DEPTH, D_MODEL)),
        "w_xq": nrm(ks[10], (DEPTH, D_MODEL, D_MODEL), D_MODEL ** -0.5),
        "w_xkv": nrm(ks[11], (DEPTH, D_MODEL, 2 * D_MODEL), D_MODEL ** -0.5),
        "w_xo": nrm(ks[12], (DEPTH, D_MODEL, D_MODEL), D_MODEL ** -0.5),
        "norm_ff_g": gain(ks[13], (DEPTH, D_MODEL)),
        "w1": nrm(ks[14], (DEPTH, D_MODEL, D_FF), D_MODEL ** -0.5),
        "w2": nrm(ks[15], (DEPTH, D_FF, D_MODEL), D_FF ** -0.5),
        "final_norm_g": gain(ks[16], (D_MODEL,)),
    }

def first_block(x, mem, norm_mix_g, w_in, fox_f_bias, hgrn_lb_logits, hgrn_norm_g, w_out,
              norm_x_g, norm_mem_g, w_xq, w_xkv, w_xo, norm_ff_g, w1, w2, final_norm_g):
    b_, s_, _ = x.shape
    lbs = jnp.cumsum(jax.nn.softmax(hgrn_lb_logits.astype(jnp.float32), axis=0), axis=0)
    split_idx = list(np.cumsum(SPLITS)[:-1])
    h = x
    for l in range(DEPTH):
        hn = rmsnorm(h, norm_mix_g[l])
        proj = hn @ w_in[l]
        fq, fk, fv, ff, gq, gf, gi, gg = jnp.split(proj, split_idx, axis=-1)
        to_heads = lambda t: t.reshape(b_, s_, FOX_HEADS, FOX_HEAD_DIM).transpose(0, 2, 1, 3)
        log_f = jax.nn.log_sigmoid((ff + fox_f_bias[l]).astype(jnp.float32)).transpose(0, 2, 1)
        fox_out = fox_attention(to_heads(fq), to_heads(fk), to_heads(fv), log_f)
        fox_out = fox_out.transpose(0, 2, 1, 3).reshape(b_, s_, FOX_WIDTH)
        rec = hgrn2_chunkwise(gq, gf, gi, lbs[l])
        rec = rmsnorm(rec, hgrn_norm_g[l]) * jax.nn.silu(
            gg.astype(jnp.float32).reshape(b_, s_, HGRN_HEADS, HGRN_VAL_DIM))
        rec = rec.reshape(b_, s_, HGRN_WIDTH).astype(h.dtype)
        h = h + jnp.concatenate([fox_out, rec], axis=-1) @ w_out[l]
        mem_n = rmsnorm(mem, norm_mem_g[l])
        h = h + memory_cross_attention(rmsnorm(h, norm_x_g[l]), mem_n, w_xq[l], w_xkv[l], w_xo[l])
        u = rmsnorm(h, norm_ff_g[l]) @ w1[l]
        h = h + jnp.square(jax.nn.relu(u)) @ w2[l]
    return rmsnorm(h, final_norm_g)


CONV_CH = D_MODEL
CONV_K = 31
D_INNER = 2 * D_MODEL
HEAD_DIM = 64
N_HEADS = D_INNER // HEAD_DIM
N_GROUPS = 8
HEADS_PER_GROUP = N_HEADS // N_GROUPS
D_STATE = 128
SSM_CONV_K = 4
XBC_CH = D_INNER + 2 * N_GROUPS * D_STATE
FFN_HIDDEN = ((8 * D_MODEL // 3 + 255) // 256) * 256
RMS_EPS = 1e-6
LN_EPS = 1e-5

OFF_Z = 2 * CONV_CH
OFF_XBC = OFF_Z + D_INNER
OFF_DT = OFF_XBC + XBC_CH
OFF_GATE = OFF_DT + N_HEADS
IN_COLS_2 = OFF_GATE + 2 * D_MODEL


def rms_norm(x, g):
    xf = x.astype(jnp.float32)
    y = xf * lax.rsqrt(jnp.mean(xf * xf, axis=-1, keepdims=True) + RMS_EPS)
    return (y * g.astype(jnp.float32)).astype(x.dtype)

def layer_norm(x, g, b):
    xf = x.astype(jnp.float32)
    mu = jnp.mean(xf, axis=-1, keepdims=True)
    xc = xf - mu
    y = xc * lax.rsqrt(jnp.mean(xc * xc, axis=-1, keepdims=True) + LN_EPS)
    return (y * g.astype(jnp.float32) + b.astype(jnp.float32)).astype(x.dtype)

def causal_depthwise_conv(u, w, b):
    k, ch = w.shape
    y = lax.conv_general_dilated(
        u, w[:, None, :], window_strides=(1,), padding=[(k - 1, 0)],
        dimension_numbers=("NWC", "WIO", "NWC"), feature_group_count=ch)
    return y + b

def conformer_conv_branch(u_glu, glu_b, dw_w, dw_b, ln_g, ln_b, pw_w, pw_b):
    u = u_glu + glu_b
    val, gt = jnp.split(u, 2, axis=-1)
    v = val * jax.nn.sigmoid(gt)
    v = causal_depthwise_conv(v, dw_w, dw_b)
    v = jax.nn.silu(layer_norm(v, ln_g, ln_b))
    return v @ pw_w + pw_b

def ssd_chunked(x, dt, a, b_mat, c_mat, d_skip):
    bsz, seqlen = x.shape[0], x.shape[1]
    nc = seqlen // CHUNK
    G, R = N_GROUPS, HEADS_PER_GROUP
    x = x.reshape(bsz, nc, CHUNK, G, R, HEAD_DIM)
    dt = dt.reshape(bsz, nc, CHUNK, G, R)
    b_mat = b_mat.reshape(bsz, nc, CHUNK, G, D_STATE)
    c_mat = c_mat.reshape(bsz, nc, CHUNK, G, D_STATE)
    a_dt = jnp.transpose(dt * a.reshape(G, R), (0, 3, 4, 1, 2))
    a_cs = jnp.cumsum(a_dt, axis=-1)
    xdt = x * dt[..., None]
    causal = jnp.tril(jnp.ones((CHUNK, CHUNK), dtype=bool))
    seg = a_cs[..., :, None] - a_cs[..., None, :]
    decay_in = jnp.exp(jnp.where(causal, seg, -jnp.inf))
    cb = jnp.einsum("bclgn,bcsgn->bgcls", c_mat, b_mat)
    y_diag = jnp.einsum("bgcls,bgrcls,bcsgrp->bclgrp", cb, decay_in, xdt)
    decay_to_end = jnp.exp(a_cs[..., -1:] - a_cs)
    chunk_states = jnp.einsum("bclgn,bgrcl,bclgrp->bcgrpn", b_mat, decay_to_end, xdt)
    chunk_decay = jnp.exp(a_cs[..., -1])

    def step(carry, inp):
        s_c, dec_c = inp
        return carry * dec_c[..., None, None] + s_c, carry

    init = jnp.zeros((bsz, G, R, HEAD_DIM, D_STATE), jnp.float32)
    _, prev = lax.scan(step, init, (jnp.moveaxis(chunk_states, 1, 0),
                                    jnp.moveaxis(chunk_decay, -1, 0)))
    prev = jnp.moveaxis(prev, 0, 1)
    y_off = jnp.einsum("bclgn,bcgrpn,bgrcl->bclgrp", c_mat, prev, jnp.exp(a_cs))
    y = y_diag + y_off + x * d_skip.reshape(G, R)[..., None]
    return y.reshape(bsz, seqlen, N_HEADS * HEAD_DIM)

def ssd_branch(z, xbc, dt_raw, conv_w, conv_b, dt_bias, a_log, d_skip, norm_g, out_w):
    f32 = jnp.float32
    bsz, seqlen = z.shape[0], z.shape[1]
    xbc = jax.nn.silu(causal_depthwise_conv(xbc, conv_w, conv_b))
    gn = N_GROUPS * D_STATE
    xs = xbc[..., :D_INNER]
    bm = xbc[..., D_INNER:D_INNER + gn]
    cm = xbc[..., D_INNER + gn:]
    dt = jax.nn.softplus(dt_raw.astype(f32) + dt_bias.astype(f32))
    a = -jnp.exp(a_log.astype(f32))
    y = ssd_chunked(xs.astype(f32).reshape(bsz, seqlen, N_HEADS, HEAD_DIM), dt, a,
                    bm.astype(f32).reshape(bsz, seqlen, N_GROUPS, D_STATE),
                    cm.astype(f32).reshape(bsz, seqlen, N_GROUPS, D_STATE),
                    d_skip.astype(f32))
    y = y * jax.nn.silu(z.astype(f32))
    yg = y.reshape(bsz, seqlen, N_GROUPS, D_INNER // N_GROUPS)
    yg = yg * lax.rsqrt(jnp.mean(yg * yg, axis=-1, keepdims=True) + RMS_EPS)
    y = (yg.reshape(bsz, seqlen, D_INNER) * norm_g.astype(f32)).astype(z.dtype)
    return y @ out_w

def second_inputs(seed: int = 0) -> dict:
    key = jax.random.key(seed)
    ks = jax.random.split(key, 24)
    f32 = jnp.float32

    def nrm(k, shape, scale):
        return jax.random.normal(k, shape, f32) * scale

    def gain(k, n):
        return 1.0 + 0.05 * jax.random.normal(k, (DEPTH, n), f32)

    u = jax.random.uniform(ks[13], (DEPTH, N_HEADS), f32)
    dt0 = jnp.exp(u * (math.log(0.1) - math.log(1e-3)) + math.log(1e-3))
    dt_bias = dt0 + jnp.log(-jnp.expm1(-dt0))
    a_log = jnp.log(jax.random.uniform(ks[14], (DEPTH, N_HEADS), f32, 1.0, 16.0))
    return {
        "x": nrm(ks[0], (BATCH, SEQ, D_MODEL), 1.0),
        "mix_pre_g": gain(ks[1], D_MODEL),
        "w_in": nrm(ks[2], (DEPTH, D_MODEL, IN_COLS_2), D_MODEL ** -0.5),
        "gate_b": nrm(ks[3], (DEPTH, 2 * D_MODEL), 0.02),
        "glu_b": nrm(ks[4], (DEPTH, 2 * CONV_CH), 0.02),
        "conv_dw_w": nrm(ks[5], (DEPTH, CONV_K, CONV_CH), CONV_K ** -0.5),
        "conv_dw_b": nrm(ks[6], (DEPTH, CONV_CH), 0.02),
        "conv_ln_g": gain(ks[7], CONV_CH),
        "conv_ln_b": nrm(ks[8], (DEPTH, CONV_CH), 0.02),
        "conv_pw_w": nrm(ks[9], (DEPTH, CONV_CH, D_MODEL), CONV_CH ** -0.5),
        "conv_pw_b": nrm(ks[10], (DEPTH, D_MODEL), 0.02),
        "ssm_conv_w": nrm(ks[11], (DEPTH, SSM_CONV_K, XBC_CH), SSM_CONV_K ** -0.5),
        "ssm_conv_b": nrm(ks[12], (DEPTH, XBC_CH), 0.02),
        "dt_bias": dt_bias,
        "a_log": a_log,
        "d_skip": 1.0 + 0.1 * jax.random.normal(ks[15], (DEPTH, N_HEADS), f32),
        "ssm_norm_g": gain(ks[16], D_INNER),
        "ssm_out_w": nrm(ks[17], (DEPTH, D_INNER, D_MODEL), D_INNER ** -0.5),
        "w_out": nrm(ks[18], (DEPTH, D_MODEL, D_MODEL), D_MODEL ** -0.5),
        "mix_post_g": gain(ks[19], D_MODEL),
        "ffn_pre_g": gain(ks[20], D_MODEL),
        "w_gate_up": nrm(ks[21], (DEPTH, D_MODEL, 2 * FFN_HIDDEN), D_MODEL ** -0.5),
        "w_down": nrm(ks[22], (DEPTH, FFN_HIDDEN, D_MODEL), FFN_HIDDEN ** -0.5),
        "ffn_post_g": gain(ks[23], D_MODEL),
    }

def second_block(x, mix_pre_g, w_in, gate_b, glu_b, conv_dw_w, conv_dw_b, conv_ln_g,
              conv_ln_b, conv_pw_w, conv_pw_b, ssm_conv_w, ssm_conv_b, dt_bias, a_log,
              d_skip, ssm_norm_g, ssm_out_w, w_out, mix_post_g, ffn_pre_g, w_gate_up,
              w_down, ffn_post_g):
    for i in range(DEPTH):
        h = rms_norm(x, mix_pre_g[i])
        proj = h @ w_in[i]
        u_glu = proj[..., :OFF_Z]
        z = proj[..., OFF_Z:OFF_XBC]
        xbc = proj[..., OFF_XBC:OFF_DT]
        dt_raw = proj[..., OFF_DT:OFF_GATE]
        gates = jax.nn.sigmoid(proj[..., OFF_GATE:] + gate_b[i])
        g_conv, g_ssm = jnp.split(gates, 2, axis=-1)
        conv_out = conformer_conv_branch(u_glu, glu_b[i], conv_dw_w[i], conv_dw_b[i],
                                         conv_ln_g[i], conv_ln_b[i], conv_pw_w[i],
                                         conv_pw_b[i])
        ssm_out = ssd_branch(z, xbc, dt_raw, ssm_conv_w[i], ssm_conv_b[i], dt_bias[i],
                             a_log[i], d_skip[i], ssm_norm_g[i], ssm_out_w[i])
        mixed = (g_conv * conv_out + g_ssm * ssm_out) @ w_out[i]
        x = x + rms_norm(mixed, mix_post_g[i])
        h = rms_norm(x, ffn_pre_g[i])
        gt, up = jnp.split(h @ w_gate_up[i], 2, axis=-1)
        f = (jax.nn.silu(gt) * up) @ w_down[i]
        x = x + rms_norm(f, ffn_post_g[i])
    return x


def setup_inputs(seed=0):
    out = dict(first_inputs(seed))
    for name, value in second_inputs(seed + 1).items():
        if name != "x":
            out[name + "_2"] = value
    return out


def reference(
    x, mem, norm_mix_g, w_in, fox_f_bias, hgrn_lb_logits, hgrn_norm_g, w_out, norm_x_g,
    norm_mem_g, w_xq, w_xkv, w_xo, norm_ff_g, w1, w2, final_norm_g, mix_pre_g_2, w_in_2,
    gate_b_2, glu_b_2, conv_dw_w_2, conv_dw_b_2, conv_ln_g_2, conv_ln_b_2, conv_pw_w_2,
    conv_pw_b_2, ssm_conv_w_2, ssm_conv_b_2, dt_bias_2, a_log_2, d_skip_2, ssm_norm_g_2,
    ssm_out_w_2, w_out_2, mix_post_g_2, ffn_pre_g_2, w_gate_up_2, w_down_2, ffn_post_g_2,
):
    x = first_block(
        x, mem, norm_mix_g, w_in, fox_f_bias, hgrn_lb_logits, hgrn_norm_g, w_out, norm_x_g,
        norm_mem_g, w_xq, w_xkv, w_xo, norm_ff_g, w1, w2, final_norm_g,
    )
    return second_block(
        x, mix_pre_g_2, w_in_2, gate_b_2, glu_b_2, conv_dw_w_2, conv_dw_b_2, conv_ln_g_2,
        conv_ln_b_2, conv_pw_w_2, conv_pw_b_2, ssm_conv_w_2, ssm_conv_b_2, dt_bias_2, a_log_2,
        d_skip_2, ssm_norm_g_2, ssm_out_w_2, w_out_2, mix_post_g_2, ffn_pre_g_2, w_gate_up_2,
        w_down_2, ffn_post_g_2,
    )


_drawn_inputs = setup_inputs


def setup_inputs(seed=0):
    import zlib

    import numpy as np

    out = dict(_drawn_inputs(seed))
    spreads = {}
    factors = {'hgrn_lb_logits': 7.492,
     'hgrn_norm_g': 4.696,
     'norm_x_g': 8.0,
     'norm_mem_g': 8.0,
     'gate_b_2': 8.0,
     'glu_b_2': 5.726,
     'conv_dw_b_2': 3.191,
     'conv_ln_b_2': 6.3,
     'conv_pw_b_2': 3.911,
     'ssm_conv_b_2': 2.914,
     'norm_ff_g': 8.0}
    for name, (base, spread) in spreads.items():
        noise = np.random.default_rng([zlib.crc32(name.encode()), seed]).standard_normal(out[name].shape)
        drawn = base * np.exp(spread * noise) if base else spread * noise
        out[name] = jnp.asarray(drawn.astype(out[name].dtype))
    for name, factor in factors.items():
        out[name] = (out[name] * factor).astype(out[name].dtype)
    return out
```

```python
from contextlib import ExitStack

import concourse.bass as bass
from concourse import mybir
import numpy as np

P = 128
S = 512
D = 1024
KT = D // P
TT = S // P
NMEM = 256
MT = NMEM // P
EPS = 1e-6
LN_EPS = 1e-5
NEG = -1.0e30

HG = 4
LEVELS = 8
FH = 8
FD = 64
XH = 4
XD = 256
FF1 = 4096
CONV_K = 31
SK = 4
GROUPS = 8
HPG = 4
NSH = GROUPS * HPG
FF2 = 2816
F2T = FF2 // P
CHUNK2 = [8, 8, 6]
STRIP = KT * P

F32 = mybir.dt.float32
F32R = mybir.dt.float32r
BF16 = mybir.dt.bfloat16
I32 = mybir.dt.int32
ALU = mybir.AluOpType
ACT = mybir.ActivationFunctionType
AX_X = mybir.AxisListType.X



def stream():
    at, out = {}, []

    def add(name, items):
        at[name] = len(out)
        out.extend(items)

    add("hgrn", [("gf", t) for t in range(HG)] + [("gq", t) for t in range(HG)] + [("gi", t) for t in range(HG)]
        + [("gg", t) for t in range(HG)])
    add("fox", [("ff", 0)] + [("fv", t) for t in range(4)] + [(n, t) for t in range(4) for n in ("fq", "fk")])
    add("mem", [("memk", t) for t in range(KT)] + [("memv", t) for t in range(KT)])
    add("w_out", [("w_out", t) for t in range(KT)])
    add("xq", [("xq", t) for t in range(KT)])
    add("xo", [("xo", t) for t in range(KT)])
    add("ffn1", [x for c in range(FF1 // D) for x in
                 [("w1", KT * c + t) for t in range(KT)] + [("w2", t, c) for t in range(KT)]])
    add("dt", [("dt", 0)])
    add("glu", [x for t in range(KT) for x in (("val", t), ("glu", t))])
    add("ssd0", [x for g in range(4) for x in group_strips(g)])
    add("ssmout0", [("ssmout", t, 0) for t in range(KT)])
    add("ssd1", [x for g in range(4, 8) for x in group_strips(g)])
    add("ssmout1", [x for t in range(KT) for x in (("gssm", t), ("ssmout", t, 1))])
    add("pw", [x for t in range(KT) for x in (("gconv", t), ("pw", t))])
    add("w_out2", [("w_out2", t) for t in range(KT)])
    f = 0
    for c, n in enumerate(CHUNK2):
        add(f"gu{c}", [x for t in range(n) for x in (("gate", f + t), ("up", f + t))])
        add(f"down{c}", [("down", t, c) for t in range(KT)])
        f += n
    return at, out


def group_strips(g):
    return [("xs", 2 * g), ("xs", 2 * g + 1), ("bm", g), ("cm", g), ("z", 2 * g), ("z", 2 * g + 1)]


AT, STREAM = stream()
NS = len(STREAM)
NS_FULL = AT["down2"]

VEC = [("mix_g", 8), ("mem_g", 8), ("x_g", 8), ("ff_g", 8), ("final_g", 8), ("pre_g", 8), ("ffn_g", 8),
       ("post_g", 8), ("ffpost_g", 8), ("hgrn_g", 1), ("lb0", 4), ("lb1", 4), ("foxb", 1), ("gate_b", 16),
       ("glu_b", 16), ("dw_w", 8 * CONV_K), ("dw_b", 8), ("ln_g", 8), ("ln_b", 8), ("pw_b", 8),
       ("sc_w", 32 * SK), ("sc_b", 32), ("dt_b", 1), ("a_log", 1), ("dskip", 16), ("ssm_g", 16)]
VOFF, _n = {}, 0
for _name, _c in VEC:
    VOFF[_name] = _n
    _n += _c
NVEC = _n

CONST = [("ones", P), ("ident", P), ("tri", P), ("neg", P), ("lev", LEVELS * P), ("reset", S), ("eps", 2)]
COFF, _n = {}, 0
for _name, _c in CONST:
    COFF[_name] = _n
    _n += _c
NCONST = _n


def constants():
    c = np.zeros((P, NCONST), np.float32)
    r = np.arange(P)
    c[:, COFF["ones"]:COFF["ones"] + P] = 1.0
    c[:, COFF["ident"]:COFF["ident"] + P] = np.eye(P)
    c[:, COFF["tri"]:COFF["tri"] + P] = r[None, :] >= r[:, None]
    c[:, COFF["neg"]:COFF["neg"] + P] = np.where(r[None, :] > r[:, None], NEG, 0.0)
    for level in range(LEVELS):
        if level == 0:
            m = r[:, None] == r[None, :]
        else:
            h = 1 << (level - 1)
            m = (r[:, None] // (2 * h) == r[None, :] // (2 * h)) & (r[:, None] % (2 * h) < h) & (r[None, :] % (2 * h) >= h)
        c[:, COFF["lev"] + level * P:COFF["lev"] + (level + 1) * P] = m
    c[:, COFF["eps"]:COFF["eps"] + 2] = [[EPS, LN_EPS]]
    c[:, COFF["reset"]:COFF["reset"] + S] = (np.arange(S) % P != 0)[None, :]
    return c


ARENA = 15104
LAST_BLOCK = 2


def val(c, i, per):
    return c if i is None else i * per + c


FILL = {(t, l): 1 + 3 * t + n for t in range(HG) for n, l in enumerate((2, 4, 6))}


def block_kernel(nc, xT, memT, weights, weights6, vectors, consts, scratch, spill, outT):
    with ExitStack() as ctx:
        def sb(name, shape, dt=F32):
            return ctx.enter_context(nc.sbuf_tensor(name, shape, dt))

        sems = {}

        def sem(name):
            if name not in sems:
                sems[name] = ctx.enter_context(nc.semaphore(name))
            return sems[name]

        h = sb("h", [P, KT * S])
        XA = (sb("XAh", [P, KT * S], F32R), sb("XAl", [P, KT * S], F32R))
        NRAW = 2
        raw = [sb(f"raw{s}", [P, STRIP]) for s in range(NRAW)]
        wh = [sb(f"wh{s}", [P, STRIP], F32R) for s in range(4)]
        wl = [sb(f"wl{s}", [P, STRIP], F32R) for s in range(4)]
        vec = sb("vec", [P, NVEC])
        cst = sb("cst", [P, NCONST])
        ident_bf = sb("ident_bf", [P, P], BF16)
        neg_bf = sb("neg_bf", [P, P], BF16)
        rstd = sb("rstd", [P, S])
        ssum = sb("ssum", [P, S])
        std = sb("std", [P, S])
        sq = sb("sq", [P, 2, S])
        xt = sb("xt", [P, 2, S])
        small = sb("small", [P, 256])
        arena = sb("arena", [P, ARENA])
        with nc.sbuf_tensor("XBh", [P, KT * S], F32R) as xbh, nc.sbuf_tensor("XBl", [P, KT * S], F32R) as xbl:
            XB = (xbh, xbl)
        early = sb("early", [P, 2 * KT * S])

        def carve(base, at, *shape):
            n = int(np.prod(shape))
            a = base[:, at[0]:at[0] + n]
            at[0] += n
            assert at[0] <= (ARENA if base is arena else 2 * KT * S), at[0]
            if len(shape) == 2:
                return a.rearrange("p (a b) -> p a b", a=shape[0])
            if len(shape) == 3:
                return a.rearrange("p (a b c) -> p a b c", a=shape[0], b=shape[1])
            return a

        bank = [ctx.enter_context(nc.psum_tensor(f"bank{s}", [P, S], F32)) for s in range(4)]
        work = [ctx.enter_context(nc.psum_tensor(f"work{s}", [P, S], F32)) for s in range(4)]

        def V(name, t=0, n=1):
            return vec[:, VOFF[name] + t:VOFF[name] + t + n]

        def C(name, t=0):
            return cst[:, COFF[name] + t * P:COFF[name] + (t + 1) * P]

        ones, ident, tri = C("ones"), C("ident"), C("tri")
        reset = cst[:, COFF["reset"]:COFF["reset"] + S]

        def tile(a, n, w=S):
            if isinstance(n, int):
                return a[:, n * S:n * S + w]
            return a[:, bass.ds(n * S, w)]

        def blocks(a):
            return a.rearrange("p (a b) -> p a b", b=P)

        at = [0]
        fq, fk, fv = carve(arena, at, 4 * S), carve(arena, at, 4 * S), carve(arena, at, TT, 4 * P)
        r1 = at[0]
        hkk, hgg, hb = carve(arena, at, HG * S), carve(arena, at, HG * S), carve(arena, at, HG * S)
        r4 = at[0]
        mem_in = carve(arena, at, KT * NMEM)
        memrstd, fneg = carve(arena, at, NMEM), carve(arena, at, S)
        at = [0]
        hqq, hgi = carve(early, at, HG * S), carve(early, at, TT, HG * P)
        hE, hZ, hattn = carve(early, at, 2, S), carve(early, at, 2, S), carve(early, at, S)
        hkt, hS = carve(early, at, 3, P), carve(early, at, 3, P)
        at = [r1]
        fPT = carve(arena, at, 2, S)
        at = [r1 + HG * S]
        memk, memv = carve(arena, at, KT * NMEM), carve(arena, at, MT, D)
        at = [r4]
        fS, nfb = carve(arena, at, 2, S), carve(arena, at, 2, S)
        at = [0]
        xqf, xP = carve(arena, at, KT * S), carve(arena, at, 2, NMEM)
        at = [r1]
        xPT = carve(arena, at, 2, MT, S)
        at = [0]
        VW = S + CONV_K - 1
        vpad = carve(arena, at, KT, VW)
        acc = arena[:, 0:KT * S]
        r5 = at[0]
        rawp = carve(arena, at, 2, S + SK - 1)
        xf = carve(arena, at, 4, S)
        zs = carve(arena, at, 2, S)
        xdt, xde, btok = carve(arena, at, TT, 2 * P), carve(arena, at, 3, 2 * P), carve(arena, at, 3, P)
        cbm, Ab, Mm = carve(arena, at, S), carve(arena, at, 2, S), carve(arena, at, 2, S)
        Ss, acs = carve(arena, at, 3, P), carve(arena, at, S)
        dacs = carve(arena, at, 2, TT, NSH)
        at = [r5]
        cv = carve(arena, at, KT * S)
        mu, rs2 = carve(arena, at, S), carve(arena, at, S)
        s_lb, s_oml, s_nea = small[:, 0:4], small[:, 4:8], small[:, 8:9]
        s_nm, s_rs, s_ri, s_eb = small[:, 16:18], small[:, 18:20], small[:, 20:22], small[:, 24:28]
        s_tmp = small[:, 32:64]
        s_dte, s_dl = small[:, 64:72], small[:, 72:80]

        raw_ready = [sem(f"raw_ready{s}") for s in range(NRAW)]
        w_hi, w_lo, strip_done = sem("w_hi"), sem("w_lo"), sem("strip_done")
        bank_free = [sem(f"bank_free{s}") for s in range(4)]
        wk_done = [sem(f"wk_done{s}") for s in range(4)]
        wk_free = [sem(f"wk_free{s}") for s in range(4)]
        x_ready, h_upd, sq_done, ssum_rdy = sem("x_ready"), sem("h_upd"), sem("sq_done"), sem("ssum_rdy")
        loaded, const_rdy = sem("loaded"), sem("const_rdy")

        XN, SQN, NORM = {}, {}, {}
        nx = nsq = nn = 0
        for name, tiles, sqs, norms in [
            ("in", KT, KT, 1), ("rec", 4, 0, 0), ("mem", KT, KT, 1), ("fox", 4, 0, 0), ("w_out", KT, KT, 1),
            ("xattn", KT, 0, 0), ("xo", KT, KT, 1), ("hid", 4 * KT, 0, 0), ("final", 0, KT, 1),
            ("pre", KT, KT, 1), ("y0", KT, 0, 0), ("y1", KT, 0, 0), ("conv", KT, KT, 2),
            ("mix", KT, 0, 0), ("post", 0, KT, 1), ("ffn", KT, KT, 1),
            ("g0", KT, 0, 0), ("g1", KT, 0, 0), ("g2", CHUNK2[2], 0, 0), ("ffpost", 0, KT, 1),
        ]:
            XN[name], SQN[name], NORM[name] = nx, nsq, nn
            nx, nsq, nn = nx + tiles, nsq + sqs, nn + norms

        uses, used = {}, [0] * 4

        def wait_full(eng, key):
            b, n = uses[key]
            eng.wait_ge(wk_done[b], n + 1)
            return work[b]

        def free(ins, key):
            ins.then_inc(wk_free[uses[key][0]], 1)

        def wait_read(eng, key):
            b, n = uses[key]
            eng.wait_ge(wk_free[b], n + 1)

        block = ctx.enter_context(nc.Block())

        @block.tensor
        def _(pe):
            mm, turn = nc.tensor.matmul, nc.tensor.transpose

            def strip(j, X, kts=range(KT), xn=None, i=None, per=4, w=S):
                s = j % 4
                pe.wait_ge(w_lo, val(j + 1, i, per))
                if j >= 4 or i is not None:
                    pe.wait_ge(bank_free[s], val(j // 4, i, per // 4))
                for n, k in enumerate(kts):
                    if xn is not None:
                        pe.wait_ge(x_ready, val(xn[n] + 1, i, KT))
                    hi, lo = wh[s][:, k * P:(k + 1) * P], wl[s][:, k * P:(k + 1) * P]
                    mm(bank[s][:, 0:w], hi, tile(X[0], k, w), start=(n == 0), stop=False)
                    mm(bank[s][:, 0:w], hi, tile(X[1], k, w), start=False, stop=False)
                    last = mm(bank[s][:, 0:w], lo, tile(X[0], k, w), start=False, stop=(n == len(kts) - 1))
                last.then_inc(strip_done, 1)

            def tiles_from(name, n=KT):
                return [XN[name] + k for k in range(n)]

            def work_bank(key, b):
                uses[key] = (b, used[b])
                if used[b]:
                    pe.wait_ge(wk_free[b], used[b])
                used[b] += 1
                return work[b]

            def norm(k, b=3):
                w = work_bank(("norm", k), b)
                pe.wait_ge(ssum_rdy, k + 1)
                mm(w[:, :], ones, ssum[:, :], start=True, stop=True).then_inc(wk_done[b], 1)

            def turn_tile(key, b, src, n=TT):
                w = work_bank(key, b)
                for c in range(n):
                    last = turn(w[:, c * P:(c + 1) * P], src[:, c * P:(c + 1) * P], ident)
                last.then_inc(wk_done[b], 1)

            pe.wait_ge(const_rdy, 1)
            for n in range(4 * HG):
                strip(AT["hgrn"] + n, XA, xn=tiles_from("in") if n == 0 else None)
                if n == 0:
                    norm(NORM["in"])
                if 9 <= n <= 12:
                    pe.wait_ge(sem("hg_raw"), n)
                    turn_tile(("gi", n - 9), (n - 9) % 2, xt[:, (n - 9) % 2, :])
            strip(AT["fox"], XA)

            for t in range(HG):
                for l in range(LEVELS):
                    if (t, l) in FILL:
                        n = FILL[t, l]
                        strip(AT["fox"] + n, XA)
                        if 2 <= n <= 5:
                            pe.wait_ge(sem("fv_raw"), n - 1)
                            turn_tile(("fv", n - 2), 2, xt[:, (n - 2) % 2, :])
                    w = work_bank(("level", t, l), l % 2)
                    if l == 0:
                        if t == 0:
                            pe.wait_ge(sem("hg_scan"), 1)
                        a, b = hkk[:, t * S:(t + 1) * S], hqq[:, t * S:(t + 1) * S]
                    else:
                        pe.wait_ge(sem("h_z"), 7 * t + l)
                        a = b = hZ[:, l % 2, :]
                    for c in range(TT):
                        last = mm(w[:, c * P:(c + 1) * P], a[:, c * P:(c + 1) * P], b[:, c * P:(c + 1) * P],
                                  start=True, stop=True)
                    last.then_inc(wk_done[l % 2], 1)
                pe.wait_ge(sem("h_qk"), t + 1)
                turn_tile(("kt", t), 2, hZ[:, 1, :], 3)
                w = work_bank(("hs", t), 3)
                wait_read(pe, ("kt", t))
                for c in range(3):
                    last = mm(w[:, c * P:(c + 1) * P], hkt[:, c, :], hgi[:, c, t * P:(t + 1) * P],
                              start=True, stop=True)
                last.then_inc(wk_done[3], 1)
                w = work_bank(("ho", t), 2)
                pe.wait_ge(sem("h_s"), t + 1)
                for c in range(TT):
                    last = mm(w[:, c * P:(c + 1) * P], hgi[:, c, t * P:(t + 1) * P], hattn[:, c * P:(c + 1) * P],
                              start=True, stop=(c == 0))
                    if c:
                        last = mm(w[:, c * P:(c + 1) * P], hS[:, c - 1, :], hZ[:, 0, c * P:(c + 1) * P],
                                  start=False, stop=True)
                last.then_inc(wk_done[2], 1)
                w = work_bank(("hn", t), 3)
                wait_read(pe, ("ho", t))
                mm(w[:, :], ones, sq[:, t % 2, :], start=True, stop=True).then_inc(wk_done[3], 1)

            def nf(hd):
                w = work_bank(("nf", hd), 2)
                if hd == 0:
                    pe.wait_ge(sem("f_neg"), 1)
                mm(w[:, :], ident[0:FH, hd:hd + 1].broadcast_to([FH, P]), fneg[0:FH, :], start=True,
                   stop=True).then_inc(wk_done[2], 1)

            def fox_scores(u):
                hd, i = u // TT, u % TT
                w = work_bank(("fs", u), u % 2)
                po, ft = FD * (hd % 2), hd // 2
                mm(w[:, 0:(i + 1) * P], fq[po:po + FD, ft * S + i * P:ft * S + (i + 1) * P],
                   fk[po:po + FD, ft * S:ft * S + (i + 1) * P], start=True, stop=False)
                mm(w[:, i * P:(i + 1) * P], ident_bf[:, :], neg_bf[:, :], start=False, stop=True)\
                    .then_inc(wk_done[u % 2], 1)

            def fox_out(u):
                hd, i = u // TT, u % TT
                if u % 8 == 0:
                    work_bank(("fo", u // 8), 3)
                po = FD * (hd % 2)
                wait_read(pe, ("ft", u))
                for c in range(i + 1):
                    last = mm(work[3][po:po + FD, i * P:(i + 1) * P], fv[:, c, hd * FD:(hd + 1) * FD],
                              fPT[:, u % 2, c * P:(c + 1) * P], start=(c == 0), stop=(c == i))
                if u % 8 == 7:
                    last.then_inc(wk_done[3], 1)

            def mem_turn(t):
                pe.wait_ge(sem("mv_raw"), t + 1)
                turn_tile(("mv", t), 2, xt[:, t % 2, :], MT)

            norm(NORM["mem"])
            nf(0)
            fox_scores(0)
            for u in range(FH * TT):
                if u % 2 == 0:
                    n = u // 2
                    strip(AT["mem"] + n, XA, xn=tiles_from("mem") if n == 0 else None, w=NMEM)
                    if n > KT:
                        mem_turn(n - KT - 1)
                if u + 1 < FH * TT:
                    if (u + 1) % TT == 0:
                        nf((u + 1) // TT)
                    fox_scores(u + 1)
                pe.wait_ge(sem("f_p"), u + 1)
                turn_tile(("ft", u), 2, fS[:, u % 2, :], u % TT + 1)
                if u:
                    fox_out(u - 1)
            mem_turn(KT - 1)
            fox_out(FH * TT - 1)

            for n in range(KT):
                xn = [XN["rec"] + k for k in range(4)] + [XN["fox"] + k for k in range(4)]
                strip(AT["w_out"] + n, XB, kts=[4, 5, 6, 7, 0, 1, 2, 3], xn=None if n else xn)
            pe.wait_ge(x_ready, XN["w_out"] + KT)
            norm(NORM["w_out"])
            with pe.Fori(0, KT // 4) as i:
                for u in range(4):
                    strip(AT["xq"] + u, XA, i=i)

            def x_scores(u):
                a, i = u // TT, u % TT
                w = work_bank(("xs", u), u % 2)
                if u == 0:
                    pe.wait_ge(sem("xq_rdy"), 1)
                for c in range(2):
                    k = 2 * a + c
                    last = mm(w[:, 0:NMEM], xqf[:, k * S + i * P:k * S + (i + 1) * P],
                              memk[:, k * NMEM:(k + 1) * NMEM], start=(c == 0), stop=(c == 1))
                last.then_inc(wk_done[u % 2], 1)

            def x_out(k):
                a = k // 2
                wait_read(pe, ("xt", TT * a + TT - 1))
                w = work_bank(("xo", k), 3)
                for c in range(MT):
                    last = mm(w[:, :], memv[:, c, k * P:(k + 1) * P], xPT[:, a % 2, c, :],
                              start=(c == 0), stop=(c == MT - 1))
                last.then_inc(wk_done[3], 1)

            x_scores(0)
            for u in range(XH * TT):
                if u + 1 < XH * TT:
                    x_scores(u + 1)
                pe.wait_ge(sem("x_p"), u + 1)
                turn_tile(("xt", u), 2, xP[:, u % 2, :], MT)
                if u % 2 and u > TT:
                    x_out((u - 5) // 2)
            x_out(KT - 2)
            x_out(KT - 1)
            for n in range(KT):
                strip(AT["xo"] + n, XB, xn=tiles_from("xattn") if n == 0 else None)
            pe.wait_ge(x_ready, XN["xo"] + KT)
            norm(NORM["xo"])
            with pe.Fori(0, FF1 // D) as i:
                for u in range(KT):
                    strip(AT["ffn1"] + u, XA, i=i, per=16)
                for u in range(KT):
                    strip(AT["ffn1"] + KT + u, XB, i=i, per=16, xn=tiles_from("hid") if u == 0 else None)
            norm(NORM["final"])
            if LAST_BLOCK == 1:
                return

            strip(AT["dt"], XA, xn=tiles_from("pre"))
            norm(NORM["pre"])
            with pe.Fori(0, 4) as i:
                for u in range(4):
                    strip(AT["glu"] + u, XA, i=i)
            w = work_bank("dacs", 2)
            pe.wait_ge(sem("s_acs"), 1)
            for c in range(TT):
                turn(w[:, c * NSH:(c + 1) * NSH], xt[0:NSH, 1, c * P:(c + 1) * P], ident[0:NSH, 0:NSH])
                last = turn(w[:, (TT + c) * NSH:(TT + c + 1) * NSH], acs[0:NSH, c * P:(c + 1) * P],
                            ident[0:NSH, 0:NSH])
            last.then_inc(wk_done[2], 1)

            def ssd_group(g):
                base = AT["ssd0"] + 6 * g if g < 4 else AT["ssd1"] + 6 * (g - 4)
                for n in range(6):
                    strip(base + n, XA)
                for q in range(2):
                    pe.wait_ge(sem("g_xf"), 4 * g + q + 1)
                    turn_tile(("x", g, q), q, xf[:, q, :])
                pe.wait_ge(sem("g_xf"), 4 * g + 4)
                turn_tile(("b", g), 2, xf[:, 2, :], 3)
                w = work_bank(("cb", g), 3)
                for c in range(TT):
                    last = mm(w[:, c * P:(c + 1) * P], xf[:, 2, c * P:(c + 1) * P], xf[:, 3, c * P:(c + 1) * P],
                              start=True, stop=True)
                last.then_inc(wk_done[3], 1)
                for q in range(2):
                    w = work_bank(("st", g, q), 0)
                    wait_read(pe, ("b", g))
                    pe.wait_ge(sem("g_xde"), 2 * g + q + 1)
                    for c in range(3):
                        last = mm(w[:, c * P:(c + 1) * P], btok[:, c, :], xde[:, c, q * P:(q + 1) * P],
                                  start=True, stop=True)
                    last.then_inc(wk_done[0], 1)
                    w = work_bank(("y", g, q), 1)
                    pe.wait_ge(sem("g_cp"), 2 * g + q + 1)
                    for hh in range(2):
                        o = w[hh * 64:(hh + 1) * 64, :]
                        for c in range(TT):
                            last = mm(o[:, c * P:(c + 1) * P], xdt[:, c, q * P + hh * 64:q * P + (hh + 1) * 64],
                                      Mm[:, hh, c * P:(c + 1) * P], start=True, stop=(c == 0))
                            if c:
                                last = mm(o[:, c * P:(c + 1) * P], Ss[:, c - 1, hh * 64:(hh + 1) * 64],
                                          Ab[:, hh, c * P:(c + 1) * P], start=False, stop=True)
                    last.then_inc(wk_done[1], 1)
                w = work_bank(("gn", g), 3)
                pe.wait_ge(sem("g_sq"), g + 1)
                mm(w[:, :], ones, sq[:, 0, :], start=True, stop=False)
                mm(w[:, :], ones, sq[:, 1, :], start=False, stop=True).then_inc(wk_done[3], 1)

            for g in range(4):
                ssd_group(g)
            for n in range(KT):
                strip(AT["ssmout0"] + n, XB, xn=tiles_from("y0") if n == 0 else None)
            for g in range(4, GROUPS):
                ssd_group(g)
            pe.wait_ge(x_ready, XN["y1"] + KT)
            with pe.Fori(0, 4) as i:
                for u in range(4):
                    strip(AT["ssmout1"] + u, XB if u % 2 else XA, i=i)
            norm(NORM["conv"])
            norm(NORM["conv"] + 1)
            pe.wait_ge(x_ready, XN["conv"] + KT)
            with pe.Fori(0, 4) as i:
                for u in range(4):
                    strip(AT["pw"] + u, XB if u % 2 else XA, i=i)
            for n in range(KT):
                strip(AT["w_out2"] + n, XB, xn=tiles_from("mix") if n == 0 else None)
            norm(NORM["post"])
            pe.wait_ge(x_ready, XN["ffn"] + KT)
            norm(NORM["ffn"])
            for c, nt in enumerate(CHUNK2):
                with pe.Fori(0, nt // 2) as i:
                    for u in range(4):
                        strip(AT[f"gu{c}"] + u, XA, i=i)
                for n in range(KT):
                    strip(AT[f"down{c}"] + n, XB, kts=range(nt), xn=tiles_from(f"g{c}", nt) if n == 0 else None)
            norm(NORM["ffpost"])

        @block.sync
        def _(sp):
            sp.dma_start(cst[:, :], consts).then_inc(loaded, 16)
            sp.dma_start(vec[:, :], vectors).then_inc(loaded, 16)
            sp.dma_start(h[:, :], xT).then_inc(loaded, 16)
            sp.dma_start(mem_in, memT).then_inc(loaded, 16)
            for j in range(2):
                sp.dma_start(raw[j % 2][:, :], weights[j]).then_inc(raw_ready[j % 2], 16)
            turns = (NS_FULL - 2) // 2
            with sp.Fori(0, turns) as i:
                for u in range(2):
                    sp.wait_ge(w_lo, i * 2 + (u + 1))
                    sp.dma_start(raw[u][:, :], weights[bass.ds(i * 2 + (2 + u), 1), :, :].rearrange("a p n -> (a p) n"))\
                        .then_inc(raw_ready[u], 16)
            for j in range(2 * turns + 2, NS):
                sp.wait_ge(w_lo, j - 1)
                w = weights[j] if j < NS_FULL else weights6[j - NS_FULL]
                sp.dma_start(raw[j % 2][:, 0:w.shape[1]], w).then_inc(raw_ready[j % 2], 16)
            sp.wait_ge(sem("result"), KT)
            sp.dma_start(outT, h[:, :]).then_inc(loaded, 16)
            sp.wait_ge(loaded, 16 * 5)

        @block.gpsimd
        def _(pool):
            def low(s, r, j, i):
                pool.wait_ge(w_hi, val(j + 1, i, 4))
                nc.gpsimd.tensor_tensor(wl[s][:, :], raw[r][:, :], wh[s][:, :].bitcast(F32), ALU.subtract)\
                    .then_inc(w_lo, 1)

            with pool.Fori(0, NS // 4) as i:
                for u in range(4):
                    low(u, u % 2, u, i)
            for j in range(NS // 4 * 4, NS):
                low(j % 4, j % 2, j, None)

        @block.scalar
        def _(act):
            act_ = nc.scalar.activation

            def high(j, i=None, per=4):
                act.wait_ge(raw_ready[j % 2], val(16 * (j // 2 + 1), i, 8 * per))
                act_(wh[j % 4][:, :], raw[j % 2][:, :], ACT.Copy).then_inc(w_hi, 1)

            def step(j, i=None, per=4, last=False):
                if j + 4 < NS and not last:
                    act.wait_ge(strip_done, val(j + 1, i, per))
                    high(j + 4, i, per)

            def square(src, t, k, w=S):
                act.wait_ge(h_upd, k + 1)
                act_(sq[:, t % 2, 0:w], src, ACT.Square).then_inc(sq_done, 1)

            def root(k, b=3, scale=1.0 / D, eps=EPS, dst=std, w=S):
                ps = wait_full(act, ("norm", k))
                free(act_(dst[:, 0:w], ps[:, 0:w], ACT.Sqrt, bias=eps_ap(eps), scale=scale), ("norm", k))

            def eps_ap(e):
                return cst[:, COFF["eps"] + (0 if e == EPS else 1):COFF["eps"] + (0 if e == EPS else 1) + 1]

            act.wait_ge(loaded, 64)
            act_(ident_bf[:, :], ident, ACT.Copy)
            act_(neg_bf[:, :], C("neg"), ACT.Copy).then_inc(const_rdy, 1)
            for t in range(4):
                high(t)
            for t in range(KT):
                square(tile(h, t), t, SQN["in"] + t)
            root(NORM["in"])
            act.wait_ge(sem("lb_sub"), 1)
            act_(s_tmp[:, 4:12], s_tmp[:, 4:12], ACT.Exp).then_inc(sem("lb_exp"), 1)
            for n in range(4 * HG):
                step(AT["hgrn"] + n)
                t = n % 4
                if n < 4:
                    act.wait_ge(sem("hg_raw"), n + 1)
                    act_(tile(hb, t), tile(hkk, t), ACT.Sigmoid)
                    act_(tile(hkk, t), tile(hkk, t), ACT.Sigmoid, scale=-1.0).then_inc(sem("hg_sig"), 1)
                elif n < 8 or n >= 12:
                    act.wait_ge(sem("hg_raw"), n + 1)
                    src = hqq if n < 8 else hgg
                    act_(sq[:, t % 2, :], tile(src, t), ACT.Sigmoid).then_inc(sem("hg_sig"), 1)
                if 9 <= n <= 12:
                    ps = wait_full(act, ("gi", n - 9))
                    free(act_(hgi[:, :, (n - 9) * P:(n - 8) * P], blocks(ps[:, :]), ACT.Copy), ("gi", n - 9))
            step(AT["fox"])
            for t in range(HG):
                act.wait_ge(sem("hg_f"), t + 1)
                act_(tile(hb, t), tile(hb, t), ACT.Ln).then_inc(sem("hg_ln"), 1)

            def out_root(t):
                ps = wait_full(act, ("hn", t))
                free(act_(std[:, :], ps[:, :], ACT.Sqrt, bias=eps_ap(EPS), scale=1.0 / P), ("hn", t))

            for t in range(HG):
                for l in range(LEVELS):
                    if (t, l) in FILL:
                        n = FILL[t, l]
                        step(AT["fox"] + n)
                        if 2 <= n <= 5:
                            ps = wait_full(act, ("fv", n - 2))
                            free(act_(fv[:, :, (n - 2) * P:(n - 1) * P], blocks(ps[:, :]), ACT.Copy), ("fv", n - 2))
                    if l:
                        half = 1 << (l - 1)
                        e = hE[:, l % 2, :].rearrange("p (n c) -> p n c", c=2 * half)
                        act.wait_ge(sem("h_d"), 7 * t + l)
                        act_(e[:, :, 0:half], e[:, :, 0:half], ACT.Exp, scale=-1.0)
                        act_(e[:, :, half:], e[:, :, half:], ACT.Exp).then_inc(sem("h_e"), 1)
                    if l == 3 and t:
                        out_root(t - 1)
                act.wait_ge(sem("h_end"), t + 1)
                act_(hE[:, 1, :], hE[:, 1, :], ACT.Exp)
                act_(hE[:, 0, :], tile(hb, t), ACT.Exp).then_inc(sem("h_eb"), 1)
                ps = wait_full(act, ("kt", t))
                free(act_(hkt[:, :, :], blocks(ps[:, 0:3 * P]), ACT.Copy), ("kt", t))
                ps = wait_full(act, ("ho", t))
                act_(tile(hb, t), ps[:, :], ACT.Copy)
                free(act_(sq[:, t % 2, :], ps[:, :], ACT.Square), ("ho", t))
            out_root(HG - 1)

            for t in range(KT):
                square(mem_in[:, t * NMEM:(t + 1) * NMEM], t, SQN["mem"] + t, NMEM)
            root(NORM["mem"], w=NMEM)
            act.wait_ge(sem("f_abs"), 1)
            act_(xt[0:FH, 0, :], xt[0:FH, 0, :], ACT.Exp, scale=-1.0).then_inc(sem("f_exp"), 1)
            act.wait_ge(sem("f_one"), 1)
            act_(xt[0:FH, 1, :], xt[0:FH, 1, :], ACT.Ln).then_inc(sem("f_exp"), 1)

            def nf(hd):
                ps = wait_full(act, ("nf", hd))
                free(act_(nfb[:, hd % 2, :], ps[:, :], ACT.Copy), ("nf", hd))

            def fox_exp(u):
                n = (u % TT + 1) * P
                act.wait_ge(sem("f_s"), u + 1)
                act_(fS[:, u % 2, 0:n], fS[:, u % 2, 0:n], ACT.Exp, bias=s_nm[:, u % 2:u % 2 + 1], scale=-1.0,
                     accum_out=s_rs[:, u % 2:u % 2 + 1]).then_inc(sem("f_e"), 1)

            def mem_turned(t):
                ps = wait_full(act, ("mv", t))
                free(act_(memv[:, :, t * P:(t + 1) * P], blocks(ps[:, 0:NMEM]), ACT.Copy), ("mv", t))

            nf(0)
            for u in range(FH * TT):
                fox_exp(u)
                if u % 2 == 0:
                    n = u // 2
                    step(AT["mem"] + n)
                    if n > KT:
                        mem_turned(n - KT - 1)
                if (u + 1) % TT == 0 and u + 1 < FH * TT:
                    nf((u + 1) // TT)
                n = (u % TT + 1) * P
                ps = wait_full(act, ("ft", u))
                free(act_(fPT[:, u % 2, 0:n], ps[:, 0:n], ACT.Copy), ("ft", u))
            mem_turned(KT - 1)

            for n in range(KT):
                step(AT["w_out"] + n)
                square(tile(h, n), n, SQN["w_out"] + n)
            root(NORM["w_out"])
            with act.Fori(0, KT // 4) as i:
                for u in range(4):
                    step(AT["xq"] + u, i)
            for u in range(XH * TT):
                a, i = u // TT, u % TT
                act.wait_ge(sem("x_m"), u + 1)
                ps = wait_full(act, ("xs", u))
                free(act_(xP[:, u % 2, :], ps[:, 0:NMEM], ACT.Exp, bias=s_nm[:, u % 2:u % 2 + 1],
                          accum_out=s_rs[:, u % 2:u % 2 + 1]), ("xs", u))
                ps = wait_full(act, ("xt", u))
                free(act_(xPT[:, a % 2, :, i * P:(i + 1) * P], blocks(ps[:, 0:NMEM]), ACT.Copy), ("xt", u))
            for n in range(KT):
                step(AT["xo"] + n)
                square(tile(h, n), n, SQN["xo"] + n)
            root(NORM["xo"])
            with act.Fori(0, FF1 // D - 1) as i:
                for u in range(16):
                    step(AT["ffn1"] + u, i, 16)
            for u in range(16):
                step(AT["ffn1"] + 48 + u)
                if u >= KT:
                    square(tile(h, u - KT), u, SQN["final"] + u - KT)
            root(NORM["final"])
            if LAST_BLOCK == 1:
                return

            for t in range(KT):
                square(tile(h, t), t, SQN["pre"] + t)
            root(NORM["pre"])
            step(AT["dt"])
            act.wait_ge(sem("s_abs"), 1)
            act_(xt[0:NSH, 0, :], xt[0:NSH, 0, :], ACT.Exp, scale=-1.0)
            act_(s_nea[0:NSH, :], V("a_log")[0:NSH, :], ACT.Exp).then_inc(sem("s_exp"), 1)
            act.wait_ge(sem("s_one"), 1)
            act_(xt[0:NSH, 1, :], xt[0:NSH, 1, :], ACT.Ln).then_inc(sem("s_exp"), 1)
            act.wait_ge(sem("s_acs"), 1)
            act.dma_start(scratch, acs[0:NSH, :]).then_inc(sem("acs_out"), 16)
            with act.Fori(0, 4) as i:
                for u in range(4):
                    step(AT["glu"] + u, i)
                    if u % 2:
                        act.wait_ge(sem("glu_g"), i * 2 + (u // 2 + 1))
                        act_(sq[:, u // 2, :], sq[:, u // 2, :], ACT.Sigmoid).then_inc(sem("glu_s"), 1)
            ps = wait_full(act, "dacs")
            free(act_(dacs.rearrange("p a b c -> p (a b c)"), ps[:, 0:2 * TT * NSH], ACT.Copy), "dacs")

            def spread(n):
                if n:
                    act.wait_ge(wk_done[1], uses[("y", (n - 1) // 2, (n - 1) % 2)][1] + 1)
                act.dma_start(Ab[:, :, :], scratch[2 * n:2 * n + 2, :].partition_broadcast(P))\
                    .then_inc(sem("spread"), 16)

            def ssd_group(g):
                base = AT["ssd0"] + 6 * g if g < 4 else AT["ssd1"] + 6 * (g - 4)
                for n in range(6):
                    step(base + n)
                    act.wait_ge(sem("g_raw"), 6 * g + n + 1)
                    act_(sq[:, n % 2, :], xt[:, n % 2, :], ACT.Sigmoid).then_inc(sem("g_sig"), 1)
                ps = wait_full(act, ("b", g))
                free(act_(btok[:, :, :], blocks(ps[:, 0:3 * P]), ACT.Copy), ("b", g))
                for q in range(2):
                    n = 2 * g + q
                    act.wait_ge(sem("g_seg"), n + 1)
                    act_(s_dte, s_dte, ACT.Exp).then_inc(sem("g_exp"), 1)
                    act_(Mm[:, :, :], Mm[:, :, :], ACT.Exp).then_inc(sem("g_exp"), 1)
                    act_(Ab[:, :, :], Ab[:, :, :], ACT.Exp).then_inc(sem("g_exp"), 1)
                    if n + 1 < 2 * GROUPS:
                        spread(n + 1)
                for q in range(2):
                    act.wait_ge(sem("g_y"), 2 * g + q + 1)
                    ins = act_(sq[:, q, :], yb[:, q, :], ACT.Square)
                ins.then_inc(sem("g_sq"), 1)
                ps = wait_full(act, ("gn", g))
                free(act_(std[:, :], ps[:, :], ACT.Sqrt, bias=eps_ap(EPS), scale=1.0 / (2 * P)), ("gn", g))

            yb = zs
            act.wait_ge(sem("acs_out"), 16)
            spread(0)
            for g in range(4):
                ssd_group(g)
            act.wait_ge(sem("dw_done"), 1)
            act.dma_start(spill, vpad[:, :, 0:S]).then_inc(sem("dw_out"), 16)
            for n in range(KT):
                step(AT["ssmout0"] + n)
            for g in range(4, GROUPS):
                ssd_group(g)
            act.wait_ge(x_ready, XN["y1"] + KT)
            act.dma_start(cv.rearrange("p (a b) -> p a b", a=KT), spill).then_inc(sem("cv_in"), 16)
            with act.Fori(0, 4) as i:
                for u in range(4):
                    step(AT["ssmout1"] + u, i)
                    if u % 2 == 0:
                        act.wait_ge(sem("gs_g"), i * 2 + (u // 2 + 1))
                        act_(sq[:, u // 2, :], sq[:, u // 2, :], ACT.Sigmoid).then_inc(sem("gs_s"), 1)
            ps = wait_full(act, ("norm", NORM["conv"]))
            free(act_(mu, ps[:, :], ACT.Copy, scale=1.0 / D), ("norm", NORM["conv"]))
            for t in range(KT):
                square(tile(cv, t), t, SQN["conv"] + t)
            root(NORM["conv"] + 1, eps=LN_EPS)
            for t in range(KT):
                act.wait_ge(sem("ln_x"), t + 1)
                act_(sq[:, t % 2, :], xt[:, t % 2, :], ACT.Sigmoid).then_inc(sem("ln_s"), 1)
            with act.Fori(0, 4) as i:
                for u in range(4):
                    step(AT["pw"] + u, i)
                    if u % 2 == 0:
                        act.wait_ge(sem("gc_g"), i * 2 + (u // 2 + 1))
                        act_(sq[:, u // 2, :], sq[:, u // 2, :], ACT.Sigmoid).then_inc(sem("gc_s"), 1)
            for n in range(KT):
                step(AT["w_out2"] + n)
                square(tile(cv, n), n, SQN["post"] + n)
            root(NORM["post"])
            for n in range(KT):
                square(tile(h, n), n, SQN["ffn"] + n)
            root(NORM["ffn"])
            k = 0
            for c, nt in enumerate(CHUNK2):
                turns = nt // 2
                with act.Fori(0, turns) as i:
                    for u in range(4):
                        step(AT[f"gu{c}"] + u, i)
                        if u % 2 == 0:
                            act.wait_ge(sem("ff_g"), i * 2 + (k + u // 2 + 1))
                            act_(sq[:, u // 2, :], xt[:, u // 2, :], ACT.Sigmoid).then_inc(sem("ff_s"), 1)
                k += nt
                for n in range(KT):
                    step(AT[f"down{c}"] + n)
                    if c == 2:
                        square(tile(acc, n), n, SQN["ffpost"] + n)
            root(NORM["ffpost"])

        @block.vector
        def _(dve):
            TTop, STT, TS = nc.vector.tensor_tensor, nc.vector.scalar_tensor_tensor, nc.vector.tensor_scalar
            copy = nc.vector.tensor_copy

            def taken(j, i=None, per=4):
                dve.wait_ge(strip_done, val(j + 1, i, per))
                return bank[j % 4]

            def leave(ins, j):
                ins.then_inc(bank_free[j % 4], 1)

            def split(src, X, k, w=S):
                copy(tile(X[0], k, w), src)
                dve.drain()
                TTop(tile(X[1], k, w), src, tile(X[0], k, w).bitcast(F32), ALU.subtract).then_inc(x_ready, 1)

            def sum_square(t, k, w=S):
                dve.wait_ge(sq_done, k + 1)
                if t == 0:
                    copy(ssum[:, 0:w], sq[:, 0, 0:w])
                else:
                    TTop(ssum[:, 0:w], ssum[:, 0:w], sq[:, t % 2, 0:w], ALU.add)
                dve.drain()

            def prep(src, g, X, t, k, w=S, first=True):
                if first:
                    dve.drain().then_inc(h_upd, 1)
                TS(xt[:, t % 2, 0:w], src, g, None, ALU.mult)
                dve.drain()
                split(xt[:, t % 2, 0:w], X, t, w)
                sum_square(t, k, w)

            def invert(k, dst, w=S):
                dve.drain().then_inc(ssum_rdy, 1)
                wait_read(dve, ("norm", k))
                nc.vector.reciprocal(dst[:, 0:w], std[:, 0:w])
                dve.drain()

            def residual(j, n, k, g=None, X=None):
                ps = taken(j)
                leave(TTop(tile(h, n), tile(h, n), ps[:, :], ALU.add), j)
                dve.drain().then_inc(h_upd, 1)
                if X is not None:
                    prep(tile(h, n), g, X, n, k, first=False)
                else:
                    sum_square(n, k)

            dve.wait_ge(loaded, 64)
            for t in range(KT):
                prep(tile(h, t), V("mix_g", t), XA, t, SQN["in"] + t)
            TTop(s_tmp[:, 0:4], V("lb0", 0, 4), V("lb1", 0, 4), ALU.max)
            dve.drain()
            TTop(s_tmp[:, 4:8], V("lb0", 0, 4), s_tmp[:, 0:4], ALU.subtract)
            TTop(s_tmp[:, 8:12], V("lb1", 0, 4), s_tmp[:, 0:4], ALU.subtract)
            dve.drain().then_inc(sem("lb_sub"), 1)
            invert(NORM["in"], rstd)
            for n in range(4 * HG):
                j, t = AT["hgrn"] + n, n % 4
                ps = taken(j)
                dst = [tile(hkk, t), tile(hqq, t), xt[:, t % 2, :], tile(hgg, t)][n // 4]
                if 10 <= n <= 11:
                    dve.wait_ge(wk_done[t % 2], uses[("gi", t - 2)][1] + 1)
                leave(TTop(dst, ps[:, :], rstd[:, :], ALU.mult), j)
                dve.drain().then_inc(sem("hg_raw"), 1)
                if n < 4:
                    dve.wait_ge(sem("hg_sig"), n + 1)
                    if n == 0:
                        dve.wait_ge(sem("lb_exp"), 1)
                        TTop(s_tmp[:, 0:4], s_tmp[:, 4:8], s_tmp[:, 8:12], ALU.add)
                        dve.drain()
                        nc.vector.reciprocal(s_tmp[:, 12:16], s_tmp[:, 0:4])
                        dve.drain()
                        TTop(s_lb, s_tmp[:, 4:8], s_tmp[:, 12:16], ALU.mult)
                        TTop(s_oml, s_tmp[:, 8:12], s_tmp[:, 12:16], ALU.mult)
                        dve.drain()
                    TS(tile(hb, t), tile(hb, t), s_oml[:, t:t + 1], s_lb[:, t:t + 1], ALU.mult, ALU.add)
                    TS(tile(hkk, t), tile(hkk, t), s_oml[:, t:t + 1], None, ALU.mult)
                    dve.drain().then_inc(sem("hg_f"), 1)
                elif n < 8 or n >= 12:
                    dve.wait_ge(sem("hg_sig"), n + 1 if n < 8 else n - 3)
                    TTop(dst, dst, sq[:, t % 2, :], ALU.mult)
                    dve.drain()

            def fox_in(n):
                j = AT["fox"] + n
                name, t = STREAM[j]
                ps = taken(j)
                if name == "ff":
                    leave(TTop(fneg[0:FH, :], ps[0:FH, :], rstd[0:FH, :], ALU.mult), j)
                elif name == "fv":
                    if t >= 2:
                        dve.wait_ge(wk_done[2], uses[("fv", t - 2)][1] + 1)
                    leave(TTop(xt[:, t % 2, :], ps[:, :], rstd[:, :], ALU.mult), j)
                    dve.drain().then_inc(sem("fv_raw"), 1)
                elif name == "fq":
                    leave(STT(tile(fq, t), ps[:, :], FD ** -0.5, rstd[:, :], ALU.mult, ALU.mult), j)
                else:
                    leave(TTop(tile(fk, t), ps[:, :], rstd[:, :], ALU.mult), j)

            for t in (2, 3):
                dve.wait_ge(wk_done[t % 2], uses[("gi", t)][1] + 1)
            fox_in(0)
            for t in range(HG):
                dve.wait_ge(sem("hg_ln"), t + 1)
                nc.vector.tensor_tensor_scan(tile(hb, t), reset, tile(hb, t), 0.0, ALU.mult, ALU.add)
            dve.drain().then_inc(sem("hg_scan"), 1)

            def out_norm(t):
                wait_read(dve, ("hn", t))
                nc.vector.reciprocal(std[:, :], std[:, :])
                dve.drain()
                TTop(tile(hb, t), tile(hb, t), std[:, :], ALU.mult)
                dve.drain()
                STT(tile(hb, t), tile(hb, t), V("hgrn_g"), tile(hgg, t), ALU.mult, ALU.mult)
                dve.drain()

            def distance(t, l):
                half = 1 << (l - 1)
                b = tile(hb, t).rearrange("p (n c) -> p n c", c=2 * half)
                TTop(hE[:, l % 2, :].rearrange("p (n c) -> p n c", c=2 * half), b,
                     b[:, :, half - 1:half].broadcast_to([P, S // (2 * half), 2 * half]), ALU.subtract)\
                    .then_inc(sem("h_d"), 1)

            def gather(t, l):
                ps = wait_full(dve, ("level", t, l))
                mask = C("lev", l).rearrange("p (a b) -> p a b", a=1).broadcast_to([P, TT, P])
                if l == 0:
                    if t:
                        dve.wait_ge(wk_done[2], uses[("ho", t - 1)][1] + 1)
                    free(TTop(blocks(hattn), blocks(ps[:, :]), mask, ALU.mult), ("level", t, l))
                else:
                    free(nc.vector.copy_predicated(blocks(hattn), mask.bitcast(I32), blocks(ps[:, :])),
                         ("level", t, l))
                dve.drain()

            for t in range(HG):
                distance(t, 1)
                gather(t, 0)
                for l in range(1, LEVELS):
                    if (t, l) in FILL:
                        fox_in(FILL[t, l])
                        dve.drain()
                    if l + 1 < LEVELS:
                        distance(t, l + 1)
                    half = 1 << (l - 1)

                    def halves(a, k):
                        return a.rearrange("p (n c) -> p n c", c=2 * half)[:, :, k * half:(k + 1) * half]

                    dve.wait_ge(sem("h_e"), 7 * t + l)
                    if l <= 2 and t:
                        dve.wait_ge(wk_done[2], uses[("ho", t - 1)][1] + 1)
                    e, z = hE[:, l % 2, :], hZ[:, l % 2, :]
                    TTop(halves(z, 0), halves(tile(hkk, t), 0), halves(e, 0), ALU.mult)
                    TTop(halves(z, 1), halves(tile(hqq, t), 1), halves(e, 1), ALU.mult)
                    dve.drain().then_inc(sem("h_z"), 1)
                    if l > 1:
                        gather(t, l - 1)
                    if l == 4 and t:
                        out_norm(t - 1)
                gather(t, LEVELS - 1)
                b = blocks(tile(hb, t))
                TTop(blocks(hE[:, 1, :]), b[:, :, P - 1:P].broadcast_to([P, TT, P]), b, ALU.subtract)\
                    .then_inc(sem("h_end"), 1)
                dve.wait_ge(sem("h_eb"), t + 1)
                TTop(hZ[:, 1, :], tile(hkk, t), hE[:, 1, :], ALU.mult)
                TTop(hZ[:, 0, :], tile(hqq, t), hE[:, 0, :], ALU.mult)
                copy(s_eb, hE[:, 0, P - 1::P])
                dve.drain().then_inc(sem("h_qk"), 1)
                ps = wait_full(dve, ("hs", t))
                copy(hS[:, 0, :], ps[:, 0:P])
                dve.drain()
                STT(hS[:, 1, :], hS[:, 0, :], s_eb[:, 1:2], ps[:, P:2 * P], ALU.mult, ALU.add)
                dve.drain()
                free(STT(hS[:, 2, :], hS[:, 1, :], s_eb[:, 2:3], ps[:, 2 * P:3 * P], ALU.mult, ALU.add), ("hs", t))
                dve.drain().then_inc(sem("h_s"), 1)
            out_norm(HG - 1)
            for t in range(HG):
                split(tile(hb, t), XB, 4 + t)
            dve.drain()

            dve.wait_ge(strip_done, AT["mem"])
            for t in range(KT):
                prep(mem_in[:, t * NMEM:(t + 1) * NMEM], V("mem_g", t), XA, t, SQN["mem"] + t, NMEM)
            invert(NORM["mem"], memrstd, NMEM)
            TS(fneg[0:FH, :], fneg[0:FH, :], V("foxb")[0:FH, :], None, ALU.add)
            dve.drain()
            STT(xt[0:FH, 0, :], fneg[0:FH, :], -1.0, fneg[0:FH, :], ALU.mult, ALU.max)
            dve.drain().then_inc(sem("f_abs"), 1)

            def log1p(rows, exp_done, one):
                dve.wait_ge(exp_done, 1)
                TS(xt[0:rows, 1, :], xt[0:rows, 0, :], 1.0, None, ALU.add)
                dve.drain()
                TS(ssum[0:rows, :], xt[0:rows, 1, :], -1.0, None, ALU.add)
                dve.drain()
                TTop(xt[0:rows, 0, :], xt[0:rows, 0, :], ssum[0:rows, :], ALU.subtract)
                dve.drain().then_inc(one, 1)
                dve.wait_ge(exp_done, 2)
                TTop(xt[0:rows, 1, :], xt[0:rows, 1, :], xt[0:rows, 0, :], ALU.add)
                dve.drain()

            log1p(FH, sem("f_exp"), sem("f_one"))
            STT(xt[0:FH, 1, :], fneg[0:FH, :], 0.0, xt[0:FH, 1, :], ALU.min, ALU.subtract)
            dve.drain()
            TS(ssum[0:FH, :], xt[0:FH, 1, :], 0.0, 1.0, ALU.mult, ALU.add)
            dve.drain()
            nc.vector.tensor_tensor_scan(fneg[0:FH, :], ssum[0:FH, :], xt[0:FH, 1, :], 0.0, ALU.mult, ALU.subtract)
            dve.drain().then_inc(sem("f_neg"), 1)

            def fox_logits(u):
                hd, n = u // TT, (u % TT + 1) * P
                if u % TT == 0:
                    wait_read(dve, ("nf", hd))
                ps = wait_full(dve, ("fs", u))
                if u >= 2:
                    dve.wait_ge(wk_done[2], uses[("ft", u - 2)][1] + 1)
                free(nc.vector.tensor_tensor_reduce(
                    out=fS[:, u % 2, 0:n], in0=ps[:, 0:n], in1=nfb[:, hd % 2, 0:n], scale=-1.0, scalar=3.0e38,
                    op0=ALU.add, op1=ALU.min, accum_out=s_nm[:, u % 2:u % 2 + 1]), ("fs", u))
                dve.drain().then_inc(sem("f_s"), 1)

            def mem_in_strip(n):
                j = AT["mem"] + n
                ps = taken(j)
                if n < KT:
                    leave(TTop(memk[:, n * NMEM:(n + 1) * NMEM], ps[:, 0:NMEM], memrstd, ALU.mult), j)
                else:
                    t = n - KT
                    if t >= 2:
                        dve.wait_ge(wk_done[2], uses[("mv", t - 2)][1] + 1)
                    leave(TTop(xt[:, t % 2, 0:NMEM], ps[:, 0:NMEM], memrstd, ALU.mult), j)
                    dve.drain().then_inc(sem("mv_raw"), 1)

            def normalise(sums_ready, n, a, u, done):
                dve.wait_ge(sums_ready, u + 1) if sums_ready is not None else None
                nc.vector.reciprocal(s_ri[:, u % 2:u % 2 + 1], s_rs[:, u % 2:u % 2 + 1])
                dve.drain()
                TS(a[:, u % 2, 0:n], a[:, u % 2, 0:n], s_ri[:, u % 2:u % 2 + 1], None, ALU.mult)
                dve.drain().then_inc(done, 1)

            def split_work(key, k):
                ps = wait_full(dve, key)
                copy(tile(XB[0], k), ps[:, :])
                dve.drain()
                free(TTop(tile(XB[1], k), ps[:, :], tile(XB[0], k).bitcast(F32), ALU.subtract), key)
                dve.drain().then_inc(x_ready, 1)

            fox_logits(0)
            for u in range(FH * TT):
                if u % 2 == 0:
                    mem_in_strip(u // 2)
                if u + 1 < FH * TT:
                    fox_logits(u + 1)
                normalise(sem("f_e"), (u % TT + 1) * P, fS, u, sem("f_p"))
                if u % 8 == 1 and u > 8:
                    split_work(("fo", u // 8 - 1), u // 8 - 1)
            split_work(("fo", 3), 3)

            for n in range(KT):
                residual(AT["w_out"] + n, n, SQN["w_out"] + n, V("x_g", n), XA)
            invert(NORM["w_out"], rstd)
            with dve.Fori(0, KT // 4) as i:
                for u in range(4):
                    ps = taken(AT["xq"] + u, i)
                    leave(STT(tile(xqf, i * 4 + u), ps[:, :], XD ** -0.5, rstd[:, :], ALU.mult, ALU.mult), AT["xq"] + u)
            dve.drain().then_inc(sem("xq_rdy"), 1)

            def x_max(u):
                ps = wait_full(dve, ("xs", u))
                nc.vector.tensor_reduce(s_nm[:, u % 2:u % 2 + 1], ps[:, 0:NMEM], AX_X, ALU.max, negate=True)\
                    .then_inc(sem("x_m"), 1)

            x_max(0)
            for u in range(XH * TT):
                if u + 1 < XH * TT:
                    if u:
                        dve.wait_ge(wk_done[2], uses[("xt", u - 1)][1] + 1)
                    x_max(u + 1)
                wait_read(dve, ("xs", u))
                normalise(None, NMEM, xP, u, sem("x_p"))
                if u % 2 == 0 and u > 5:
                    split_work(("xo", (u - 6) // 2), (u - 6) // 2)
            for k in range(KT - 3, KT):
                split_work(("xo", k), k)
            for n in range(KT):
                residual(AT["xo"] + n, n, SQN["xo"] + n, V("ff_g", n), XA)
            invert(NORM["xo"], rstd)

            def hidden(j, u, i):
                ps = taken(j, i, 16)
                leave(STT(xt[:, u % 2, :], ps[:, :], 0.0, rstd[:, :], ALU.max, ALU.mult), j)
                dve.drain()
                TTop(xt[:, u % 2, :], xt[:, u % 2, :], xt[:, u % 2, :], ALU.mult)
                dve.drain()
                split(xt[:, u % 2, :], XB, u)

            with dve.Fori(0, FF1 // D - 1) as i:
                for u in range(KT):
                    hidden(AT["ffn1"] + u, u, i)
                for u in range(KT):
                    j = AT["ffn1"] + KT + u
                    ps = taken(j, i, 16)
                    leave(TTop(tile(h, u), tile(h, u), ps[:, :], ALU.add), j)
                dve.drain()
            for u in range(KT):
                hidden(AT["ffn1"] + 48 + u, u, None)
            for u in range(KT):
                residual(AT["ffn1"] + 56 + u, u, SQN["final"] + u)
            invert(NORM["final"], rstd)

            def scale_tile(n, g):
                STT(tile(h, n), tile(h, n), g, rstd[:, :], ALU.mult, ALU.mult)

            if LAST_BLOCK == 1:
                for n in range(KT):
                    scale_tile(n, V("final_g", n))
                    dve.drain().then_inc(sem("result"), 1)
                return
            for n in range(KT):
                scale_tile(n, V("final_g", n))
                dve.drain().then_inc(h_upd, 1)
                prep(tile(h, n), V("pre_g", n), XA, n, SQN["pre"] + n, first=False)
            invert(NORM["pre"], rstd)
            nc.vector.memset(vpad[:, :, 0:CONV_K - 1], 0.0)
            nc.vector.memset(rawp[:, :, 0:SK - 1], 0.0)
            ps = taken(AT["dt"])
            leave(TTop(acs[0:NSH, :], ps[0:NSH, :], rstd[0:NSH, :], ALU.mult), AT["dt"])
            dve.drain()
            TS(acs[0:NSH, :], acs[0:NSH, :], V("dt_b")[0:NSH, :], None, ALU.add)
            dve.drain()
            STT(xt[0:NSH, 0, :], acs[0:NSH, :], -1.0, acs[0:NSH, :], ALU.mult, ALU.max)
            dve.drain().then_inc(sem("s_abs"), 1)
            log1p(NSH, sem("s_exp"), sem("s_one"))
            STT(xt[0:NSH, 1, :], acs[0:NSH, :], 0.0, xt[0:NSH, 1, :], ALU.max, ALU.add)
            dve.drain()
            TS(acs[0:NSH, :], xt[0:NSH, 1, :], s_nea[0:NSH, :], -1.0, ALU.mult, ALU.mult)
            dve.drain()
            nc.vector.tensor_tensor_scan(acs[0:NSH, :], reset[0:NSH, :], acs[0:NSH, :], 0.0, ALU.mult, ALU.add)
            dve.drain().then_inc(sem("s_acs"), 1)
            with dve.Fori(0, 4) as i:
                for u in range(4):
                    j, t = AT["glu"] + u, i * 2 + u // 2
                    v = arena[:, bass.ds(t * VW + (CONV_K - 1), S)]
                    ps = taken(j, i)
                    if u % 2 == 0:
                        leave(TTop(v, ps[:, :], rstd[:, :], ALU.mult), j)
                        dve.drain()
                        TS(v, v, vec[:, bass.ds(t + VOFF["glu_b"], 1)], None, ALU.add)
                    else:
                        leave(TTop(sq[:, u // 2, :], ps[:, :], rstd[:, :], ALU.mult), j)
                        dve.drain()
                        TS(sq[:, u // 2, :], sq[:, u // 2, :], vec[:, bass.ds(t + (VOFF["glu_b"] + KT), 1)], None, ALU.add)
                        dve.drain().then_inc(sem("glu_g"), 1)
                        dve.wait_ge(sem("glu_s"), i * 2 + (u // 2 + 1))
                        TTop(v, v, sq[:, u // 2, :], ALU.mult)
                        dve.drain()
            wait_read(dve, "dacs")

            def depthwise(t):
                v = vpad[:, t, :]
                c = ssum[:, :]
                TS(c, v[:, CONV_K - 1:], V("dw_w", t * CONV_K + CONV_K - 1), V("dw_b", t), ALU.mult, ALU.add)
                for k in range(CONV_K - 2, -1, -1):
                    dve.drain()
                    STT(v[:, 0:S] if k == 0 else c, v[:, k:k + S], V("dw_w", t * CONV_K + k), c, ALU.mult, ALU.add)
                dve.drain()

            def ssd_group(g):
                base = AT["ssd0"] + 6 * g if g < 4 else AT["ssd1"] + 6 * (g - 4)

                def gate(n):
                    dve.wait_ge(sem("g_sig"), 6 * g + n + 1)
                    dst = xf[:, n, :] if n < 4 else zs[:, n - 4, :]
                    TTop(dst, xt[:, n % 2, :], sq[:, n % 2, :], ALU.mult)
                    dve.drain().then_inc(sem("g_xf"), 1) if n < 4 else dve.drain()

                for n in range(6):
                    j = base + n
                    ps = taken(j)
                    x = xt[:, n % 2, :]
                    if n < 4:
                        r = rawp[:, n % 2, :]
                        leave(TTop(r[:, SK - 1:], ps[:, :], rstd[:, :], ALU.mult), j)
                        dve.drain()
                        ct = [2 * g, 2 * g + 1, 16 + g, 24 + g][n]
                        TS(x, r[:, 0:S], V("sc_w", ct * SK), V("sc_b", ct), ALU.mult, ALU.add)
                        for k in range(1, SK):
                            dve.drain()
                            STT(x, r[:, k:k + S], V("sc_w", ct * SK + k), x, ALU.mult, ALU.add)
                    else:
                        leave(TTop(x, ps[:, :], rstd[:, :], ALU.mult), j)
                    dve.drain().then_inc(sem("g_raw"), 1)
                    if n:
                        gate(n - 1)
                gate(5)
                for q in range(2):
                    ps = wait_full(dve, ("x", g, q))
                    dt = dacs[:, 0, :, 4 * g + 2 * q:4 * g + 2 * q + 2].rearrange("p c (h o) -> p c h o", o=1)
                    free(TTop(xdt[:, :, q * P:(q + 1) * P].rearrange("p c (h v) -> p c h v", h=2),
                              ps[:, :].rearrange("p (c h v) -> p c h v", c=TT, h=2),
                              dt.broadcast_to([P, TT, 2, 64]), ALU.mult), ("x", g, q))
                ps = wait_full(dve, ("cb", g))
                free(TTop(blocks(cbm), blocks(ps[:, :]),
                          tri.rearrange("p (a b) -> p a b", a=1).broadcast_to([P, TT, P]), ALU.mult), ("cb", g))
                for q in range(2):
                    n = 2 * g + q
                    hd = 4 * g + 2 * q
                    a4 = Ab.rearrange("p h (c l) -> p h c l", c=TT)
                    acol = dacs[:, 1, :, hd:hd + 2].rearrange("p c (h o) -> p h c o", o=1)
                    dve.wait_ge(sem("spread"), 16 * (n + 1))
                    TTop(Mm.rearrange("p h (c l) -> p h c l", c=TT), a4, acol.broadcast_to([P, 2, TT, P]), ALU.subtract)
                    TTop(s_dte.rearrange("p (h c o) -> p h c o", h=2, o=1), a4[:, :, :, P - 1:P], acol, ALU.subtract)
                    dve.drain()
                    TS(Mm[:, :, :], Mm[:, :, :], 0.0, None, ALU.min)
                    dve.drain().then_inc(sem("g_seg"), 1)
                    dve.wait_ge(sem("g_exp"), 3 * n + 1)
                    TTop(xde[:, :, q * P:(q + 1) * P].rearrange("p c (h v) -> p c h v", h=2),
                         xdt[:, 0:3, q * P:(q + 1) * P].rearrange("p c (h v) -> p c h v", h=2),
                         s_dte.rearrange("p (h c o) -> p c h o", h=2, o=1)[:, 0:3].broadcast_to([P, 3, 2, 64]), ALU.mult)
                    dve.drain().then_inc(sem("g_xde"), 1)
                    dve.wait_ge(sem("g_exp"), 3 * n + 2)
                    TTop(Mm[:, :, :], Mm[:, :, :], cbm.rearrange("p (a b) -> p a b", a=1).broadcast_to([P, 2, S]), ALU.mult)
                    dve.wait_ge(sem("g_exp"), 3 * n + 3)
                    copy(s_dl.rearrange("p (h c o) -> p h c o", h=2, o=1), a4[:, :, :, P - 1:P])
                    dve.drain()
                    TTop(Ab[:, :, :], Ab[:, :, :], xf[:, 3:4, :].broadcast_to([P, 2, S]), ALU.mult)
                    ps = wait_full(dve, ("st", g, q))
                    copy(Ss[:, 0, :], ps[:, 0:P])
                    for c in (1, 2):
                        dve.drain()
                        dl = s_dl.rearrange("p (h c) -> p h c", h=2)[:, :, c:c + 1].broadcast_to([P, 2, 64])
                        TTop(Ss[:, c, :].rearrange("p (h v) -> p h v", h=2),
                             Ss[:, c - 1, :].rearrange("p (h v) -> p h v", h=2), dl, ALU.mult)
                        dve.drain()
                        ins = TTop(Ss[:, c, :], Ss[:, c, :], ps[:, c * P:(c + 1) * P], ALU.add)
                    free(ins, ("st", g, q))
                    dve.drain().then_inc(sem("g_cp"), 1)
                    ps = wait_full(dve, ("y", g, q))
                    free(STT(xt[:, q, :], xf[:, q, :], V("dskip", 2 * g + q), ps[:, :], ALU.mult, ALU.add), ("y", g, q))
                    dve.drain()
                    TTop(zs[:, q, :], xt[:, q, :], zs[:, q, :], ALU.mult)
                    dve.drain().then_inc(sem("g_y"), 1)
                if g < 4:
                    depthwise(2 * g)
                    depthwise(2 * g + 1)
                wait_read(dve, ("gn", g))
                nc.vector.reciprocal(std[:, :], std[:, :])
                dve.drain()
                for q in range(2):
                    STT(xt[:, q, :], zs[:, q, :], V("ssm_g", 2 * g + q), std[:, :], ALU.mult, ALU.mult)
                    dve.drain()
                    split(xt[:, q, :], XB, 2 * (g % 4) + q)

            for g in range(4):
                ssd_group(g)
            dve.drain().then_inc(sem("dw_done"), 1)
            dve.wait_ge(sem("dw_out"), 16)
            for n in range(KT):
                j = AT["ssmout0"] + n
                ps = taken(j)
                leave(copy(tile(acc, n), ps[:, :]), j)
            for g in range(4, GROUPS):
                ssd_group(g)

            def gate_logit(j, i, u, col, done):
                ps = taken(j, i)
                leave(TTop(sq[:, u // 2, :], ps[:, :], rstd[:, :], ALU.mult), j)
                dve.drain()
                TS(sq[:, u // 2, :], sq[:, u // 2, :], vec[:, bass.ds(i * 2 + (col + u // 2), 1)], None, ALU.add)
                dve.drain().then_inc(done, 1)

            with dve.Fori(0, 4) as i:
                for u in range(0, 4, 2):
                    j, t = AT["ssmout1"] + u, i * 2 + u // 2
                    gate_logit(j, i, u, VOFF["gate_b"] + KT, sem("gs_g"))
                    ps = taken(j + 1, i)
                    leave(TTop(tile(acc, t), tile(acc, t), ps[:, :], ALU.add), j + 1)
                    dve.drain()
                    dve.wait_ge(sem("gs_s"), i * 2 + (u // 2 + 1))
                    TTop(tile(acc, t), tile(acc, t), sq[:, u // 2, :], ALU.mult)
                    dve.drain()
            dve.wait_ge(sem("cv_in"), 16)
            copy(ssum[:, :], tile(cv, 0))
            for n in range(1, KT):
                dve.drain()
                TTop(ssum[:, :], ssum[:, :], tile(cv, n), ALU.add)
            dve.drain().then_inc(ssum_rdy, 1)
            wait_read(dve, ("norm", NORM["conv"]))
            for n in range(KT):
                TTop(tile(cv, n), tile(cv, n), mu, ALU.subtract)
                dve.drain().then_inc(h_upd, 1)
                sum_square(n, SQN["conv"] + n)
            invert(NORM["conv"] + 1, rs2)

            def ln_gate(n):
                dve.wait_ge(sem("ln_s"), n + 1)
                TTop(xt[:, n % 2, :], xt[:, n % 2, :], sq[:, n % 2, :], ALU.mult)
                dve.drain()
                split(xt[:, n % 2, :], XB, n)
                dve.drain()

            for n in range(KT):
                STT(xt[:, n % 2, :], tile(cv, n), V("ln_g", n), rs2, ALU.mult, ALU.mult)
                dve.drain()
                TS(xt[:, n % 2, :], xt[:, n % 2, :], V("ln_b", n), None, ALU.add)
                dve.drain().then_inc(sem("ln_x"), 1)
                if n:
                    ln_gate(n - 1)
            ln_gate(KT - 1)
            with dve.Fori(0, 4) as i:
                for u in range(0, 4, 2):
                    j, t = AT["pw"] + u, i * 2 + u // 2
                    gate_logit(j, i, u, VOFF["gate_b"], sem("gc_g"))
                    ps = taken(j + 1, i)
                    dve.wait_ge(sem("gc_s"), i * 2 + (u // 2 + 1))
                    leave(STT(xt[:, u // 2, :], ps[:, :], vec[:, bass.ds(t + VOFF["pw_b"], 1)], sq[:, u // 2, :],
                              ALU.add, ALU.mult), j + 1)
                    dve.drain()
                    TTop(tile(acc, t), tile(acc, t), xt[:, u // 2, :], ALU.add)
                    dve.drain()
            for n in range(KT):
                split(tile(acc, n), XB, n)
                dve.drain()
            for n in range(KT):
                j = AT["w_out2"] + n
                ps = taken(j)
                leave(copy(tile(cv, n), ps[:, :]), j)
                dve.drain().then_inc(h_upd, 1)
                sum_square(n, SQN["post"] + n)
            invert(NORM["post"], rstd)
            for n in range(KT):
                STT(xt[:, n % 2, :], tile(cv, n), V("post_g", n), rstd[:, :], ALU.mult, ALU.mult)
                dve.drain()
                TTop(tile(h, n), tile(h, n), xt[:, n % 2, :], ALU.add)
                dve.drain().then_inc(h_upd, 1)
                prep(tile(h, n), V("ffn_g", n), XA, n, SQN["ffn"] + n, first=False)
            invert(NORM["ffn"], rstd)
            k = 0
            for c, nt in enumerate(CHUNK2):
                with dve.Fori(0, nt // 2) as i:
                    for u in range(0, 4, 2):
                        j, x = AT[f"gu{c}"] + u, xt[:, u // 2, :]
                        ps = taken(j, i)
                        leave(TTop(x, ps[:, :], rstd[:, :], ALU.mult), j)
                        dve.drain().then_inc(sem("ff_g"), 1)
                        dve.wait_ge(sem("ff_s"), i * 2 + (k + u // 2 + 1))
                        TTop(x, x, sq[:, u // 2, :], ALU.mult)
                        dve.drain()
                        TTop(x, x, rstd[:, :], ALU.mult)
                        dve.drain()
                        ps = taken(j + 1, i)
                        leave(TTop(x, x, ps[:, :], ALU.mult), j + 1)
                        dve.drain()
                        split(x, XB, i * 2 + u // 2)
                        dve.drain()
                k += nt
                for n in range(KT):
                    j = AT[f"down{c}"] + n
                    ps = taken(j)
                    if c == 0:
                        leave(copy(tile(acc, n), ps[:, :]), j)
                        continue
                    leave(TTop(tile(acc, n), tile(acc, n), ps[:, :], ALU.add), j)
                    if c == 2:
                        dve.drain().then_inc(h_upd, 1)
                        sum_square(n, SQN["ffpost"] + n)
                dve.drain()
            invert(NORM["ffpost"], rstd)
            for n in range(KT):
                STT(xt[:, n % 2, :], tile(acc, n), V("ffpost_g", n), rstd[:, :], ALU.mult, ALU.mult)
                dve.drain()
                TTop(tile(h, n), tile(h, n), xt[:, n % 2, :], ALU.add)
                dve.drain().then_inc(sem("result"), 1)


def by_features(a):
    t, f = a.shape
    return np.ascontiguousarray(a.T.reshape(f // P, P, t).transpose(1, 0, 2).reshape(P, -1))


def strip_of(w, n, k0=0, kn=KT):
    part = w[k0 * P:(k0 + kn) * P, n * P:(n + 1) * P]
    if part.shape[1] < P:
        part = np.pad(part, ((0, 0), (0, P - part.shape[1])))
    return part.reshape(kn, P, P).transpose(1, 0, 2).reshape(P, kn * P)


def columns(v):
    v = np.asarray(v).reshape(-1)
    n = -(-v.size // P)
    return np.pad(v, (0, n * P - v.size)).reshape(n, P).T


def lay_out(x):
    g = {k: np.asarray(v) for k, v in x.items()}
    w_in, w_in2, wkv, gu = g["w_in"][0], g["w_in_2"][0], g["w_xkv"][0], g["w_gate_up_2"][0]
    fox, hg = 512, 512
    o = np.cumsum([0, fox, fox, fox, FH, hg, hg, hg, hg])
    part = {n: w_in[:, o[i]:o[i + 1]] for i, n in enumerate(["fq", "fk", "fv", "ff", "gq", "gf", "gi", "gg"])}
    o = np.cumsum([0, D, D, 2 * D, 2 * D, D, D, NSH, D, D])
    part |= {n: w_in2[:, o[i]:o[i + 1]] for i, n in
             enumerate(["val", "glu", "z", "xs", "bm", "cm", "dt", "gconv", "gssm"])}
    part |= {"memk": wkv[:, :D], "memv": wkv[:, D:], "w_out": g["w_out"][0], "xq": g["w_xq"][0], "xo": g["w_xo"][0],
             "w1": g["w1"][0], "w2": g["w2"][0], "ssmout": g["ssm_out_w_2"][0], "pw": g["conv_pw_w_2"][0],
             "w_out2": g["w_out_2"][0], "gate": gu[:, :FF2], "up": gu[:, FF2:], "down": g["w_down_2"][0]}
    full = np.stack([strip_of(part[s[0]], s[1], KT * (s[2] if len(s) > 2 else 0)) for s in STREAM[:NS_FULL]])
    six = np.stack([strip_of(part[s[0]], s[1], KT * s[2], CHUNK2[2]) for s in STREAM[NS_FULL:]])
    lb = g["hgrn_lb_logits"]
    taps = lambda w: w.reshape(w.shape[0], -1, P).transpose(2, 1, 0).reshape(P, -1)
    cols = {"mix_g": g["norm_mix_g"], "mem_g": g["norm_mem_g"], "x_g": g["norm_x_g"], "ff_g": g["norm_ff_g"],
            "final_g": g["final_norm_g"], "pre_g": g["mix_pre_g_2"], "ffn_g": g["ffn_pre_g_2"],
            "post_g": g["mix_post_g_2"], "ffpost_g": g["ffn_post_g_2"], "hgrn_g": g["hgrn_norm_g"], "lb0": lb[0],
            "lb1": lb[1], "foxb": g["fox_f_bias"], "gate_b": g["gate_b_2"], "glu_b": g["glu_b_2"],
            "dw_b": g["conv_dw_b_2"], "ln_g": g["conv_ln_g_2"], "ln_b": g["conv_ln_b_2"], "pw_b": g["conv_pw_b_2"],
            "sc_b": g["ssm_conv_b_2"], "dt_b": g["dt_bias_2"], "a_log": g["a_log_2"],
            "dskip": np.repeat(g["d_skip_2"][0], 64), "ssm_g": g["ssm_norm_g_2"]}
    cols = {k: columns(v) for k, v in cols.items()}
    cols["dw_w"], cols["sc_w"] = taps(g["conv_dw_w_2"][0]), taps(g["ssm_conv_w_2"][0])
    return {"xT": by_features(g["x"][0]), "memT": by_features(g["mem"][0]), "weights": full, "weights6": six,
            "vectors": np.ascontiguousarray(np.concatenate([cols[n] for n, _ in VEC], 1)), "consts": constants()}


def kernel(**inputs):
    import concourse.bacc as _bacc
    from concourse.bass_utils import run_bass_kernel_spmd as _run

    nc = _bacc.Bacc("TRN2", target_bir_lowering=False, num_devices=1)
    arrays, args = {}, []
    for name, a in lay_out(inputs).items():
        arrays[f"in_{name}"] = a
        args.append(nc.dram_tensor(f"in_{name}", a.shape, mybir.dt.from_np(a.dtype), kind="ExternalInput").ap())
    args.append(nc.dram_tensor("scratch", (NSH, S), F32, kind="Internal").ap())
    args.append(nc.dram_tensor("spill", (P, KT, S), F32, kind="Internal").ap())
    args.append(nc.dram_tensor("out_0", (P, KT * S), F32, kind="ExternalOutput").ap())
    block_kernel(nc, *args)
    r = _run(nc, [arrays], core_ids=[0])
    out = np.asarray(r.results[0]["out_0"]).reshape(P, KT, S).transpose(2, 1, 0).reshape(1, S, D)
    return np.ascontiguousarray(out)
```

```python
from contextlib import ExitStack

import concourse.bass as bass
from concourse import mybir
import numpy as np

P = 128
S = 512
D = 1024
KT = D // P
TT = S // P
NMEM = 256
MT = NMEM // P
EPS = 1e-6
LN_EPS = 1e-5
NEG = -1.0e30

HG = 4
LEVELS = 8
FH = 8
FD = 64
XH = 4
XD = 256
FF1 = 4096
CONV_K = 31
SK = 4
GROUPS = 8
HPG = 4
NSH = GROUPS * HPG
FF2 = 2816
F2T = FF2 // P
CHUNK2 = [8, 8, 6]
STRIP = KT * P
OUT0_AT = {2: [0], 3: [1, 2], 4: [3, 4], 5: [5, 6, 7]}

F32 = mybir.dt.float32
F32R = mybir.dt.float32r
BF16 = mybir.dt.bfloat16
I32 = mybir.dt.int32
ALU = mybir.AluOpType
ACT = mybir.ActivationFunctionType
AX_X = mybir.AxisListType.X



def stream():
    at, out = {}, []

    def add(name, items):
        at[name] = len(out)
        out.extend(items)

    add("hgrn", [("gf", t) for t in range(HG)] + [("gq", t) for t in range(HG)] + [("gi", t) for t in range(HG)]
        + [("gg", t) for t in range(HG)])
    add("fox", [("ff", 0)] + [("fv", t) for t in range(4)] + [(n, t) for t in range(4) for n in ("fq", "fk")])
    add("mem", [("memk", t) for t in range(KT)] + [("memv", t) for t in range(KT)])
    add("w_out", [("w_out", t) for t in range(KT)])
    add("xq", [("xq", t) for t in range(KT)])
    add("xo", [("xo", t) for t in range(KT)])
    add("ffn1", [x for c in range(FF1 // D) for x in
                 [("w1", KT * c + t) for t in range(KT)] + [("w2", t, c) for t in range(KT)]])
    add("dt", [("dt", 0)])
    add("glu", [x for t in range(KT) for x in (("val", t), ("glu", t))])
    for g in range(GROUPS):
        for k, item in enumerate(group_strips(g)):
            add(("ssd", g, k), [item])
            for t in OUT0_AT.get(k, []) if g == 5 else []:
                add(("out0", t), [("ssmout", t, 0)])
    add("gssm", [("gssm", t) for t in range(KT)])
    add("ssmout1", [("ssmout", t, 1) for t in range(KT)])
    add("gconv", [("gconv", t) for t in range(KT)])
    add("pw", [("pw", t) for t in range(KT)])
    add("w_out2", [("w_out2", t) for t in range(KT)])
    f = 0
    for c, n in enumerate(CHUNK2):
        add(f"gu{c}", [x for t in range(n) for x in (("gate", f + t), ("up", f + t))])
        add(f"down{c}", [("down", t, c) for t in range(KT)])
        f += n
    return at, out


def group_strips(g):
    return [("xs", 2 * g), ("xs", 2 * g + 1), ("bm", g), ("cm", g), ("z", 2 * g), ("z", 2 * g + 1)]


AT, STREAM = stream()
NS = len(STREAM)
NS_FULL = AT["down2"]

VEC = [("mix_g", 8), ("mem_g", 8), ("x_g", 8), ("ff_g", 8), ("final_g", 8), ("pre_g", 8), ("ffn_g", 8),
       ("post_g", 8), ("ffpost_g", 8), ("hgrn_g", 1), ("lb0", 4), ("lb1", 4), ("foxb", 1), ("gate_b", 16),
       ("glu_b", 16), ("dw_w", 8 * CONV_K), ("dw_b", 8), ("ln_g", 8), ("ln_b", 8), ("pw_b", 8),
       ("sc_w", 32 * SK), ("sc_b", 32), ("dt_b", 1), ("a_log", 1), ("dskip", 16), ("ssm_g", 16)]
VOFF, _n = {}, 0
for _name, _c in VEC:
    VOFF[_name] = _n
    _n += _c
NVEC = _n

CONST = [("ones", P), ("ident", P), ("tri", P), ("neg", P), ("lev", LEVELS * P), ("reset", S), ("eps", 2)]
COFF, _n = {}, 0
for _name, _c in CONST:
    COFF[_name] = _n
    _n += _c
NCONST = _n


def constants():
    c = np.zeros((P, NCONST), np.float32)
    r = np.arange(P)
    c[:, COFF["ones"]:COFF["ones"] + P] = 1.0
    c[:, COFF["ident"]:COFF["ident"] + P] = np.eye(P)
    c[:, COFF["tri"]:COFF["tri"] + P] = r[None, :] >= r[:, None]
    c[:, COFF["neg"]:COFF["neg"] + P] = np.where(r[None, :] > r[:, None], NEG, 0.0)
    for level in range(LEVELS):
        if level == 0:
            m = r[:, None] == r[None, :]
        else:
            h = 1 << (level - 1)
            m = (r[:, None] // (2 * h) == r[None, :] // (2 * h)) & (r[:, None] % (2 * h) < h) & (r[None, :] % (2 * h) >= h)
        c[:, COFF["lev"] + level * P:COFF["lev"] + (level + 1) * P] = m
    c[:, COFF["eps"]:COFF["eps"] + 2] = [[EPS, LN_EPS]]
    c[:, COFF["reset"]:COFF["reset"] + S] = (np.arange(S) % P != 0)[None, :]
    return c


ARENA = 15366
LAST_BLOCK = 2


def val(c, i, per):
    return c if i is None else i * per + c


FILL = {(t, l): 1 + 3 * t + n for t in range(HG) for n, l in enumerate((2, 4, 6))}


def block_kernel(nc, xT, memT, weights, weights6, vectors, consts, scratch, spill, outT):
    with ExitStack() as ctx:
        def sb(name, shape, dt=F32):
            return ctx.enter_context(nc.sbuf_tensor(name, shape, dt))

        sems = {}

        def sem(name):
            if name not in sems:
                sems[name] = ctx.enter_context(nc.semaphore(name))
            return sems[name]

        h = sb("h", [P, KT * S])
        XA = (sb("XAh", [P, KT * S], F32R), sb("XAl", [P, KT * S], F32R))
        NRAW = 2
        raw = [sb(f"raw{s}", [P, STRIP]) for s in range(NRAW)]
        wh = [sb(f"wh{s}", [P, STRIP], F32R) for s in range(4)]
        wl = [sb(f"wl{s}", [P, STRIP], F32R) for s in range(4)]
        vec = sb("vec", [P, NVEC])
        cst = sb("cst", [P, NCONST])
        ident_bf = sb("ident_bf", [P, P], BF16)
        neg_bf = sb("neg_bf", [P, P], BF16)
        rstd = sb("rstd", [P, S])
        ssum = sb("ssum", [P, S])
        std = sb("std", [P, S])
        sq = sb("sq", [P, 2, S])
        xt = sb("xt", [P, 2, S])
        small = sb("small", [P, 256])
        arena = sb("arena", [P, ARENA])
        with nc.sbuf_tensor("XBh", [P, KT * S], F32R) as xbh, nc.sbuf_tensor("XBl", [P, KT * S], F32R) as xbl:
            XB = (xbh, xbl)
        early = sb("early", [P, 2 * KT * S])

        def carve(base, at, *shape):
            n = int(np.prod(shape))
            a = base[:, at[0]:at[0] + n]
            at[0] += n
            assert at[0] <= (ARENA if base is arena else 2 * KT * S), at[0]
            if len(shape) == 2:
                return a.rearrange("p (a b) -> p a b", a=shape[0])
            if len(shape) == 3:
                return a.rearrange("p (a b c) -> p a b c", a=shape[0], b=shape[1])
            return a

        bank = [ctx.enter_context(nc.psum_tensor(f"bank{s}", [P, S], F32)) for s in range(4)]
        work = [ctx.enter_context(nc.psum_tensor(f"work{s}", [P, S], F32)) for s in range(4)]

        def V(name, t=0, n=1):
            return vec[:, VOFF[name] + t:VOFF[name] + t + n]

        def C(name, t=0):
            return cst[:, COFF[name] + t * P:COFF[name] + (t + 1) * P]

        ones, ident, tri = C("ones"), C("ident"), C("tri")
        reset = cst[:, COFF["reset"]:COFF["reset"] + S]

        def tile(a, n, w=S):
            if isinstance(n, int):
                return a[:, n * S:n * S + w]
            return a[:, bass.ds(n * S, w)]

        def blocks(a):
            return a.rearrange("p (a b) -> p a b", b=P)

        at = [0]
        fq, fk, fv = carve(arena, at, 4 * S), carve(arena, at, 4 * S), carve(arena, at, TT, 4 * P)
        r1 = at[0]
        hkk, hgg, hb = carve(arena, at, HG * S), carve(arena, at, HG * S), carve(arena, at, HG * S)
        r4 = at[0]
        mem_in = carve(arena, at, KT * NMEM)
        memrstd, fneg = carve(arena, at, NMEM), carve(arena, at, S)
        at = [0]
        hqq, hgi = carve(early, at, HG * S), carve(early, at, TT, HG * P)
        hE, hZ, hattn = carve(early, at, 2, S), carve(early, at, 2, S), carve(early, at, S)
        hkt, hS = carve(early, at, 3, P), carve(early, at, 3, P)
        at = [r1]
        fPT = carve(arena, at, 2, S)
        at = [r1 + HG * S]
        memk, memv = carve(arena, at, KT * NMEM), carve(arena, at, MT, D)
        at = [r4]
        fS, nfb = carve(arena, at, 2, S), carve(arena, at, 2, S)
        at = [0]
        xqf, xP = carve(arena, at, KT * S), carve(arena, at, 2, NMEM)
        at = [r1]
        xPT = carve(arena, at, 2, MT, S)
        at = [0]
        VW = S + CONV_K - 1
        vpad = carve(arena, at, KT, VW)
        acc = arena[:, 0:KT * S]
        r5 = at[0]
        rawp = carve(arena, at, 2, S + SK - 1)
        xf = carve(arena, at, 4, S)
        xdt, xde, btok = carve(arena, at, TT, 2 * P), carve(arena, at, 3, 2 * P), carve(arena, at, 3, P)
        zs2 = carve(arena, at, 2, 2, S)
        cbm, Ab, Mm = carve(arena, at, S), carve(arena, at, 2, S), carve(arena, at, 2, S)
        Ss, acs = carve(arena, at, 3, P), carve(arena, at, S)
        lev = cst[:, COFF["lev"]:COFF["lev"] + 2 * S]
        xfs = [[lev[:, 0:S], lev[:, S:2 * S], acs, rstd[:, :]], [xf[:, n, :] for n in range(4)]]
        gates = [lev[:, 0:S], lev[:, S:2 * S], acs, rstd[:, :], zs2[:, 0, 0, :], zs2[:, 0, 1, :],
                 xt[:, 0, :], xt[:, 1, :]]
        dacs = carve(arena, at, 2, TT, NSH)
        at = [r5]
        cv = carve(arena, at, KT * S)
        mu, rs2 = carve(arena, at, S), carve(arena, at, S)
        s_lb, s_oml, s_nea = small[:, 0:4], small[:, 4:8], small[:, 8:9]
        s_nm, s_rs, s_ri, s_eb = small[:, 16:18], small[:, 18:20], small[:, 20:22], small[:, 24:28]
        s_tmp = small[:, 32:64]
        s_dte, s_dl = small[:, 64:72], small[:, 72:80]

        raw_ready = [sem(f"raw_ready{s}") for s in range(NRAW)]
        w_hi, w_lo, strip_done = sem("w_hi"), sem("w_lo"), sem("strip_done")
        bank_free = [sem(f"bank_free{s}") for s in range(4)]
        wk_done = [sem(f"wk_done{s}") for s in range(4)]
        wk_free = [sem(f"wk_free{s}") for s in range(4)]
        x_ready, h_upd, sq_done, ssum_rdy = sem("x_ready"), sem("h_upd"), sem("sq_done"), sem("ssum_rdy")
        loaded, const_rdy, hi_done = sem("loaded"), sem("const_rdy"), sem("hi_done")
        HI = {n: KT * k for k, n in enumerate(["in", "mem", "w_out", "xo", "pre", "conv", "mix", "ffn"])}

        XN, SQN, NORM = {}, {}, {}
        nx = nsq = nn = 0
        for name, tiles, sqs, norms in [
            ("in", KT, KT, 1), ("rec", 4, 0, 0), ("mem", KT, KT, 1), ("fox", 4, 0, 0), ("w_out", KT, KT, 1),
            ("xattn", KT, 0, 0), ("xo", KT, KT, 1), ("hid", 4 * KT, 0, 0), ("final", 0, KT, 1),
            ("pre", KT, KT, 1), ("y0", KT, 0, 0), ("y1", KT, 0, 0), ("conv", KT, KT, 2),
            ("mix", KT, 0, 0), ("post", 0, KT, 1), ("ffn", KT, KT, 1),
            ("g0", KT, 0, 0), ("g1", KT, 0, 0), ("g2", CHUNK2[2], 0, 0), ("ffpost", 0, KT, 1),
        ]:
            XN[name], SQN[name], NORM[name] = nx, nsq, nn
            nx, nsq, nn = nx + tiles, nsq + sqs, nn + norms

        uses, used = {}, [0] * 4

        def wait_full(eng, key):
            b, n = uses[key]
            eng.wait_ge(wk_done[b], n + 1)
            return work[b]

        def free(ins, key):
            ins.then_inc(wk_free[uses[key][0]], 1)

        def wait_read(eng, key):
            b, n = uses[key]
            eng.wait_ge(wk_free[b], n + 1)

        block = ctx.enter_context(nc.Block())

        @block.tensor
        def _(pe):
            mm, turn = nc.tensor.matmul, nc.tensor.transpose

            def strip(j, X, kts=range(KT), xn=None, i=None, per=4, w=S):
                s = j % 4
                pe.wait_ge(w_lo, val(j + 1, i, per))
                if j >= 4 or i is not None:
                    pe.wait_ge(bank_free[s], val(j // 4, i, per // 4))
                for n, k in enumerate(kts):
                    if xn is not None:
                        pe.wait_ge(x_ready, val(xn[n] + 1, i, KT))
                    hi, lo = wh[s][:, k * P:(k + 1) * P], wl[s][:, k * P:(k + 1) * P]
                    mm(bank[s][:, 0:w], hi, tile(X[0], k, w), start=(n == 0), stop=False)
                    mm(bank[s][:, 0:w], hi, tile(X[1], k, w), start=False, stop=False)
                    last = mm(bank[s][:, 0:w], lo, tile(X[0], k, w), start=False, stop=(n == len(kts) - 1))
                last.then_inc(strip_done, 1)

            def tiles_from(name, n=KT):
                return [XN[name] + k for k in range(n)]

            def work_bank(key, b):
                uses[key] = (b, used[b])
                if used[b]:
                    pe.wait_ge(wk_free[b], used[b])
                used[b] += 1
                return work[b]

            def norm(k, b=3):
                w = work_bank(("norm", k), b)
                pe.wait_ge(ssum_rdy, k + 1)
                mm(w[:, :], ones, ssum[:, :], start=True, stop=True).then_inc(wk_done[b], 1)

            def turn_tile(key, b, src, n=TT):
                w = work_bank(key, b)
                for c in range(n):
                    last = turn(w[:, c * P:(c + 1) * P], src[:, c * P:(c + 1) * P], ident)
                last.then_inc(wk_done[b], 1)

            pe.wait_ge(const_rdy, 1)
            for n in range(4 * HG):
                strip(AT["hgrn"] + n, XA, xn=tiles_from("in") if n == 0 else None)
                if n == 0:
                    norm(NORM["in"])
                if 9 <= n <= 12:
                    pe.wait_ge(sem("hg_raw"), n)
                    turn_tile(("gi", n - 9), (n - 9) % 2, xt[:, (n - 9) % 2, :])
            strip(AT["fox"], XA)

            for t in range(HG):
                for l in range(LEVELS):
                    if (t, l) in FILL:
                        n = FILL[t, l]
                        strip(AT["fox"] + n, XA)
                        if 2 <= n <= 5:
                            pe.wait_ge(sem("fv_raw"), n - 1)
                            turn_tile(("fv", n - 2), 2, xt[:, (n - 2) % 2, :])
                    w = work_bank(("level", t, l), l % 2)
                    if l == 0:
                        if t == 0:
                            pe.wait_ge(sem("hg_scan"), 1)
                        a, b = hkk[:, t * S:(t + 1) * S], hqq[:, t * S:(t + 1) * S]
                    else:
                        pe.wait_ge(sem("h_z"), 7 * t + l)
                        a = b = hZ[:, l % 2, :]
                    for c in range(TT):
                        last = mm(w[:, c * P:(c + 1) * P], a[:, c * P:(c + 1) * P], b[:, c * P:(c + 1) * P],
                                  start=True, stop=True)
                    last.then_inc(wk_done[l % 2], 1)
                pe.wait_ge(sem("h_qk"), t + 1)
                turn_tile(("kt", t), 2, hZ[:, 1, :], 3)
                w = work_bank(("hs", t), 3)
                wait_read(pe, ("kt", t))
                for c in range(3):
                    last = mm(w[:, c * P:(c + 1) * P], hkt[:, c, :], hgi[:, c, t * P:(t + 1) * P],
                              start=True, stop=True)
                last.then_inc(wk_done[3], 1)
                w = work_bank(("ho", t), 2)
                pe.wait_ge(sem("h_s"), t + 1)
                for c in range(TT):
                    last = mm(w[:, c * P:(c + 1) * P], hgi[:, c, t * P:(t + 1) * P], hattn[:, c * P:(c + 1) * P],
                              start=True, stop=(c == 0))
                    if c:
                        last = mm(w[:, c * P:(c + 1) * P], hS[:, c - 1, :], hZ[:, 0, c * P:(c + 1) * P],
                                  start=False, stop=True)
                last.then_inc(wk_done[2], 1)
                w = work_bank(("hn", t), 3)
                wait_read(pe, ("ho", t))
                mm(w[:, :], ones, sq[:, t % 2, :], start=True, stop=True).then_inc(wk_done[3], 1)

            def nf(hd):
                w = work_bank(("nf", hd), 2)
                if hd == 0:
                    pe.wait_ge(sem("f_neg"), 1)
                mm(w[:, :], ident[0:FH, hd:hd + 1].broadcast_to([FH, P]), fneg[0:FH, :], start=True,
                   stop=True).then_inc(wk_done[2], 1)

            def fox_scores(u):
                hd, i = u // TT, u % TT
                w = work_bank(("fs", u), u % 2)
                po, ft = FD * (hd % 2), hd // 2
                mm(w[:, 0:(i + 1) * P], fq[po:po + FD, ft * S + i * P:ft * S + (i + 1) * P],
                   fk[po:po + FD, ft * S:ft * S + (i + 1) * P], start=True, stop=False)
                mm(w[:, i * P:(i + 1) * P], ident_bf[:, :], neg_bf[:, :], start=False, stop=True)\
                    .then_inc(wk_done[u % 2], 1)

            def fox_out(u):
                hd, i = u // TT, u % TT
                if u % 8 == 0:
                    work_bank(("fo", u // 8), 3)
                po = FD * (hd % 2)
                wait_read(pe, ("ft", u))
                for c in range(i + 1):
                    last = mm(work[3][po:po + FD, i * P:(i + 1) * P], fv[:, c, hd * FD:(hd + 1) * FD],
                              fPT[:, u % 2, c * P:(c + 1) * P], start=(c == 0), stop=(c == i))
                if u % 8 == 7:
                    last.then_inc(wk_done[3], 1)

            def mem_turn(t):
                pe.wait_ge(sem("mv_raw"), t + 1)
                turn_tile(("mv", t), 2, xt[:, t % 2, :], MT)

            norm(NORM["mem"])
            nf(0)
            fox_scores(0)
            for u in range(FH * TT):
                if u % 2 == 0:
                    n = u // 2
                    strip(AT["mem"] + n, XA, xn=tiles_from("mem") if n == 0 else None, w=NMEM)
                    if n > KT:
                        mem_turn(n - KT - 1)
                if u + 1 < FH * TT:
                    if (u + 1) % TT == 0:
                        nf((u + 1) // TT)
                    fox_scores(u + 1)
                pe.wait_ge(sem("f_p"), u + 1)
                turn_tile(("ft", u), 2, fS[:, u % 2, :], u % TT + 1)
                if u:
                    fox_out(u - 1)
            mem_turn(KT - 1)
            fox_out(FH * TT - 1)

            for n in range(KT):
                xn = [XN["rec"] + k for k in range(4)] + [XN["fox"] + k for k in range(4)]
                strip(AT["w_out"] + n, XB, kts=[4, 5, 6, 7, 0, 1, 2, 3], xn=None if n else xn)
            pe.wait_ge(x_ready, XN["w_out"] + KT)
            norm(NORM["w_out"])
            with pe.Fori(0, KT // 4) as i:
                for u in range(4):
                    strip(AT["xq"] + u, XA, i=i)

            def x_scores(u):
                a, i = u // TT, u % TT
                w = work_bank(("xs", u), u % 2)
                if u == 0:
                    pe.wait_ge(sem("xq_rdy"), 1)
                for c in range(2):
                    k = 2 * a + c
                    last = mm(w[:, 0:NMEM], xqf[:, k * S + i * P:k * S + (i + 1) * P],
                              memk[:, k * NMEM:(k + 1) * NMEM], start=(c == 0), stop=(c == 1))
                last.then_inc(wk_done[u % 2], 1)

            def x_out(k):
                a = k // 2
                wait_read(pe, ("xt", TT * a + TT - 1))
                w = work_bank(("xo", k), 3)
                for c in range(MT):
                    last = mm(w[:, :], memv[:, c, k * P:(k + 1) * P], xPT[:, a % 2, c, :],
                              start=(c == 0), stop=(c == MT - 1))
                last.then_inc(wk_done[3], 1)

            x_scores(0)
            for u in range(XH * TT):
                if u + 1 < XH * TT:
                    x_scores(u + 1)
                pe.wait_ge(sem("x_p"), u + 1)
                turn_tile(("xt", u), 2, xP[:, u % 2, :], MT)
                if u % 2 and u > TT:
                    x_out((u - 5) // 2)
            x_out(KT - 2)
            x_out(KT - 1)
            for n in range(KT):
                strip(AT["xo"] + n, XB, xn=tiles_from("xattn") if n == 0 else None)
            pe.wait_ge(x_ready, XN["xo"] + KT)
            norm(NORM["xo"])
            with pe.Fori(0, FF1 // D) as i:
                for u in range(KT):
                    strip(AT["ffn1"] + u, XA, i=i, per=16)
                for u in range(KT):
                    strip(AT["ffn1"] + KT + u, XB, i=i, per=16, xn=tiles_from("hid") if u == 0 else None)
            norm(NORM["final"])
            if LAST_BLOCK == 1:
                return

            norm(NORM["pre"])
            strip(AT["dt"], XA, xn=tiles_from("pre"))
            for n in range(2 * KT):
                strip(AT["glu"] + n, XA)
            w = work_bank("dacs", 2)
            pe.wait_ge(sem("s_acs"), 1)
            for c in range(TT):
                turn(w[:, c * NSH:(c + 1) * NSH], xt[0:NSH, 1, c * P:(c + 1) * P], ident[0:NSH, 0:NSH])
                last = turn(w[:, (TT + c) * NSH:(TT + c + 1) * NSH], acs[0:NSH, c * P:(c + 1) * P],
                            ident[0:NSH, 0:NSH])
            last.then_inc(wk_done[2], 1)

            def group_turns(g):
                x = xfs[g % 2]
                for q in range(2):
                    pe.wait_ge(sem("g_xf"), 4 * g + q + 1)
                    turn_tile(("x", g, q), q, x[q])
                pe.wait_ge(sem("g_xf"), 4 * g + 4)
                turn_tile(("b", g), 2, x[2], 3)
                w = work_bank(("cb", g), 3)
                for c in range(TT):
                    last = mm(w[:, c * P:(c + 1) * P], x[2][:, c * P:(c + 1) * P], x[3][:, c * P:(c + 1) * P],
                              start=True, stop=True)
                last.then_inc(wk_done[3], 1)

            def pair_states(g, q):
                w = work_bank(("st", g, q), 0)
                wait_read(pe, ("b", g))
                pe.wait_ge(sem("g_xde"), 2 * g + q + 1)
                for c in range(3):
                    last = mm(w[:, c * P:(c + 1) * P], btok[:, c, :], xde[:, c, q * P:(q + 1) * P],
                              start=True, stop=True)
                last.then_inc(wk_done[0], 1)

            def pair_out(g, q):
                w = work_bank(("y", g, q), 1)
                pe.wait_ge(sem("g_cp"), 2 * g + q + 1)
                pe.wait_ge(sem("g_ab"), 2 * g + q + 1)
                for hh in range(2):
                    o = w[hh * 64:(hh + 1) * 64, :]
                    for c in range(TT):
                        last = mm(o[:, c * P:(c + 1) * P], xdt[:, c, q * P + hh * 64:q * P + (hh + 1) * 64],
                                  Mm[:, hh, c * P:(c + 1) * P], start=True, stop=(c == 0))
                        if c:
                            last = mm(o[:, c * P:(c + 1) * P], Ss[:, c - 1, hh * 64:(hh + 1) * 64],
                                      Ab[:, hh, c * P:(c + 1) * P], start=False, stop=True)
                last.then_inc(wk_done[1], 1)

            def group_norm(g):
                w = work_bank(("gn", g), 3)
                pe.wait_ge(sem("g_sq"), g + 1)
                mm(w[:, :], ones, sq[:, 0, :], start=True, stop=False)
                mm(w[:, :], ones, sq[:, 1, :], start=False, stop=True).then_inc(wk_done[3], 1)

            for g in range(-1, GROUPS):
                for k in range(6):
                    if g + 1 < GROUPS:
                        strip(AT["ssd", g + 1, k], XA)
                        for t in OUT0_AT.get(k, []) if g == 4 else []:
                            strip(AT["out0", t], XB, xn=tiles_from("y0") if t == 0 else None)
                    else:
                        strip(AT["gssm"] + k, XA)
                    if g < 0:
                        continue
                    if k == 0:
                        group_turns(g)
                    elif k == 1:
                        if g:
                            group_norm(g - 1)
                        pair_states(g, 0)
                    elif k == 2:
                        pair_out(g, 0)
                    elif k == 4:
                        pair_states(g, 1)
                    elif k == 5:
                        pair_out(g, 1)
            strip(AT["gssm"] + 6, XA)
            group_norm(GROUPS - 1)
            strip(AT["gssm"] + 7, XA)
            for n in range(KT):
                strip(AT["ssmout1"] + n, XB, xn=tiles_from("y1") if n == 0 else None)
                if n == 2:
                    norm(NORM["conv"])
                if n == 5:
                    norm(NORM["conv"] + 1)
            for n in range(KT):
                strip(AT["gconv"] + n, XA)
            for n in range(KT):
                strip(AT["pw"] + n, XB, xn=tiles_from("conv") if n == 0 else None)
            for n in range(KT):
                strip(AT["w_out2"] + n, XA, xn=tiles_from("mix") if n == 0 else None)
            norm(NORM["post"])
            pe.wait_ge(x_ready, XN["ffn"] + KT)
            norm(NORM["ffn"])
            for c, nt in enumerate(CHUNK2):
                with pe.Fori(0, nt // 2) as i:
                    for u in range(4):
                        strip(AT[f"gu{c}"] + u, XA, i=i)
                for n in range(KT):
                    strip(AT[f"down{c}"] + n, XB, kts=range(nt), xn=tiles_from(f"g{c}", nt) if n == 0 else None)
            norm(NORM["ffpost"])

        @block.sync
        def _(sp):
            sp.dma_start(cst[:, :], consts).then_inc(loaded, 16)
            sp.dma_start(vec[:, :], vectors).then_inc(loaded, 16)
            sp.dma_start(h[:, :], xT).then_inc(loaded, 16)
            sp.dma_start(mem_in, memT).then_inc(loaded, 16)
            for j in range(2):
                sp.dma_start(raw[j % 2][:, :], weights[j]).then_inc(raw_ready[j % 2], 16)
            turns = (NS_FULL - 2) // 2
            with sp.Fori(0, turns) as i:
                for u in range(2):
                    sp.wait_ge(w_lo, i * 2 + (u + 1))
                    sp.dma_start(raw[u][:, :], weights[bass.ds(i * 2 + (2 + u), 1), :, :].rearrange("a p n -> (a p) n"))\
                        .then_inc(raw_ready[u], 16)
            for j in range(2 * turns + 2, NS):
                sp.wait_ge(w_lo, j - 1)
                w = weights[j] if j < NS_FULL else weights6[j - NS_FULL]
                sp.dma_start(raw[j % 2][:, 0:w.shape[1]], w).then_inc(raw_ready[j % 2], 16)
            sp.wait_ge(sem("result"), KT)
            sp.dma_start(outT, h[:, :]).then_inc(loaded, 16)
            sp.wait_ge(loaded, 16 * 5)

        @block.gpsimd
        def _(pool):
            def low(s, r, j, i):
                pool.wait_ge(w_hi, val(j + 1, i, 4))
                nc.gpsimd.tensor_tensor(wl[s][:, :], raw[r][:, :], wh[s][:, :].bitcast(F32), ALU.subtract)\
                    .then_inc(w_lo, 1)

            first = (AT["ssd", 0, 0] + 4) // 4 * 4
            with pool.Fori(0, first // 4) as i:
                for u in range(4):
                    low(u, u % 2, u, i)
            if LAST_BLOCK == 1:
                return

            def decays(g, q):
                n, hd = 2 * g + q, 4 * g + 2 * q
                a4 = Ab.rearrange("p h (c l) -> p h c l", c=TT)
                acol = dacs[:, 1, :, hd:hd + 2].rearrange("p c (h o) -> p h c o", o=1)
                pool.wait_ge(sem("spread"), 16 * (n + 1))
                if n == 0:
                    wait_read(pool, "dacs")
                sub = nc.gpsimd.tensor_tensor
                sub(s_dte.rearrange("p (h c o) -> p h c o", h=2, o=1), a4[:, :, :, P - 1:P], acol, ALU.subtract)
                sub(Mm.rearrange("p h (c l) -> p h c l", c=TT), a4, acol.broadcast_to([P, 2, TT, P]), ALU.subtract)
                pool.drain()
                nc.gpsimd.tensor_scalar(Mm[:, :, :], Mm[:, :, :], 0.0, None, ALU.min)
                pool.drain().then_inc(sem("g_seg"), 1)

            def decayed_c(g, q):
                pool.wait_ge(sem("g_exp"), 3 * (2 * g + q) + 3)
                pool.wait_ge(sem("g_xf"), 4 * g + 4)
                c = xfs[g % 2][3].rearrange("p (a b) -> p a b", a=1)
                nc.gpsimd.tensor_tensor(Ab[:, :, :], Ab[:, :, :], c.broadcast_to([P, 2, S]), ALU.mult)
                pool.drain().then_inc(sem("g_ab"), 1)

            j = first
            for g in range(-1, GROUPS):
                for k in range(6):
                    at_slot = AT["ssd", g + 1, k] if g + 1 < GROUPS else AT["gssm"] + k
                    at_slot += len(OUT0_AT.get(k, [])) if g == 4 else 0
                    while j <= at_slot + 4:
                        low(j % 4, j % 2, j, None)
                        j += 1
                    if k == 5 and g + 1 < GROUPS:
                        decays(g + 1, 0)
                    if k == 2 and g >= 0:
                        decays(g, 1)
                    if k in (1, 4) and g >= 0:
                        decayed_c(g, k // 3)
            while j % 4:
                low(j % 4, j % 2, j, None)
                j += 1
            with pool.Fori(0, (NS - j) // 4) as i:
                for u in range(4):
                    pool.wait_ge(w_hi, i * 4 + (j + u + 1))
                    nc.gpsimd.tensor_tensor(wl[u][:, :], raw[u % 2][:, :], wh[u][:, :].bitcast(F32), ALU.subtract)\
                        .then_inc(w_lo, 1)
            for j in range(j + (NS - j) // 4 * 4, NS):
                low(j % 4, j % 2, j, None)

        @block.scalar
        def _(act):
            act_ = nc.scalar.activation

            def high(j, i=None, per=4):
                act.wait_ge(raw_ready[j % 2], val(16 * (j // 2 + 1), i, 8 * per))
                act_(wh[j % 4][:, :], raw[j % 2][:, :], ACT.Copy).then_inc(w_hi, 1)

            def step(j, i=None, per=4, last=False):
                if j + 4 < NS and not last:
                    act.wait_ge(strip_done, val(j + 1, i, per))
                    high(j + 4, i, per)

            def square(src, t, k, w=S):
                act.wait_ge(h_upd, k + 1)
                act_(sq[:, t % 2, 0:w], src, ACT.Square).then_inc(sq_done, 1)

            def high_tile(src, g, t, k, w=S):
                act.wait_ge(h_upd, k + 1)
                act_(tile(XA[0], t, w), src, ACT.Identity, scale=g).then_inc(hi_done, 1)
                act_(sq[:, t % 2, 0:w], src, ACT.Square).then_inc(sq_done, 1)

            def root(k, b=3, scale=1.0 / D, eps=EPS, dst=std, w=S):
                ps = wait_full(act, ("norm", k))
                free(act_(dst[:, 0:w], ps[:, 0:w], ACT.Sqrt, bias=eps_ap(eps), scale=scale), ("norm", k))

            def eps_ap(e):
                return cst[:, COFF["eps"] + (0 if e == EPS else 1):COFF["eps"] + (0 if e == EPS else 1) + 1]

            act.wait_ge(loaded, 64)
            act_(ident_bf[:, :], ident, ACT.Copy)
            act_(neg_bf[:, :], C("neg"), ACT.Copy).then_inc(const_rdy, 1)
            for t in range(4):
                high(t)
            for t in range(KT):
                high_tile(tile(h, t), V("mix_g", t), t, SQN["in"] + t)
            root(NORM["in"])
            act.wait_ge(sem("lb_sub"), 1)
            act_(s_tmp[:, 4:12], s_tmp[:, 4:12], ACT.Exp).then_inc(sem("lb_exp"), 1)
            for n in range(4 * HG):
                step(AT["hgrn"] + n)
                t = n % 4
                if n < 4:
                    act.wait_ge(sem("hg_raw"), n + 1)
                    act_(tile(hb, t), tile(hkk, t), ACT.Sigmoid)
                    act_(tile(hkk, t), tile(hkk, t), ACT.Sigmoid, scale=-1.0).then_inc(sem("hg_sig"), 1)
                elif n < 8 or n >= 12:
                    act.wait_ge(sem("hg_raw"), n + 1)
                    src = hqq if n < 8 else hgg
                    act_(sq[:, t % 2, :], tile(src, t), ACT.Sigmoid).then_inc(sem("hg_sig"), 1)
                if 9 <= n <= 12:
                    ps = wait_full(act, ("gi", n - 9))
                    free(act_(hgi[:, :, (n - 9) * P:(n - 8) * P], blocks(ps[:, :]), ACT.Copy), ("gi", n - 9))
            step(AT["fox"])
            for t in range(HG):
                act.wait_ge(sem("hg_f"), t + 1)
                act_(tile(hb, t), tile(hb, t), ACT.Ln).then_inc(sem("hg_ln"), 1)

            def out_root(t):
                ps = wait_full(act, ("hn", t))
                free(act_(std[:, :], ps[:, :], ACT.Sqrt, bias=eps_ap(EPS), scale=1.0 / P), ("hn", t))

            for t in range(HG):
                for l in range(LEVELS):
                    if (t, l) in FILL:
                        n = FILL[t, l]
                        step(AT["fox"] + n)
                        if 2 <= n <= 5:
                            ps = wait_full(act, ("fv", n - 2))
                            free(act_(fv[:, :, (n - 2) * P:(n - 1) * P], blocks(ps[:, :]), ACT.Copy), ("fv", n - 2))
                    if l:
                        half = 1 << (l - 1)
                        e = hE[:, l % 2, :].rearrange("p (n c) -> p n c", c=2 * half)
                        act.wait_ge(sem("h_d"), 7 * t + l)
                        act_(e[:, :, 0:half], e[:, :, 0:half], ACT.Exp, scale=-1.0)
                        act_(e[:, :, half:], e[:, :, half:], ACT.Exp).then_inc(sem("h_e"), 1)
                    if l == 3 and t:
                        out_root(t - 1)
                act.wait_ge(sem("h_end"), t + 1)
                act_(hE[:, 1, :], hE[:, 1, :], ACT.Exp)
                act_(hE[:, 0, :], tile(hb, t), ACT.Exp).then_inc(sem("h_eb"), 1)
                ps = wait_full(act, ("kt", t))
                free(act_(hkt[:, :, :], blocks(ps[:, 0:3 * P]), ACT.Copy), ("kt", t))
                ps = wait_full(act, ("ho", t))
                act_(tile(hb, t), ps[:, :], ACT.Copy)
                free(act_(sq[:, t % 2, :], ps[:, :], ACT.Square), ("ho", t))
            out_root(HG - 1)

            for t in range(KT):
                high_tile(mem_in[:, t * NMEM:(t + 1) * NMEM], V("mem_g", t), t, SQN["mem"] + t, NMEM)
            root(NORM["mem"], w=NMEM)
            act.wait_ge(sem("f_abs"), 1)
            act_(xt[0:FH, 0, :], xt[0:FH, 0, :], ACT.Exp, scale=-1.0).then_inc(sem("f_exp"), 1)
            act.wait_ge(sem("f_one"), 1)
            act_(xt[0:FH, 1, :], xt[0:FH, 1, :], ACT.Ln).then_inc(sem("f_exp"), 1)

            def nf(hd):
                ps = wait_full(act, ("nf", hd))
                free(act_(nfb[:, hd % 2, :], ps[:, :], ACT.Copy), ("nf", hd))

            def fox_exp(u):
                n = (u % TT + 1) * P
                act.wait_ge(sem("f_s"), u + 1)
                act_(fS[:, u % 2, 0:n], fS[:, u % 2, 0:n], ACT.Exp, bias=s_nm[:, u % 2:u % 2 + 1], scale=-1.0,
                     accum_out=s_rs[:, u % 2:u % 2 + 1]).then_inc(sem("f_e"), 1)

            def mem_turned(t):
                ps = wait_full(act, ("mv", t))
                free(act_(memv[:, :, t * P:(t + 1) * P], blocks(ps[:, 0:NMEM]), ACT.Copy), ("mv", t))

            nf(0)
            for u in range(FH * TT):
                fox_exp(u)
                if u % 2 == 0:
                    n = u // 2
                    step(AT["mem"] + n)
                    if n > KT:
                        mem_turned(n - KT - 1)
                if (u + 1) % TT == 0 and u + 1 < FH * TT:
                    nf((u + 1) // TT)
                n = (u % TT + 1) * P
                ps = wait_full(act, ("ft", u))
                free(act_(fPT[:, u % 2, 0:n], ps[:, 0:n], ACT.Copy), ("ft", u))
            mem_turned(KT - 1)

            for n in range(KT):
                step(AT["w_out"] + n)
                high_tile(tile(h, n), V("x_g", n), n, SQN["w_out"] + n)
            root(NORM["w_out"])
            with act.Fori(0, KT // 4) as i:
                for u in range(4):
                    step(AT["xq"] + u, i)
            for u in range(XH * TT):
                a, i = u // TT, u % TT
                act.wait_ge(sem("x_m"), u + 1)
                ps = wait_full(act, ("xs", u))
                free(act_(xP[:, u % 2, :], ps[:, 0:NMEM], ACT.Exp, bias=s_nm[:, u % 2:u % 2 + 1],
                          accum_out=s_rs[:, u % 2:u % 2 + 1]), ("xs", u))
                ps = wait_full(act, ("xt", u))
                free(act_(xPT[:, a % 2, :, i * P:(i + 1) * P], blocks(ps[:, 0:NMEM]), ACT.Copy), ("xt", u))
            for n in range(KT):
                step(AT["xo"] + n)
                high_tile(tile(h, n), V("ff_g", n), n, SQN["xo"] + n)
            root(NORM["xo"])
            with act.Fori(0, FF1 // D - 1) as i:
                for u in range(16):
                    step(AT["ffn1"] + u, i, 16)
            for u in range(16):
                step(AT["ffn1"] + 48 + u)
                if u >= KT:
                    square(tile(h, u - KT), u, SQN["final"] + u - KT)
            root(NORM["final"])
            if LAST_BLOCK == 1:
                return

            for t in range(KT):
                square(tile(h, t), t, SQN["pre"] + t)
            root(NORM["pre"])
            for t in range(KT):
                act.wait_ge(sem("pre_x"), t + 1)
                act_(tile(XA[0], t), xt[:, t % 2, :], ACT.Copy).then_inc(hi_done, 1)
            step(AT["dt"])
            act.wait_ge(sem("s_abs"), 1)
            act_(xt[0:NSH, 0, :], xt[0:NSH, 0, :], ACT.Exp, scale=-1.0)
            act_(s_nea[0:NSH, :], V("a_log")[0:NSH, :], ACT.Exp).then_inc(sem("s_exp"), 1)
            act.wait_ge(sem("s_one"), 1)
            act_(xt[0:NSH, 1, :], xt[0:NSH, 1, :], ACT.Ln).then_inc(sem("s_exp"), 1)
            act.wait_ge(sem("s_acs"), 1)
            act.dma_start(scratch, acs[0:NSH, :]).then_inc(sem("acs_out"), 16)
            for n in range(2 * KT):
                j, t = AT["glu"] + n, n // 2
                step(j)
                if n % 2:
                    if t > 1:
                        act.wait_ge(sem("glu_v"), t - 1)
                    act.wait_ge(strip_done, j + 1)
                    act_(sq[:, t % 2, :], bank[j % 4][:, :], ACT.Sigmoid, bias=V("glu_b", KT + t))
                    act.drain().then_inc(bank_free[j % 4], 1)
            ps = wait_full(act, "dacs")
            free(act_(dacs.rearrange("p a b c -> p (a b c)"), ps[:, 0:2 * TT * NSH], ACT.Copy), "dacs")

            def spread(n):
                if n:
                    act.wait_ge(wk_done[1], uses[("y", (n - 1) // 2, (n - 1) % 2)][1] + 1)
                act.dma_start(Ab[:, :, :], scratch[2 * n:2 * n + 2, :].partition_broadcast(P))\
                    .then_inc(sem("spread"), 16)

            def leave(ins, j):
                ins.then_inc(bank_free[j % 4], 1)

            def group_in(g, k):
                j = AT["ssd", g, k]
                step(j)
                act.wait_ge(strip_done, j + 1)
                ps = bank[j % 4]
                if k < 4:
                    c, x = 4 * g + k, xt[:, k % 2, :]
                    if c >= 2:
                        act.wait_ge(sem("g_raw"), c - 1)
                    r = rawp[:, k % 2, :]
                    leave(act_(r[:, SK - 1:], ps[:, :], ACT.Copy), j)
                    act.drain()
                    ct = [2 * g, 2 * g + 1, 16 + g, 24 + g][k]
                    act_(x, r[:, 0:S], ACT.Identity, bias=V("sc_b", ct), scale=V("sc_w", ct * SK))
                    act.drain().then_inc(sem("g_tap"), 1)
                else:
                    if g >= 2:
                        act.wait_ge(x_ready, x_of_group(g - 2) + 2)
                    leave(act_(zs2[:, g % 2, k - 4, :], ps[:, :], ACT.Silu), j)
                    act.drain().then_inc(sem("g_z"), 1)
                if 1 <= k <= 4:
                    act.wait_ge(sem("g_raw"), 4 * g + k)
                    if g >= 2:
                        act.wait_ge(sem("g_y"), 2 * g - 2)
                    act_(xfs[g % 2][k - 1], xt[:, (k - 1) % 2, :], ACT.Silu).then_inc(sem("g_xf"), 1)

            def x_of_group(g):
                return XN["y0" if g < 4 else "y1"] + 2 * (g % 4)

            def exps(g, q):
                n = 2 * g + q
                act.wait_ge(sem("g_seg"), n + 1)
                act_(s_dte, s_dte, ACT.Exp).then_inc(sem("g_exp"), 1)
                act_(Mm[:, :, :], Mm[:, :, :], ACT.Exp).then_inc(sem("g_exp"), 1)
                a4 = Ab.rearrange("p h (c l) -> p h c l", c=TT)
                act_(s_dl.rearrange("p (h c o) -> p h c o", h=2, o=1), a4[:, :, :, P - 1:P], ACT.Exp)
                act.drain()
                act_(Ab[:, :, :], Ab[:, :, :], ACT.Exp)
                act.drain().then_inc(sem("g_exp"), 1)

            def y_square(g, q):
                act.wait_ge(sem("g_y"), 2 * g + q + 1)
                ins = act_(sq[:, q, :], zs2[:, g % 2, q, :], ACT.Square)
                if q:
                    ins.then_inc(sem("g_sq"), 1)

            def group_root(g):
                ps = wait_full(act, ("gn", g))
                free(act_(std[:, :], ps[:, :], ACT.Sqrt, bias=eps_ap(EPS), scale=1.0 / (2 * P)), ("gn", g))

            def gate(name, col, t, after=None):
                j = AT[name] + t
                step(j)
                act.wait_ge(strip_done, j + 1)
                if after:
                    act.wait_ge(*after)
                leave(act_(gates[t], bank[j % 4][:, :], ACT.Sigmoid, bias=V("gate_b", col + t)), j)

            act.wait_ge(sem("acs_out"), 16)
            spread(0)
            for g in range(-1, GROUPS):
                for k in range(6):
                    if g + 1 < GROUPS:
                        group_in(g + 1, k)
                        for t in OUT0_AT.get(k, []) if g == 4 else []:
                            j = AT["out0", t]
                            step(j)
                            if t == 0:
                                act.wait_ge(sem("dw_out"), 16)
                            act.wait_ge(strip_done, j + 1)
                            leave(act_(tile(acc, t), bank[j % 4][:, :], ACT.Copy), j)
                    else:
                        gate("gssm", KT, k, (sem("g_y"), 13 + k) if k < 2 else (x_ready, x_of_group(6) + 2))
                    if g < 0:
                        continue
                    if k == 0:
                        if g:
                            y_square(g - 1, 1)
                        exps(g, 0)
                        ps = wait_full(act, ("b", g))
                        free(act_(btok[:, :, :], blocks(ps[:, 0:3 * P]), ACT.Copy), ("b", g))
                    elif k == 1 and g:
                        group_root(g - 1)
                    elif k == 2:
                        spread(2 * g + 1)
                    elif k == 3:
                        exps(g, 1)
                    elif k == 4:
                        y_square(g, 0)
                    elif k == 5 and g + 1 < GROUPS:
                        spread(2 * g + 2)
                if g == 3:
                    act.wait_ge(sem("dw_done"), 1)
                    act.dma_start(spill, vpad[:, :, 0:S]).then_inc(sem("dw_out"), 16)
            y_square(GROUPS - 1, 1)
            act.dma_start(cv.rearrange("p (a b) -> p a b", a=KT), spill).then_inc(sem("cv_in"), 16)
            gate("gssm", KT, 6)
            group_root(GROUPS - 1)
            gate("gssm", KT, 7)
            act.drain().then_inc(sem("gates_s"), 1)
            for n in range(KT):
                step(AT["ssmout1"] + n)
                if n == 2:
                    ps = wait_full(act, ("norm", NORM["conv"]))
                    free(act_(mu, ps[:, :], ACT.Copy, scale=1.0 / D), ("norm", NORM["conv"]))
                    for t in range(KT):
                        square(tile(cv, t), t, SQN["conv"] + t)
                if n == 5:
                    root(NORM["conv"] + 1, eps=LN_EPS)
            for t in range(KT):
                act.wait_ge(sem("ln_x"), t + 1)
                act_(tile(cv, t), tile(cv, t), ACT.Silu, bias=V("ln_b", t))
            act.drain()
            for t in range(KT):
                act.wait_ge(strip_done, AT["ssmout1"] + KT)
                act_(tile(XB[0], t), tile(cv, t), ACT.Copy)
                act.drain().then_inc(hi_done, 1)
            for t in range(KT):
                gate("gconv", 0, t, (sem("acc_g"), KT))
            act.drain().then_inc(sem("gates_s"), 1)
            for t in range(KT):
                step(AT["pw"] + t)
                act.wait_ge(sem("mixed"), t + 1)
                act_(tile(XA[0], t), tile(acc, t), ACT.Copy).then_inc(hi_done, 1)
            for n in range(KT):
                j = AT["w_out2"] + n
                step(j)
                act.wait_ge(strip_done, j + 1)
                if n == 0:
                    act.wait_ge(x_ready, XN["mix"] + KT)
                act_(tile(cv, n), bank[j % 4][:, :], ACT.Copy)
                act.wait_ge(h_upd, SQN["post"] + n + 1)
                leave(act_(sq[:, n % 2, :], bank[j % 4][:, :], ACT.Square), j)
                act.drain().then_inc(sq_done, 1)
            root(NORM["post"])
            for n in range(KT):
                high_tile(tile(h, n), V("ffn_g", n), n, SQN["ffn"] + n)
            root(NORM["ffn"])
            k = 0
            for c, nt in enumerate(CHUNK2):
                turns = nt // 2
                with act.Fori(0, turns) as i:
                    for u in range(4):
                        step(AT[f"gu{c}"] + u, i)
                        if u % 2 == 0:
                            act.wait_ge(sem("ff_g"), i * 2 + (k + u // 2 + 1))
                            act_(sq[:, u // 2, :], xt[:, u // 2, :], ACT.Sigmoid).then_inc(sem("ff_s"), 1)
                k += nt
                for n in range(KT):
                    step(AT[f"down{c}"] + n)
                    if c == 2:
                        square(tile(acc, n), n, SQN["ffpost"] + n)
            root(NORM["ffpost"])

        @block.vector
        def _(dve):
            TTop, STT, TS = nc.vector.tensor_tensor, nc.vector.scalar_tensor_tensor, nc.vector.tensor_scalar
            copy = nc.vector.tensor_copy

            def taken(j, i=None, per=4):
                dve.wait_ge(strip_done, val(j + 1, i, per))
                return bank[j % 4]

            def leave(ins, j):
                ins.then_inc(bank_free[j % 4], 1)

            def split(src, X, k, w=S):
                copy(tile(X[0], k, w), src)
                dve.drain()
                TTop(tile(X[1], k, w), src, tile(X[0], k, w).bitcast(F32), ALU.subtract).then_inc(x_ready, 1)

            def sum_square(t, k, w=S):
                dve.wait_ge(sq_done, k + 1)
                if t == 0:
                    copy(ssum[:, 0:w], sq[:, 0, 0:w])
                else:
                    TTop(ssum[:, 0:w], ssum[:, 0:w], sq[:, t % 2, 0:w], ALU.add)
                dve.drain()

            def low_tile(src, g, t, name, w=S):
                dve.wait_ge(hi_done, HI[name] + t + 1)
                STT(tile(XA[1], t, w), src, g, tile(XA[0], t, w).bitcast(F32), ALU.mult, ALU.subtract)\
                    .then_inc(x_ready, 1)
                sum_square(t, SQN[name] + t, w)

            def prep(src, g, name, w=S):
                for t in range(KT):
                    dve.drain().then_inc(h_upd, 1)
                    if t:
                        low_tile(src(t - 1), V(g, t - 1), t - 1, name, w)
                low_tile(src(KT - 1), V(g, KT - 1), KT - 1, name, w)

            def invert(k, dst, w=S):
                dve.drain().then_inc(ssum_rdy, 1)
                wait_read(dve, ("norm", k))
                nc.vector.reciprocal(dst[:, 0:w], std[:, 0:w])
                dve.drain()

            def residual(n, name, j, g=None):
                ps = taken(j)
                leave(TTop(tile(h, n), tile(h, n), ps[:, :], ALU.add), j)
                dve.drain().then_inc(h_upd, 1)
                for t in ([n - 1] if n else []) + ([n] if n == KT - 1 else []):
                    if g is None:
                        sum_square(t, SQN[name] + t)
                    else:
                        low_tile(tile(h, t), V(g, t), t, name)

            dve.wait_ge(loaded, 64)
            prep(lambda t: tile(h, t), "mix_g", "in")
            TTop(s_tmp[:, 0:4], V("lb0", 0, 4), V("lb1", 0, 4), ALU.max)
            dve.drain()
            TTop(s_tmp[:, 4:8], V("lb0", 0, 4), s_tmp[:, 0:4], ALU.subtract)
            TTop(s_tmp[:, 8:12], V("lb1", 0, 4), s_tmp[:, 0:4], ALU.subtract)
            dve.drain().then_inc(sem("lb_sub"), 1)
            invert(NORM["in"], rstd)
            for n in range(4 * HG):
                j, t = AT["hgrn"] + n, n % 4
                ps = taken(j)
                dst = [tile(hkk, t), tile(hqq, t), xt[:, t % 2, :], tile(hgg, t)][n // 4]
                if 10 <= n <= 11:
                    dve.wait_ge(wk_done[t % 2], uses[("gi", t - 2)][1] + 1)
                leave(TTop(dst, ps[:, :], rstd[:, :], ALU.mult), j)
                dve.drain().then_inc(sem("hg_raw"), 1)
                if n < 4:
                    dve.wait_ge(sem("hg_sig"), n + 1)
                    if n == 0:
                        dve.wait_ge(sem("lb_exp"), 1)
                        TTop(s_tmp[:, 0:4], s_tmp[:, 4:8], s_tmp[:, 8:12], ALU.add)
                        dve.drain()
                        nc.vector.reciprocal(s_tmp[:, 12:16], s_tmp[:, 0:4])
                        dve.drain()
                        TTop(s_lb, s_tmp[:, 4:8], s_tmp[:, 12:16], ALU.mult)
                        TTop(s_oml, s_tmp[:, 8:12], s_tmp[:, 12:16], ALU.mult)
                        dve.drain()
                    TS(tile(hb, t), tile(hb, t), s_oml[:, t:t + 1], s_lb[:, t:t + 1], ALU.mult, ALU.add)
                    TS(tile(hkk, t), tile(hkk, t), s_oml[:, t:t + 1], None, ALU.mult)
                    dve.drain().then_inc(sem("hg_f"), 1)
                elif n < 8 or n >= 12:
                    dve.wait_ge(sem("hg_sig"), n + 1 if n < 8 else n - 3)
                    TTop(dst, dst, sq[:, t % 2, :], ALU.mult)
                    dve.drain()

            def fox_in(n):
                j = AT["fox"] + n
                name, t = STREAM[j]
                ps = taken(j)
                if name == "ff":
                    leave(TTop(fneg[0:FH, :], ps[0:FH, :], rstd[0:FH, :], ALU.mult), j)
                elif name == "fv":
                    if t >= 2:
                        dve.wait_ge(wk_done[2], uses[("fv", t - 2)][1] + 1)
                    leave(TTop(xt[:, t % 2, :], ps[:, :], rstd[:, :], ALU.mult), j)
                    dve.drain().then_inc(sem("fv_raw"), 1)
                elif name == "fq":
                    leave(STT(tile(fq, t), ps[:, :], FD ** -0.5, rstd[:, :], ALU.mult, ALU.mult), j)
                else:
                    leave(TTop(tile(fk, t), ps[:, :], rstd[:, :], ALU.mult), j)

            for t in (2, 3):
                dve.wait_ge(wk_done[t % 2], uses[("gi", t)][1] + 1)
            fox_in(0)
            for t in range(HG):
                dve.wait_ge(sem("hg_ln"), t + 1)
                nc.vector.tensor_tensor_scan(tile(hb, t), reset, tile(hb, t), 0.0, ALU.mult, ALU.add)
            dve.drain().then_inc(sem("hg_scan"), 1)

            def out_norm(t):
                wait_read(dve, ("hn", t))
                nc.vector.reciprocal(std[:, :], std[:, :])
                dve.drain()
                TTop(tile(hb, t), tile(hb, t), std[:, :], ALU.mult)
                dve.drain()
                STT(tile(hb, t), tile(hb, t), V("hgrn_g"), tile(hgg, t), ALU.mult, ALU.mult)
                dve.drain()

            def distance(t, l):
                half = 1 << (l - 1)
                b = tile(hb, t).rearrange("p (n c) -> p n c", c=2 * half)
                TTop(hE[:, l % 2, :].rearrange("p (n c) -> p n c", c=2 * half), b,
                     b[:, :, half - 1:half].broadcast_to([P, S // (2 * half), 2 * half]), ALU.subtract)\
                    .then_inc(sem("h_d"), 1)

            def gather(t, l):
                ps = wait_full(dve, ("level", t, l))
                mask = C("lev", l).rearrange("p (a b) -> p a b", a=1).broadcast_to([P, TT, P])
                if l == 0:
                    if t:
                        dve.wait_ge(wk_done[2], uses[("ho", t - 1)][1] + 1)
                    free(TTop(blocks(hattn), blocks(ps[:, :]), mask, ALU.mult), ("level", t, l))
                else:
                    free(nc.vector.copy_predicated(blocks(hattn), mask.bitcast(I32), blocks(ps[:, :])),
                         ("level", t, l))
                dve.drain()

            for t in range(HG):
                distance(t, 1)
                gather(t, 0)
                for l in range(1, LEVELS):
                    if (t, l) in FILL:
                        fox_in(FILL[t, l])
                        dve.drain()
                    if l + 1 < LEVELS:
                        distance(t, l + 1)
                    half = 1 << (l - 1)

                    def halves(a, k):
                        return a.rearrange("p (n c) -> p n c", c=2 * half)[:, :, k * half:(k + 1) * half]

                    dve.wait_ge(sem("h_e"), 7 * t + l)
                    if l <= 2 and t:
                        dve.wait_ge(wk_done[2], uses[("ho", t - 1)][1] + 1)
                    e, z = hE[:, l % 2, :], hZ[:, l % 2, :]
                    TTop(halves(z, 0), halves(tile(hkk, t), 0), halves(e, 0), ALU.mult)
                    TTop(halves(z, 1), halves(tile(hqq, t), 1), halves(e, 1), ALU.mult)
                    dve.drain().then_inc(sem("h_z"), 1)
                    if l > 1:
                        gather(t, l - 1)
                    if l == 4 and t:
                        out_norm(t - 1)
                gather(t, LEVELS - 1)
                b = blocks(tile(hb, t))
                TTop(blocks(hE[:, 1, :]), b[:, :, P - 1:P].broadcast_to([P, TT, P]), b, ALU.subtract)\
                    .then_inc(sem("h_end"), 1)
                dve.wait_ge(sem("h_eb"), t + 1)
                TTop(hZ[:, 1, :], tile(hkk, t), hE[:, 1, :], ALU.mult)
                TTop(hZ[:, 0, :], tile(hqq, t), hE[:, 0, :], ALU.mult)
                copy(s_eb, hE[:, 0, P - 1::P])
                dve.drain().then_inc(sem("h_qk"), 1)
                ps = wait_full(dve, ("hs", t))
                copy(hS[:, 0, :], ps[:, 0:P])
                dve.drain()
                STT(hS[:, 1, :], hS[:, 0, :], s_eb[:, 1:2], ps[:, P:2 * P], ALU.mult, ALU.add)
                dve.drain()
                free(STT(hS[:, 2, :], hS[:, 1, :], s_eb[:, 2:3], ps[:, 2 * P:3 * P], ALU.mult, ALU.add), ("hs", t))
                dve.drain().then_inc(sem("h_s"), 1)
            out_norm(HG - 1)
            for t in range(HG):
                split(tile(hb, t), XB, 4 + t)
            dve.drain()

            dve.wait_ge(strip_done, AT["mem"])
            prep(lambda t: mem_in[:, t * NMEM:(t + 1) * NMEM], "mem_g", "mem", NMEM)
            invert(NORM["mem"], memrstd, NMEM)
            TS(fneg[0:FH, :], fneg[0:FH, :], V("foxb")[0:FH, :], None, ALU.add)
            dve.drain()
            STT(xt[0:FH, 0, :], fneg[0:FH, :], -1.0, fneg[0:FH, :], ALU.mult, ALU.max)
            dve.drain().then_inc(sem("f_abs"), 1)

            def log1p(rows, exp_done, one):
                dve.wait_ge(exp_done, 1)
                TS(xt[0:rows, 1, :], xt[0:rows, 0, :], 1.0, None, ALU.add)
                dve.drain()
                TS(ssum[0:rows, :], xt[0:rows, 1, :], -1.0, None, ALU.add)
                dve.drain()
                TTop(xt[0:rows, 0, :], xt[0:rows, 0, :], ssum[0:rows, :], ALU.subtract)
                dve.drain().then_inc(one, 1)
                dve.wait_ge(exp_done, 2)
                TTop(xt[0:rows, 1, :], xt[0:rows, 1, :], xt[0:rows, 0, :], ALU.add)
                dve.drain()

            log1p(FH, sem("f_exp"), sem("f_one"))
            STT(xt[0:FH, 1, :], fneg[0:FH, :], 0.0, xt[0:FH, 1, :], ALU.min, ALU.subtract)
            dve.drain()
            TS(ssum[0:FH, :], xt[0:FH, 1, :], 0.0, 1.0, ALU.mult, ALU.add)
            dve.drain()
            nc.vector.tensor_tensor_scan(fneg[0:FH, :], ssum[0:FH, :], xt[0:FH, 1, :], 0.0, ALU.mult, ALU.subtract)
            dve.drain().then_inc(sem("f_neg"), 1)

            def fox_logits(u):
                hd, n = u // TT, (u % TT + 1) * P
                if u % TT == 0:
                    wait_read(dve, ("nf", hd))
                ps = wait_full(dve, ("fs", u))
                if u >= 2:
                    dve.wait_ge(wk_done[2], uses[("ft", u - 2)][1] + 1)
                free(nc.vector.tensor_tensor_reduce(
                    out=fS[:, u % 2, 0:n], in0=ps[:, 0:n], in1=nfb[:, hd % 2, 0:n], scale=-1.0, scalar=3.0e38,
                    op0=ALU.add, op1=ALU.min, accum_out=s_nm[:, u % 2:u % 2 + 1]), ("fs", u))
                dve.drain().then_inc(sem("f_s"), 1)

            def mem_in_strip(n):
                j = AT["mem"] + n
                ps = taken(j)
                if n < KT:
                    leave(TTop(memk[:, n * NMEM:(n + 1) * NMEM], ps[:, 0:NMEM], memrstd, ALU.mult), j)
                else:
                    t = n - KT
                    if t >= 2:
                        dve.wait_ge(wk_done[2], uses[("mv", t - 2)][1] + 1)
                    leave(TTop(xt[:, t % 2, 0:NMEM], ps[:, 0:NMEM], memrstd, ALU.mult), j)
                    dve.drain().then_inc(sem("mv_raw"), 1)

            def normalise(sums_ready, n, a, u, done):
                dve.wait_ge(sums_ready, u + 1) if sums_ready is not None else None
                nc.vector.reciprocal(s_ri[:, u % 2:u % 2 + 1], s_rs[:, u % 2:u % 2 + 1])
                dve.drain()
                TS(a[:, u % 2, 0:n], a[:, u % 2, 0:n], s_ri[:, u % 2:u % 2 + 1], None, ALU.mult)
                dve.drain().then_inc(done, 1)

            def split_work(key, k):
                ps = wait_full(dve, key)
                copy(tile(XB[0], k), ps[:, :])
                dve.drain()
                free(TTop(tile(XB[1], k), ps[:, :], tile(XB[0], k).bitcast(F32), ALU.subtract), key)
                dve.drain().then_inc(x_ready, 1)

            fox_logits(0)
            for u in range(FH * TT):
                if u % 2 == 0:
                    mem_in_strip(u // 2)
                if u + 1 < FH * TT:
                    fox_logits(u + 1)
                normalise(sem("f_e"), (u % TT + 1) * P, fS, u, sem("f_p"))
                if u % 8 == 1 and u > 8:
                    split_work(("fo", u // 8 - 1), u // 8 - 1)
            split_work(("fo", 3), 3)

            for n in range(KT):
                residual(n, "w_out", AT["w_out"] + n, "x_g")
            invert(NORM["w_out"], rstd)
            with dve.Fori(0, KT // 4) as i:
                for u in range(4):
                    ps = taken(AT["xq"] + u, i)
                    leave(STT(tile(xqf, i * 4 + u), ps[:, :], XD ** -0.5, rstd[:, :], ALU.mult, ALU.mult), AT["xq"] + u)
            dve.drain().then_inc(sem("xq_rdy"), 1)

            def x_max(u):
                ps = wait_full(dve, ("xs", u))
                nc.vector.tensor_reduce(s_nm[:, u % 2:u % 2 + 1], ps[:, 0:NMEM], AX_X, ALU.max, negate=True)\
                    .then_inc(sem("x_m"), 1)

            x_max(0)
            for u in range(XH * TT):
                if u + 1 < XH * TT:
                    if u:
                        dve.wait_ge(wk_done[2], uses[("xt", u - 1)][1] + 1)
                    x_max(u + 1)
                wait_read(dve, ("xs", u))
                normalise(None, NMEM, xP, u, sem("x_p"))
                if u % 2 == 0 and u > 5:
                    split_work(("xo", (u - 6) // 2), (u - 6) // 2)
            for k in range(KT - 3, KT):
                split_work(("xo", k), k)
            for n in range(KT):
                residual(n, "xo", AT["xo"] + n, "ff_g")
            invert(NORM["xo"], rstd)

            def hidden(j, u, i):
                ps = taken(j, i, 16)
                leave(STT(xt[:, u % 2, :], ps[:, :], 0.0, rstd[:, :], ALU.max, ALU.mult), j)
                dve.drain()
                TTop(xt[:, u % 2, :], xt[:, u % 2, :], xt[:, u % 2, :], ALU.mult)
                dve.drain()
                split(xt[:, u % 2, :], XB, u)

            with dve.Fori(0, FF1 // D - 1) as i:
                for u in range(KT):
                    hidden(AT["ffn1"] + u, u, i)
                for u in range(KT):
                    j = AT["ffn1"] + KT + u
                    ps = taken(j, i, 16)
                    leave(TTop(tile(h, u), tile(h, u), ps[:, :], ALU.add), j)
                dve.drain()
            for u in range(KT):
                hidden(AT["ffn1"] + 48 + u, u, None)
            for u in range(KT):
                residual(u, "final", AT["ffn1"] + 56 + u)
            invert(NORM["final"], rstd)

            def scale_tile(n, g):
                STT(tile(h, n), tile(h, n), g, rstd[:, :], ALU.mult, ALU.mult)

            if LAST_BLOCK == 1:
                for n in range(KT):
                    scale_tile(n, V("final_g", n))
                    dve.drain().then_inc(sem("result"), 1)
                return
            for n in range(KT):
                scale_tile(n, V("final_g", n))
                dve.drain().then_inc(h_upd, 1)
                if n:
                    sum_square(n - 1, SQN["pre"] + n - 1)
            sum_square(KT - 1, SQN["pre"] + KT - 1)
            nc.vector.memset(vpad[:, :, 0:CONV_K - 1], 0.0)
            nc.vector.memset(rawp[:, :, 0:SK - 1], 0.0)
            invert(NORM["pre"], rstd)

            def pre_low(t):
                dve.wait_ge(hi_done, HI["pre"] + t + 1)
                TTop(tile(XA[1], t), xt[:, t % 2, :], tile(XA[0], t).bitcast(F32), ALU.subtract).then_inc(x_ready, 1)

            for t in range(KT):
                STT(xt[:, t % 2, :], tile(h, t), V("pre_g", t), rstd[:, :], ALU.mult, ALU.mult)
                dve.drain().then_inc(sem("pre_x"), 1)
                if t:
                    pre_low(t - 1)
                    dve.drain()
            pre_low(KT - 1)
            dve.drain()
            ps = taken(AT["dt"])
            leave(TS(acs[0:NSH, :], ps[0:NSH, :], V("dt_b")[0:NSH, :], None, ALU.add), AT["dt"])
            dve.drain()
            STT(xt[0:NSH, 0, :], acs[0:NSH, :], -1.0, acs[0:NSH, :], ALU.mult, ALU.max)
            dve.drain().then_inc(sem("s_abs"), 1)
            log1p(NSH, sem("s_exp"), sem("s_one"))
            STT(xt[0:NSH, 1, :], acs[0:NSH, :], 0.0, xt[0:NSH, 1, :], ALU.max, ALU.add)
            dve.drain()
            TS(acs[0:NSH, :], xt[0:NSH, 1, :], s_nea[0:NSH, :], -1.0, ALU.mult, ALU.mult)
            dve.drain()
            nc.vector.tensor_tensor_scan(acs[0:NSH, :], reset[0:NSH, :], acs[0:NSH, :], 0.0, ALU.mult, ALU.add)
            dve.drain().then_inc(sem("s_acs"), 1)
            def depthwise(part):
                t = part // 2
                v, c = vpad[:, t, :], ssum[:, :]
                if part % 2 == 0:
                    TS(c, v[:, CONV_K - 1:], V("dw_w", t * CONV_K + CONV_K - 1), V("dw_b", t), ALU.mult, ALU.add)
                for k in range(CONV_K - 2, CONV_K // 2, -1) if part % 2 == 0 else range(CONV_K // 2, -1, -1):
                    dve.drain()
                    STT(v[:, 0:S] if k == 0 else c, v[:, k:k + S], V("dw_w", t * CONV_K + k), c, ALU.mult, ALU.add)
                dve.drain()

            for t in range(KT):
                j = AT["glu"] + 2 * t
                dve.wait_ge(bank_free[(j + 1) % 4], (j + 1) // 4 + 1)
                ps = taken(j)
                v = vpad[:, t, CONV_K - 1:]
                leave(STT(v, ps[:, :], V("glu_b", t), sq[:, t % 2, :], ALU.add, ALU.mult), j)
                dve.drain().then_inc(sem("glu_v"), 1)
                if t:
                    depthwise(t - 1)
            depthwise(KT - 1)

            def convolve(g, k):
                ct = [2 * g, 2 * g + 1, 16 + g, 24 + g][k]
                x = xt[:, k % 2, :]
                dve.wait_ge(sem("g_tap"), 4 * g + k + 1)
                for tap in range(1, SK):
                    STT(x, rawp[:, k % 2, tap:tap + S], V("sc_w", ct * SK + tap), x, ALU.mult, ALU.add)
                    if tap < SK - 1:
                        dve.drain()
                dve.drain().then_inc(sem("g_raw"), 1)

            def heads(a):
                return a.rearrange("p c (h v) -> p c h v", h=2)

            def group_tokens(g):
                for q in range(2):
                    ps = wait_full(dve, ("x", g, q))
                    dt = dacs[:, 0, :, 4 * g + 2 * q:4 * g + 2 * q + 2].rearrange("p c (h o) -> p c h o", o=1)
                    if g == 0:
                        wait_read(dve, "dacs")
                    free(TTop(heads(xdt[:, :, q * P:(q + 1) * P]), ps[:, :].rearrange("p (c h v) -> p c h v", c=TT, h=2),
                              dt.broadcast_to([P, TT, 2, 64]), ALU.mult), ("x", g, q))
                ps = wait_full(dve, ("cb", g))
                free(TTop(blocks(cbm), blocks(ps[:, :]),
                          tri.rearrange("p (a b) -> p a b", a=1).broadcast_to([P, TT, P]), ALU.mult), ("cb", g))
                dve.drain()

            def to_end(g, q):
                dve.wait_ge(sem("g_exp"), 3 * (2 * g + q) + 1)
                TTop(heads(xde[:, :, q * P:(q + 1) * P]), heads(xdt[:, 0:3, q * P:(q + 1) * P]),
                     s_dte.rearrange("p (h c o) -> p c h o", h=2, o=1)[:, 0:3].broadcast_to([P, 3, 2, 64]), ALU.mult)
                dve.drain().then_inc(sem("g_xde"), 1)

            def products(g, q):
                n = 2 * g + q
                dve.wait_ge(sem("g_exp"), 3 * n + 2)
                TTop(Mm[:, :, :], Mm[:, :, :], cbm.rearrange("p (a b) -> p a b", a=1).broadcast_to([P, 2, S]), ALU.mult)
                ps = wait_full(dve, ("st", g, q))
                dve.wait_ge(sem("g_exp"), 3 * n + 3)
                copy(Ss[:, 0, :], ps[:, 0:P])
                for c in (1, 2):
                    dve.drain()
                    dl = s_dl.rearrange("p (h c) -> p h c", h=2)[:, :, c:c + 1].broadcast_to([P, 2, 64])
                    TTop(Ss[:, c, :].rearrange("p (h v) -> p h v", h=2),
                         Ss[:, c - 1, :].rearrange("p (h v) -> p h v", h=2), dl, ALU.mult)
                    dve.drain()
                    ins = TTop(Ss[:, c, :], Ss[:, c, :], ps[:, c * P:(c + 1) * P], ALU.add)
                free(ins, ("st", g, q))
                dve.drain().then_inc(sem("g_cp"), 1)

            def pair_out(g, q):
                ps = wait_full(dve, ("y", g, q))
                y = ssm_y[:, :]
                free(STT(y, xfs[g % 2][q], V("dskip", 2 * g + q), ps[:, :], ALU.mult, ALU.add), ("y", g, q))
                dve.wait_ge(sem("g_z"), 2 * g + q + 1)
                dve.drain()
                z = zs2[:, g % 2, q, :]
                TTop(z, y, z, ALU.mult)
                dve.drain().then_inc(sem("g_y"), 1)

            def group_out(g):
                wait_read(dve, ("gn", g))
                nc.vector.reciprocal(std[:, :], std[:, :])
                dve.drain()
                for q in range(2):
                    z = zs2[:, g % 2, q, :]
                    STT(z, z, V("ssm_g", 2 * g + q), std[:, :], ALU.mult, ALU.mult)
                dve.drain()
                if g == 4:
                    dve.wait_ge(strip_done, AT["out0", KT - 1] + 1)
                for q in range(2):
                    copy(tile(XB[0], 2 * (g % 4) + q), zs2[:, g % 2, q, :])
                dve.drain()
                for q in range(2):
                    k = 2 * (g % 4) + q
                    TTop(tile(XB[1], k), zs2[:, g % 2, q, :], tile(XB[0], k).bitcast(F32), ALU.subtract)\
                        .then_inc(x_ready, 1)

            ssm_y = std
            for g in range(-1, GROUPS):
                for k in range(6):
                    if g >= 0:
                        if k == 0:
                            if g:
                                pair_out(g - 1, 1)
                            group_tokens(g)
                            to_end(g, 0)
                        elif k == 1 and g:
                            group_out(g - 1)
                        elif k == 2:
                            products(g, 0)
                        elif k == 3:
                            pair_out(g, 0)
                        elif k == 4:
                            to_end(g, 1)
                        elif k == 5:
                            products(g, 1)
                    if g + 1 < GROUPS and k < 4:
                        convolve(g + 1, k)
                    if 0 <= g < 4 and k >= 4:
                        depthwise(8 + 2 * g + k - 4)
                if g == 3:
                    dve.drain().then_inc(sem("dw_done"), 1)
            pair_out(GROUPS - 1, 1)
            group_out(GROUPS - 1)
            dve.wait_ge(sem("cv_in"), 16)
            copy(ssum[:, :], tile(cv, 0))
            for n in range(1, KT):
                dve.drain()
                TTop(ssum[:, :], ssum[:, :], tile(cv, n), ALU.add)
            dve.drain().then_inc(ssum_rdy, 1)
            dve.wait_ge(sem("gates_s"), 1)

            def out1(n):
                j = AT["ssmout1"] + n
                ps = taken(j)
                leave(TTop(tile(acc, n), tile(acc, n), ps[:, :], ALU.add), j)
                dve.drain()
                TTop(tile(acc, n), tile(acc, n), gates[n], ALU.mult)
                dve.drain().then_inc(sem("acc_g"), 1)

            for n in range(3):
                out1(n)
            wait_read(dve, ("norm", NORM["conv"]))
            for n in range(KT):
                TTop(tile(cv, n), tile(cv, n), mu, ALU.subtract)
                dve.drain().then_inc(h_upd, 1)
                if n:
                    sum_square(n - 1, SQN["conv"] + n - 1)
                if n in (3, 6):
                    out1(n // 3 + 2)
            sum_square(KT - 1, SQN["conv"] + KT - 1)
            dve.drain().then_inc(ssum_rdy, 1)
            out1(5)
            wait_read(dve, ("norm", NORM["conv"] + 1))
            nc.vector.reciprocal(rs2, std[:, :])
            dve.drain()
            out1(6)
            for n in range(KT):
                STT(tile(cv, n), tile(cv, n), V("ln_g", n), rs2, ALU.mult, ALU.mult)
                dve.drain().then_inc(sem("ln_x"), 1)
            out1(7)
            for n in range(KT):
                dve.wait_ge(hi_done, HI["conv"] + n + 1)
                TTop(tile(XB[1], n), tile(cv, n), tile(XB[0], n).bitcast(F32), ALU.subtract).then_inc(x_ready, 1)
            dve.wait_ge(sem("gates_s"), 2)

            def mix_low(n):
                dve.wait_ge(hi_done, HI["mix"] + n + 1)
                TTop(tile(XA[1], n), tile(acc, n), tile(XA[0], n).bitcast(F32), ALU.subtract).then_inc(x_ready, 1)

            for n in range(KT):
                j = AT["pw"] + n
                ps = taken(j)
                leave(STT(tile(cv, n), ps[:, :], V("pw_b", n), gates[n], ALU.add, ALU.mult), j)
                dve.drain()
                TTop(tile(acc, n), tile(acc, n), tile(cv, n), ALU.add)
                dve.drain().then_inc(sem("mixed"), 1)
                if n:
                    mix_low(n - 1)
            mix_low(KT - 1)
            for n in range(KT):
                dve.drain().then_inc(h_upd, 1)
                if n:
                    sum_square(n - 1, SQN["post"] + n - 1)
            sum_square(KT - 1, SQN["post"] + KT - 1)
            invert(NORM["post"], rstd)
            for n in range(KT):
                STT(xt[:, n % 2, :], tile(cv, n), V("post_g", n), rstd[:, :], ALU.mult, ALU.mult)
                dve.drain()
                TTop(tile(h, n), tile(h, n), xt[:, n % 2, :], ALU.add)
                dve.drain().then_inc(h_upd, 1)
                if n:
                    low_tile(tile(h, n - 1), V("ffn_g", n - 1), n - 1, "ffn")
            low_tile(tile(h, KT - 1), V("ffn_g", KT - 1), KT - 1, "ffn")
            invert(NORM["ffn"], rstd)
            k = 0
            for c, nt in enumerate(CHUNK2):
                with dve.Fori(0, nt // 2) as i:
                    for u in range(0, 4, 2):
                        j, x = AT[f"gu{c}"] + u, xt[:, u // 2, :]
                        ps = taken(j, i)
                        leave(TTop(x, ps[:, :], rstd[:, :], ALU.mult), j)
                        dve.drain().then_inc(sem("ff_g"), 1)
                        dve.wait_ge(sem("ff_s"), i * 2 + (k + u // 2 + 1))
                        TTop(x, x, sq[:, u // 2, :], ALU.mult)
                        dve.drain()
                        TTop(x, x, rstd[:, :], ALU.mult)
                        dve.drain()
                        ps = taken(j + 1, i)
                        leave(TTop(x, x, ps[:, :], ALU.mult), j + 1)
                        dve.drain()
                        split(x, XB, i * 2 + u // 2)
                        dve.drain()
                k += nt
                for n in range(KT):
                    j = AT[f"down{c}"] + n
                    ps = taken(j)
                    if c == 0:
                        leave(copy(tile(acc, n), ps[:, :]), j)
                        continue
                    leave(TTop(tile(acc, n), tile(acc, n), ps[:, :], ALU.add), j)
                    if c == 2:
                        dve.drain().then_inc(h_upd, 1)
                        sum_square(n, SQN["ffpost"] + n)
                dve.drain()
            invert(NORM["ffpost"], rstd)
            for n in range(KT):
                STT(xt[:, n % 2, :], tile(acc, n), V("ffpost_g", n), rstd[:, :], ALU.mult, ALU.mult)
                dve.drain()
                TTop(tile(h, n), tile(h, n), xt[:, n % 2, :], ALU.add)
                dve.drain().then_inc(sem("result"), 1)


def by_features(a):
    t, f = a.shape
    return np.ascontiguousarray(a.T.reshape(f // P, P, t).transpose(1, 0, 2).reshape(P, -1))


def strip_of(w, n, k0=0, kn=KT):
    part = w[k0 * P:(k0 + kn) * P, n * P:(n + 1) * P]
    if part.shape[1] < P:
        part = np.pad(part, ((0, 0), (0, P - part.shape[1])))
    return part.reshape(kn, P, P).transpose(1, 0, 2).reshape(P, kn * P)


def columns(v):
    v = np.asarray(v).reshape(-1)
    n = -(-v.size // P)
    return np.pad(v, (0, n * P - v.size)).reshape(n, P).T


def lay_out(x):
    g = {k: np.asarray(v) for k, v in x.items()}
    w_in, w_in2, wkv, gu = g["w_in"][0], g["w_in_2"][0], g["w_xkv"][0], g["w_gate_up_2"][0]
    fox, hg = 512, 512
    o = np.cumsum([0, fox, fox, fox, FH, hg, hg, hg, hg])
    part = {n: w_in[:, o[i]:o[i + 1]] for i, n in enumerate(["fq", "fk", "fv", "ff", "gq", "gf", "gi", "gg"])}
    o = np.cumsum([0, D, D, 2 * D, 2 * D, D, D, NSH, D, D])
    part |= {n: w_in2[:, o[i]:o[i + 1]] for i, n in
             enumerate(["val", "glu", "z", "xs", "bm", "cm", "dt", "gconv", "gssm"])}
    part |= {"memk": wkv[:, :D], "memv": wkv[:, D:], "w_out": g["w_out"][0], "xq": g["w_xq"][0], "xo": g["w_xo"][0],
             "w1": g["w1"][0], "w2": g["w2"][0], "ssmout": g["ssm_out_w_2"][0], "pw": g["conv_pw_w_2"][0],
             "w_out2": g["w_out_2"][0], "gate": gu[:, :FF2], "up": gu[:, FF2:], "down": g["w_down_2"][0]}
    full = np.stack([strip_of(part[s[0]], s[1], KT * (s[2] if len(s) > 2 else 0)) for s in STREAM[:NS_FULL]])
    six = np.stack([strip_of(part[s[0]], s[1], KT * s[2], CHUNK2[2]) for s in STREAM[NS_FULL:]])
    lb = g["hgrn_lb_logits"]
    taps = lambda w: w.reshape(w.shape[0], -1, P).transpose(2, 1, 0).reshape(P, -1)
    cols = {"mix_g": g["norm_mix_g"], "mem_g": g["norm_mem_g"], "x_g": g["norm_x_g"], "ff_g": g["norm_ff_g"],
            "final_g": g["final_norm_g"], "pre_g": g["mix_pre_g_2"], "ffn_g": g["ffn_pre_g_2"],
            "post_g": g["mix_post_g_2"], "ffpost_g": g["ffn_post_g_2"], "hgrn_g": g["hgrn_norm_g"], "lb0": lb[0],
            "lb1": lb[1], "foxb": g["fox_f_bias"], "gate_b": g["gate_b_2"], "glu_b": g["glu_b_2"],
            "dw_b": g["conv_dw_b_2"], "ln_g": g["conv_ln_g_2"], "ln_b": g["conv_ln_b_2"], "pw_b": g["conv_pw_b_2"],
            "sc_b": g["ssm_conv_b_2"], "dt_b": g["dt_bias_2"], "a_log": g["a_log_2"],
            "dskip": np.repeat(g["d_skip_2"][0], 64), "ssm_g": g["ssm_norm_g_2"]}
    cols = {k: columns(v) for k, v in cols.items()}
    cols["dw_w"], cols["sc_w"] = taps(g["conv_dw_w_2"][0]), taps(g["ssm_conv_w_2"][0])
    return {"xT": by_features(g["x"][0]), "memT": by_features(g["mem"][0]), "weights": full, "weights6": six,
            "vectors": np.ascontiguousarray(np.concatenate([cols[n] for n, _ in VEC], 1)), "consts": constants()}


def kernel(**inputs):
    import concourse.bacc as _bacc
    from concourse.bass_utils import run_bass_kernel_spmd as _run

    nc = _bacc.Bacc("TRN2", target_bir_lowering=False, num_devices=1)
    arrays, args = {}, []
    for name, a in lay_out(inputs).items():
        arrays[f"in_{name}"] = a
        args.append(nc.dram_tensor(f"in_{name}", a.shape, mybir.dt.from_np(a.dtype), kind="ExternalInput").ap())
    args.append(nc.dram_tensor("scratch", (NSH, S), F32, kind="Internal").ap())
    args.append(nc.dram_tensor("spill", (P, KT, S), F32, kind="Internal").ap())
    args.append(nc.dram_tensor("out_0", (P, KT * S), F32, kind="ExternalOutput").ap())
    block_kernel(nc, *args)
    r = _run(nc, [arrays], core_ids=[0])
    out = np.asarray(r.results[0]["out_0"]).reshape(P, KT, S).transpose(2, 1, 0).reshape(1, S, D)
    return np.ascontiguousarray(out)
```

```python
from contextlib import ExitStack

import concourse.bass as bass
from concourse import mybir
import numpy as np

P = 128
S = 512
D = 1024
KT = D // P
TT = S // P
NMEM = 256
MT = NMEM // P
EPS = 1e-6
LN_EPS = 1e-5
NEG = -1.0e30

HG = 4
LEVELS = 8
FH = 8
FD = 64
XH = 4
XD = 256
FF1 = 4096
CONV_K = 31
SK = 4
GROUPS = 8
HPG = 4
NSH = GROUPS * HPG
FF2 = 2816
F2T = FF2 // P
CHUNK2 = [8, 8, 6]
STRIP = KT * P
OUT0_AT = {2: [0], 3: [1, 2], 4: [3, 4], 5: [5, 6, 7]}

F32 = mybir.dt.float32
F32R = mybir.dt.float32r
BF16 = mybir.dt.bfloat16
I32 = mybir.dt.int32
ALU = mybir.AluOpType
ACT = mybir.ActivationFunctionType
AX_X = mybir.AxisListType.X



def stream():
    at, out = {}, []

    def add(name, items):
        at[name] = len(out)
        out.extend(items)

    add("hgrn", [("gf", t) for t in range(HG)] + [("gq", t) for t in range(HG)] + [("gi", t) for t in range(HG)])
    fox = [("fv", t) for t in range(4)] + [(n, t) for t in range(4) for n in ("fq", "fk")]
    add(("fox", 0), [("ff", 0)])
    for t in range(HG):
        add(("gg", t), [("gg", t)])
        for n in range(3 * t, 3 * t + 3):
            add(("fox", n + 1), [fox[n]])
    add("mem", [("memk", t) for t in range(KT)] + [("memv", t) for t in range(KT)])
    add("w_out", [("w_out", t) for t in range(KT)])
    add("xq", [("xq", t) for t in range(KT)])
    add("xo", [("xo", t) for t in range(KT)])
    add("ffn1", [x for c in range(FF1 // D) for x in
                 [("w1", KT * c + t) for t in range(KT)] + [("w2", t, c) for t in range(KT)]])
    add("dt", [("dt", 0)])
    add("glu", [x for t in range(KT) for x in (("val", t), ("glu", t))])
    for g in range(GROUPS):
        for k, item in enumerate(group_strips(g)):
            add(("ssd", g, k), [item])
            for t in OUT0_AT.get(k, []) if g == 5 else []:
                add(("out0", t), [("ssmout", t, 0)])
    add("gssm", [("gssm", t) for t in range(KT)])
    add("ssmout1", [("ssmout", t, 1) for t in range(KT)])
    add("gconv", [("gconv", t) for t in range(KT)])
    add("pw", [("pw", t) for t in range(KT)])
    add("w_out2", [("w_out2", t) for t in range(KT)])
    f = 0
    for c, n in enumerate(CHUNK2):
        add(f"gu{c}", [x for t in range(n) for x in (("gate", f + t), ("up", f + t))])
        add(f"down{c}", [("down", t, c) for t in range(KT)])
        f += n
    return at, out


def group_strips(g):
    return [("xs", 2 * g), ("xs", 2 * g + 1), ("bm", g), ("cm", g), ("z", 2 * g), ("z", 2 * g + 1)]


AT, STREAM = stream()
NS = len(STREAM)
NS_FULL = AT["down2"]

VEC = [("mix_g", 8), ("mem_g", 8), ("x_g", 8), ("ff_g", 8), ("final_g", 8), ("pre_g", 8), ("ffn_g", 8),
       ("post_g", 8), ("ffpost_g", 8), ("hgrn_g", 1), ("lb0", 4), ("lb1", 4), ("foxb", 1), ("gate_b", 16),
       ("glu_b", 16), ("dw_w", 8 * CONV_K), ("dw_b", 8), ("ln_g", 8), ("ln_b", 8), ("pw_b", 8),
       ("sc_w", 32 * SK), ("sc_b", 32), ("dt_b", 1), ("a_log", 1), ("dskip", 16), ("ssm_g", 16)]
VOFF, _n = {}, 0
for _name, _c in VEC:
    VOFF[_name] = _n
    _n += _c
NVEC = _n

CONST = [("ones", P), ("ident", P), ("tri", P), ("neg", P), ("lev", LEVELS * P), ("reset", S), ("eps", 2)]
COFF, _n = {}, 0
for _name, _c in CONST:
    COFF[_name] = _n
    _n += _c
NCONST = _n


def constants():
    c = np.zeros((P, NCONST), np.float32)
    r = np.arange(P)
    c[:, COFF["ones"]:COFF["ones"] + P] = 1.0
    c[:, COFF["ident"]:COFF["ident"] + P] = np.eye(P)
    c[:, COFF["tri"]:COFF["tri"] + P] = r[None, :] >= r[:, None]
    c[:, COFF["neg"]:COFF["neg"] + P] = np.where(r[None, :] > r[:, None], NEG, 0.0)
    for level in range(LEVELS):
        if level == 0:
            m = r[:, None] == r[None, :]
        else:
            h = 1 << (level - 1)
            m = (r[:, None] // (2 * h) == r[None, :] // (2 * h)) & (r[:, None] % (2 * h) < h) & (r[None, :] % (2 * h) >= h)
        c[:, COFF["lev"] + level * P:COFF["lev"] + (level + 1) * P] = m
    c[:, COFF["eps"]:COFF["eps"] + 2] = [[EPS, LN_EPS]]
    c[:, COFF["reset"]:COFF["reset"] + S] = (np.arange(S) % P != 0)[None, :]
    return c


ARENA = 15366


def val(c, i, per):
    return c if i is None else i * per + c


FILL = {(t, l): 1 + 3 * t + n for t in range(HG) for n, l in enumerate((4, "hs", "ho"))}


def block_kernel(nc, xT, memT, weights, weights6, vectors, consts, scratch, spill, outT):
    with ExitStack() as ctx:
        def sb(name, shape, dt=F32):
            return ctx.enter_context(nc.sbuf_tensor(name, shape, dt))

        sems = {}

        def sem(name):
            if name not in sems:
                sems[name] = ctx.enter_context(nc.semaphore(name))
            return sems[name]

        h = sb("h", [P, KT * S])
        XA = (sb("XAh", [P, KT * S], F32R), sb("XAl", [P, KT * S], F32R))
        NRAW = 2
        raw = [sb(f"raw{s}", [P, STRIP]) for s in range(NRAW)]
        wh = [sb(f"wh{s}", [P, STRIP], F32R) for s in range(4)]
        wl = [sb(f"wl{s}", [P, STRIP], F32R) for s in range(4)]
        vec = sb("vec", [P, NVEC])
        cst = sb("cst", [P, NCONST])
        ident_bf = sb("ident_bf", [P, P], BF16)
        neg_bf = sb("neg_bf", [P, P], BF16)
        rstd = sb("rstd", [P, S])
        ssum = sb("ssum", [P, S])
        std = sb("std", [P, S])
        sq = sb("sq", [P, 2, S])
        xt = sb("xt", [P, 2, S])
        small = sb("small", [P, 256])
        arena = sb("arena", [P, ARENA])
        with nc.sbuf_tensor("XBh", [P, KT * S], F32R) as xbh, nc.sbuf_tensor("XBl", [P, KT * S], F32R) as xbl:
            XB = (xbh, xbl)
        early = sb("early", [P, 2 * KT * S])

        def carve(base, at, *shape):
            n = int(np.prod(shape))
            a = base[:, at[0]:at[0] + n]
            at[0] += n
            assert at[0] <= (ARENA if base is arena else 2 * KT * S), at[0]
            if len(shape) == 2:
                return a.rearrange("p (a b) -> p a b", a=shape[0])
            if len(shape) == 3:
                return a.rearrange("p (a b c) -> p a b c", a=shape[0], b=shape[1])
            return a

        bank = [ctx.enter_context(nc.psum_tensor(f"bank{s}", [P, S], F32)) for s in range(4)]
        work = [ctx.enter_context(nc.psum_tensor(f"work{s}", [P, S], F32)) for s in range(4)]

        def V(name, t=0, n=1):
            return vec[:, VOFF[name] + t:VOFF[name] + t + n]

        def C(name, t=0):
            return cst[:, COFF[name] + t * P:COFF[name] + (t + 1) * P]

        ones, ident, tri = C("ones"), C("ident"), C("tri")
        reset = cst[:, COFF["reset"]:COFF["reset"] + S]

        def tile(a, n, w=S):
            if isinstance(n, int):
                return a[:, n * S:n * S + w]
            return a[:, bass.ds(n * S, w)]

        def blocks(a):
            return a.rearrange("p (a b) -> p a b", b=P)

        at = [0]
        fq, fk, fv = carve(arena, at, 4 * S), carve(arena, at, 4 * S), carve(arena, at, TT, 4 * P)
        r1 = at[0]
        hkk, hgg, hb = carve(arena, at, HG * S), carve(arena, at, HG * S), carve(arena, at, HG * S)
        r4 = at[0]
        mem_in = carve(arena, at, KT * NMEM)
        memrstd, fneg = carve(arena, at, NMEM), carve(arena, at, S)
        at = [0]
        hqq, hgi = carve(early, at, HG * S), carve(early, at, TT, HG * P)
        hE, hZ, hattn = carve(early, at, 2, S), carve(early, at, 3, S), carve(early, at, S)
        hkt, hS = carve(early, at, 3, P), carve(early, at, 3, P)
        at = [r1]
        fPT = carve(arena, at, 2, S)
        at = [r1 + HG * S]
        memk, memv = carve(arena, at, KT * NMEM), carve(arena, at, MT, D)
        at = [r4]
        fS = carve(arena, at, 4, S)
        at = [r1 + 2 * S]
        nfb = carve(arena, at, 2, S)
        at = [0]
        xqf, xP = carve(arena, at, KT * S), carve(arena, at, 4, NMEM)
        at = [r1]
        xPT = carve(arena, at, 2, MT, S)
        at = [0]
        VW = S + CONV_K - 1
        vpad = carve(arena, at, KT, VW)
        r5 = at[0]
        rawp = carve(arena, at, 2, S + SK - 1)
        xf = carve(arena, at, 4, S)
        xdt, xde, btok = carve(arena, at, TT, 2 * P), carve(arena, at, 3, 2 * P), carve(arena, at, 3, P)
        zs2 = carve(arena, at, 2, 2, S)
        cbm, Ab, Mm = carve(arena, at, S), carve(arena, at, 2, S), carve(arena, at, 2, S)
        Ss, acs = carve(arena, at, 3, P), carve(arena, at, S)
        staged = reset
        lev = cst[:, COFF["lev"]:COFF["lev"] + 2 * S]
        xfs = [[lev[:, 0:S], lev[:, S:2 * S], acs, rstd[:, :]], [xf[:, n, :] for n in range(4)]]
        gates = [lev[:, 0:S], lev[:, S:2 * S], acs, rstd[:, :], zs2[:, 0, 0, :], zs2[:, 0, 1, :],
                 xt[:, 0, :], xt[:, 1, :]]
        dacs = carve(arena, at, 2, TT, NSH)
        at = [r5]
        acc = carve(arena, at, KT * S)
        mu, rs2 = carve(arena, at, S), carve(arena, at, S)

        def cv(t):
            return vpad[:, t, 0:S]

        s_lb, s_oml, s_nea = small[:, 0:4], small[:, 4:8], small[:, 8:9]
        s_nm, s_rs, s_ri, s_eb = small[:, 16:20], small[:, 20:24], small[:, 28:32], small[:, 24:28]
        s_tmp = small[:, 32:64]
        s_dte, s_dl = small[:, 64:72], small[:, 72:80]

        raw_ready = [sem(f"raw_ready{s}") for s in range(NRAW)]
        w_hi, w_lo, strip_done = sem("w_hi"), sem("w_lo"), sem("strip_done")
        bank_free = [sem(f"bank_free{s}") for s in range(4)]
        wk_done = [sem(f"wk_done{s}") for s in range(4)]
        wk_free = [sem(f"wk_free{s}") for s in range(4)]
        x_ready, h_upd, sq_done, ssum_rdy = sem("x_ready"), sem("h_upd"), sem("sq_done"), sem("ssum_rdy")
        loaded, const_rdy, hi_done = sem("loaded"), sem("const_rdy"), sem("hi_done")
        HI = {n: KT * k for k, n in enumerate(["in", "mem", "w_out", "xo", "pre", "conv", "mix", "ffn"])}

        XN, SQN, NORM = {}, {}, {}
        nx = nsq = nn = 0
        for name, tiles, sqs, norms in [
            ("in", KT, KT, 1), ("mem", KT, KT, 1), ("rec", 4, 0, 0), ("fox", 4, 0, 0), ("w_out", KT, KT, 1),
            ("xattn", KT, 0, 0), ("xo", KT, KT, 1), ("hid", 4 * KT, 0, 0), ("final", 0, KT, 1),
            ("pre", KT, KT, 1), ("y0", KT, 0, 0), ("y1", KT, 0, 0), ("conv", KT, KT, 2),
            ("mix", KT, 0, 0), ("post", 0, KT, 1), ("ffn", KT, KT, 1),
            ("g0", KT, 0, 0), ("g1", KT, 0, 0), ("g2", CHUNK2[2], 0, 0), ("ffpost", 0, KT, 1),
        ]:
            XN[name], SQN[name], NORM[name] = nx, nsq, nn
            nx, nsq, nn = nx + tiles, nsq + sqs, nn + norms

        uses, used = {}, [0] * 4

        def wait_full(eng, key):
            b, n = uses[key]
            eng.wait_ge(wk_done[b], n + 1)
            return work[b]

        def free(ins, key):
            ins.then_inc(wk_free[uses[key][0]], 1)

        def wait_read(eng, key):
            b, n = uses[key]
            eng.wait_ge(wk_free[b], n + 1)

        block = ctx.enter_context(nc.Block())

        @block.tensor
        def _(pe):
            mm, turn = nc.tensor.matmul, nc.tensor.transpose

            def strip(j, X, kts=range(KT), xn=None, i=None, per=4, w=S):
                s = j % 4
                pe.wait_ge(w_lo, val(j + 1, i, per))
                if j >= 4 or i is not None:
                    pe.wait_ge(bank_free[s], val(j // 4, i, per // 4))
                for n, k in enumerate(kts):
                    if xn is not None:
                        pe.wait_ge(x_ready, val(xn[n] + 1, i, KT))
                    hi, lo = wh[s][:, k * P:(k + 1) * P], wl[s][:, k * P:(k + 1) * P]
                    mm(bank[s][:, 0:w], hi, tile(X[0], k, w), start=(n == 0), stop=False)
                    mm(bank[s][:, 0:w], hi, tile(X[1], k, w), start=False, stop=False)
                    last = mm(bank[s][:, 0:w], lo, tile(X[0], k, w), start=False, stop=(n == len(kts) - 1))
                last.then_inc(strip_done, 1)

            def tiles_from(name, n=KT):
                return [XN[name] + k for k in range(n)]

            def work_bank(key, b):
                uses[key] = (b, used[b])
                if used[b]:
                    pe.wait_ge(wk_free[b], used[b])
                used[b] += 1
                return work[b]

            def norm(k, b=3):
                w = work_bank(("norm", k), b)
                pe.wait_ge(ssum_rdy, k + 1)
                mm(w[:, :], ones, ssum[:, :], start=True, stop=True).then_inc(wk_done[b], 1)

            def turn_tile(key, b, src, n=TT):
                w = work_bank(key, b)
                for c in range(n):
                    last = turn(w[:, c * P:(c + 1) * P], src[:, c * P:(c + 1) * P], ident)
                last.then_inc(wk_done[b], 1)

            def turn_values(t):
                pe.wait_ge(sem("hg_raw"), 2 * HG + t + 1)
                turn_tile(("gi", t), t % 2, xt[:, t % 2, :])

            for n in range(3 * HG):
                strip(AT["hgrn"] + n, XA, xn=tiles_from("in") if n == 0 else None)
                if n == 0:
                    pe.wait_ge(const_rdy, 1)
                    norm(NORM["in"])
                if n >= 9:
                    turn_values(n - 9)
            strip(AT["fox", 0], XA)
            turn_values(HG - 1)

            def fox_strip(n):
                strip(AT["fox", n], XA)
                if 3 <= n <= 6:
                    pe.wait_ge(sem("fv_raw"), n - 2)
                    turn_tile(("fv", n - 3), 2, xt[:, (n - 3) % 2, :])

            for t in range(HG):
                for l in range(LEVELS):
                    if l == 2:
                        strip(AT["gg", t], XA)
                    if (t, l) in FILL:
                        fox_strip(FILL[t, l])
                    w = work_bank(("level", t, l), l % 2)
                    if l == 0:
                        if t == 0:
                            pe.wait_ge(sem("hg_scan"), 1)
                        a, b = hkk[:, t * S:(t + 1) * S], hqq[:, t * S:(t + 1) * S]
                    else:
                        pe.wait_ge(sem("h_z"), 7 * t + l)
                        a = b = hZ[:, l % 2, :]
                    for c in range(TT):
                        last = mm(w[:, c * P:(c + 1) * P], a[:, c * P:(c + 1) * P], b[:, c * P:(c + 1) * P],
                                  start=True, stop=True)
                    last.then_inc(wk_done[l % 2], 1)
                pe.wait_ge(sem("h_qk"), t + 1)
                turn_tile(("kt", t), 2, hZ[:, 0, :], 3)
                fox_strip(FILL[t, "hs"])
                w = work_bank(("hs", t), 3)
                wait_read(pe, ("kt", t))
                for c in range(3):
                    last = mm(w[:, c * P:(c + 1) * P], hkt[:, c, :], hgi[:, c, t * P:(t + 1) * P],
                              start=True, stop=True)
                last.then_inc(wk_done[3], 1)
                fox_strip(FILL[t, "ho"])
                w = work_bank(("ho", t), 2)
                pe.wait_ge(sem("h_s"), t + 1)
                for c in range(TT):
                    last = mm(w[:, c * P:(c + 1) * P], hgi[:, c, t * P:(t + 1) * P], hattn[:, c * P:(c + 1) * P],
                              start=True, stop=(c == 0))
                    if c:
                        last = mm(w[:, c * P:(c + 1) * P], hS[:, c - 1, :], hZ[:, 2, c * P:(c + 1) * P],
                                  start=False, stop=True)
                last.then_inc(wk_done[2], 1)
                w = work_bank(("hn", t), 3)
                wait_read(pe, ("ho", t))
                mm(w[:, :], ones, sq[:, t % 2, :], start=True, stop=True).then_inc(wk_done[3], 1)

            def nf(hd):
                w = work_bank(("nf", hd), 2)
                if hd == 0:
                    pe.wait_ge(sem("f_neg"), 1)
                mm(w[:, :], ident[0:FH, hd:hd + 1].broadcast_to([FH, P]), fneg[0:FH, :], start=True,
                   stop=True).then_inc(wk_done[2], 1)

            def fox_scores(u):
                hd, i = u // TT, u % TT
                w = work_bank(("fs", u), u % 2)
                po, ft = FD * (hd % 2), hd // 2
                mm(w[:, 0:(i + 1) * P], fq[po:po + FD, ft * S + i * P:ft * S + (i + 1) * P],
                   fk[po:po + FD, ft * S:ft * S + (i + 1) * P], start=True, stop=False)
                mm(w[:, i * P:(i + 1) * P], ident_bf[:, :], neg_bf[:, :], start=False, stop=True)\
                    .then_inc(wk_done[u % 2], 1)

            def fox_out(u):
                hd, i = u // TT, u % TT
                if u % 8 == 0:
                    work_bank(("fo", u // 8), 3)
                po = FD * (hd % 2)
                wait_read(pe, ("ft", u))
                for c in range(i + 1):
                    last = mm(work[3][po:po + FD, i * P:(i + 1) * P], fv[:, c, hd * FD:(hd + 1) * FD],
                              fPT[:, u % 2, c * P:(c + 1) * P], start=(c == 0), stop=(c == i))
                if u % 8 == 7:
                    last.then_inc(wk_done[3], 1)

            def mem_turn(t):
                pe.wait_ge(sem("mv_raw"), t + 1)
                turn_tile(("mv", t), 2, xt[:, t % 2, :], MT)

            nf(0)
            fox_scores(0)
            fox_scores(1)
            strip(AT["mem"], XA, xn=tiles_from("mem"), w=NMEM)
            norm(NORM["mem"])
            for u in range(FH * TT):
                if u % 2 == 0:
                    n = u // 2
                    if n:
                        strip(AT["mem"] + n, XA, w=NMEM)
                    if n > KT:
                        mem_turn(n - KT - 1)
                if u + 2 < FH * TT:
                    if (u + 2) % TT == 0:
                        nf((u + 2) // TT)
                    fox_scores(u + 2)
                pe.wait_ge(sem("f_p"), u + 1)
                turn_tile(("ft", u), 2, fS[:, u % 4, :], u % TT + 1)
                if u:
                    fox_out(u - 1)
            mem_turn(KT - 1)
            fox_out(FH * TT - 1)

            for n in range(KT):
                xn = [XN["rec"] + k for k in range(4)] + [XN["fox"] + k for k in range(4)]
                strip(AT["w_out"] + n, XB, kts=[4, 5, 6, 7, 0, 1, 2, 3], xn=None if n else xn)
            for n in range(KT):
                strip(AT["xq"] + n, XA, xn=tiles_from("w_out") if n == 0 else None)
                if n == 0:
                    norm(NORM["w_out"])

            def x_scores(u):
                a, i = u // TT, u % TT
                w = work_bank(("xs", u), u % 2)
                if u == 0:
                    pe.wait_ge(sem("xq_rdy"), 1)
                for c in range(2):
                    k = 2 * a + c
                    last = mm(w[:, 0:NMEM], xqf[:, k * S + i * P:k * S + (i + 1) * P],
                              memk[:, k * NMEM:(k + 1) * NMEM], start=(c == 0), stop=(c == 1))
                last.then_inc(wk_done[u % 2], 1)

            def x_out(k):
                a = k // 2
                wait_read(pe, ("xt", TT * a + TT - 1))
                w = work_bank(("xo", k), 3)
                for c in range(MT):
                    last = mm(w[:, :], memv[:, c, k * P:(k + 1) * P], xPT[:, a % 2, c, :],
                              start=(c == 0), stop=(c == MT - 1))
                last.then_inc(wk_done[3], 1)

            x_scores(0)
            x_scores(1)
            for u in range(XH * TT):
                if u + 2 < XH * TT:
                    x_scores(u + 2)
                pe.wait_ge(sem("x_p"), u + 1)
                turn_tile(("xt", u), 2, xP[:, u % 4, :], MT)
                if u % 2 and u > TT:
                    x_out((u - 5) // 2)
            x_out(KT - 2)
            x_out(KT - 1)
            for n in range(KT):
                strip(AT["xo"] + n, XB, xn=tiles_from("xattn") if n == 0 else None)
            for u in range(KT):
                strip(AT["ffn1"] + u, XA, xn=tiles_from("xo") if u == 0 else None)
                if u == 0:
                    norm(NORM["xo"])
            for u in range(KT):
                strip(AT["ffn1"] + KT + u, XB, xn=tiles_from("hid") if u == 0 else None)
            with pe.Fori(0, FF1 // D - 1) as i:
                for u in range(KT):
                    strip(AT["ffn1"] + 16 + u, XA, i=i, per=16)
                for u in range(KT):
                    strip(AT["ffn1"] + 16 + KT + u, XB, i=i, per=16,
                          xn=[x + KT for x in tiles_from("hid")] if u == 0 else None)
            norm(NORM["final"])

            norm(NORM["pre"])
            strip(AT["dt"], XA, xn=tiles_from("pre"))
            for n in range(2 * KT):
                strip(AT["glu"] + n, XA)
            w = work_bank("dacs", 2)
            pe.wait_ge(sem("s_acs"), 1)
            for c in range(TT):
                turn(w[:, c * NSH:(c + 1) * NSH], xt[0:NSH, 1, c * P:(c + 1) * P], ident[0:NSH, 0:NSH])
                last = turn(w[:, (TT + c) * NSH:(TT + c + 1) * NSH], acs[0:NSH, c * P:(c + 1) * P],
                            ident[0:NSH, 0:NSH])
            last.then_inc(wk_done[2], 1)

            def group_turns(g):
                x = xfs[g % 2]
                for q in range(2):
                    pe.wait_ge(sem("g_xf"), 4 * g + q + 1)
                    turn_tile(("x", g, q), q, x[q])
                pe.wait_ge(sem("g_xf"), 4 * g + 4)
                turn_tile(("b", g), 2, x[2], 3)
                w = work_bank(("cb", g), 3)
                for c in range(TT):
                    last = mm(w[:, c * P:(c + 1) * P], x[2][:, c * P:(c + 1) * P], x[3][:, c * P:(c + 1) * P],
                              start=True, stop=True)
                last.then_inc(wk_done[3], 1)

            def pair_states(g, q):
                w = work_bank(("st", g, q), 0)
                wait_read(pe, ("b", g))
                pe.wait_ge(sem("g_xde"), 2 * g + q + 1)
                for c in range(3):
                    last = mm(w[:, c * P:(c + 1) * P], btok[:, c, :], xde[:, c, q * P:(q + 1) * P],
                              start=True, stop=True)
                last.then_inc(wk_done[0], 1)

            def pair_out(g, q):
                w = work_bank(("y", g, q), 1)
                pe.wait_ge(sem("g_cp"), 2 * g + q + 1)
                pe.wait_ge(sem("g_ab"), 2 * g + q + 1)
                for hh in range(2):
                    o = w[hh * 64:(hh + 1) * 64, :]
                    for c in range(TT):
                        last = mm(o[:, c * P:(c + 1) * P], xdt[:, c, q * P + hh * 64:q * P + (hh + 1) * 64],
                                  Mm[:, hh, c * P:(c + 1) * P], start=True, stop=(c == 0))
                        if c:
                            last = mm(o[:, c * P:(c + 1) * P], Ss[:, c - 1, hh * 64:(hh + 1) * 64],
                                      Ab[:, hh, c * P:(c + 1) * P], start=False, stop=True)
                last.then_inc(wk_done[1], 1)

            def group_norm(g):
                w = work_bank(("gn", g), 3)
                pe.wait_ge(sem("g_sq"), g + 1)
                mm(w[:, :], ones, sq[:, 0, :], start=True, stop=False)
                mm(w[:, :], ones, sq[:, 1, :], start=False, stop=True).then_inc(wk_done[3], 1)

            for g in range(-1, GROUPS):
                for k in range(6):
                    if g + 1 < GROUPS:
                        strip(AT["ssd", g + 1, k], XA)
                        for t in OUT0_AT.get(k, []) if g == 4 else []:
                            strip(AT["out0", t], XB, xn=tiles_from("y0") if t == 0 else None)
                    else:
                        strip(AT["gssm"] + k, XA)
                    if g < 0:
                        continue
                    if k == 0:
                        group_turns(g)
                    elif k == 1:
                        pair_states(g, 0)
                        if g:
                            group_norm(g - 1)
                    elif k == 2:
                        pair_out(g, 0)
                    elif k == 3:
                        pair_states(g, 1)
                    elif k == 5:
                        pair_out(g, 1)
            strip(AT["gssm"] + 6, XA)
            group_norm(GROUPS - 1)
            strip(AT["gssm"] + 7, XA)
            for n in range(KT):
                strip(AT["ssmout1"] + n, XB, xn=tiles_from("y1") if n == 0 else None)
                if n == 2:
                    norm(NORM["conv"])
                if n == 5:
                    norm(NORM["conv"] + 1)
            for n in range(KT):
                strip(AT["gconv"] + n, XA)
            for n in range(KT):
                strip(AT["pw"] + n, XB, xn=tiles_from("conv") if n == 0 else None)
            for n in range(KT):
                strip(AT["w_out2"] + n, XA, xn=tiles_from("mix") if n == 0 else None)
            norm(NORM["post"])
            for c, nt in enumerate(CHUNK2):
                if c == 0:
                    for n in range(2 * nt):
                        strip(AT["gu0"] + n, XA, xn=tiles_from("ffn") if n == 0 else None)
                        if n == 0:
                            norm(NORM["ffn"])
                else:
                    with pe.Fori(0, nt // 2) as i:
                        for u in range(4):
                            strip(AT[f"gu{c}"] + u, XA, i=i)
                for n in range(KT):
                    strip(AT[f"down{c}"] + n, XB, kts=range(nt), xn=tiles_from(f"g{c}", nt) if n == 0 else None)
            norm(NORM["ffpost"])

        @block.sync
        def _(sp):
            sp.dma_start(vec[:, :], vectors).then_inc(sem("vec_loaded"), 16)
            for q in range(2):
                sp.dma_start(h[:, q * 4 * S:(q + 1) * 4 * S], xT[:, q * 4 * S:(q + 1) * 4 * S])\
                    .then_inc(sem(f"h_in{q}"), 16)
                sp.dma_start(raw[q][:, :], weights[q]).then_inc(raw_ready[q], 16)
            sp.dma_start(cst[:, :], consts).then_inc(loaded, 16)
            sp.dma_start(mem_in, memT).then_inc(sem("mem_loaded"), 16)
            turns = (NS_FULL - 2) // 2
            with sp.Fori(0, turns) as i:
                for u in range(2):
                    sp.wait_ge(w_lo, i * 2 + (u + 1))
                    sp.dma_start(raw[u][:, :], weights[bass.ds(i * 2 + (2 + u), 1), :, :].rearrange("a p n -> (a p) n"))\
                        .then_inc(raw_ready[u], 16)
            for j in range(2 * turns + 2, NS):
                sp.wait_ge(w_lo, j - 1)
                w = weights[j] if j < NS_FULL else weights6[j - NS_FULL]
                sp.dma_start(raw[j % 2][:, 0:w.shape[1]], w).then_inc(raw_ready[j % 2], 16)
            for n in range(0, KT, 2):
                sp.wait_ge(sem("result"), n + 2)
                sp.dma_start(outT[:, n * S:(n + 2) * S], tile(h, n, 2 * S)).then_inc(sem("stored"), 16)
            sp.wait_ge(sem("stored"), 16 * KT // 2)

        @block.gpsimd
        def _(pool):
            def low(s, r, j, i):
                pool.wait_ge(w_hi, val(j + 1, i, 4))
                nc.gpsimd.tensor_tensor(wl[s][:, :], raw[r][:, :], wh[s][:, :].bitcast(F32), ALU.subtract)\
                    .then_inc(w_lo, 1)

            first = (AT["ssd", 0, 0] + 4) // 4 * 4
            with pool.Fori(0, first // 4) as i:
                for u in range(4):
                    low(u, u % 2, u, i)

            def decays(g, q):
                n, hd = 2 * g + q, 4 * g + 2 * q
                a4 = Ab.rearrange("p h (c l) -> p h c l", c=TT)
                acol = dacs[:, 1, :, hd:hd + 2].rearrange("p c (h o) -> p h c o", o=1)
                pool.wait_ge(sem("spread"), 16 * (n + 1))
                if n == 0:
                    wait_read(pool, "dacs")
                sub = nc.gpsimd.tensor_tensor
                sub(s_dte.rearrange("p (h c o) -> p h c o", h=2, o=1), a4[:, :, :, P - 1:P], acol, ALU.subtract)
                pool.drain().then_inc(sem("g_dte"), 1)
                sub(Mm.rearrange("p h (c l) -> p h c l", c=TT), a4, acol.broadcast_to([P, 2, TT, P]), ALU.subtract)
                pool.drain()
                nc.gpsimd.tensor_scalar(Mm[:, :, :], Mm[:, :, :], 0.0, None, ALU.min)
                pool.drain().then_inc(sem("g_seg"), 1)

            def decayed_c(g, q):
                pool.wait_ge(sem("g_exp"), 3 * (2 * g + q) + 3)
                pool.wait_ge(sem("g_xf"), 4 * g + 4)
                c = xfs[g % 2][3].rearrange("p (a b) -> p a b", a=1)
                nc.gpsimd.tensor_tensor(Ab[:, :, :], Ab[:, :, :], c.broadcast_to([P, 2, S]), ALU.mult)
                pool.drain().then_inc(sem("g_ab"), 1)

            j = first
            for g in range(-1, GROUPS):
                for k in range(6):
                    at_slot = AT["ssd", g + 1, k] if g + 1 < GROUPS else AT["gssm"] + k
                    at_slot += len(OUT0_AT.get(k, [])) if g == 4 else 0
                    if k in (1, 4) and g >= 0:
                        decayed_c(g, k // 3)
                    while j <= at_slot + 4:
                        low(j % 4, j % 2, j, None)
                        j += 1
                    if k == 5 and g + 1 < GROUPS:
                        decays(g + 1, 0)
                    if k == 2 and g >= 0:
                        decays(g, 1)
            def lows(j, end):
                while j % 4:
                    low(j % 4, j % 2, j, None)
                    j += 1
                with pool.Fori(0, (end - j) // 4) as i:
                    for u in range(4):
                        pool.wait_ge(w_hi, i * 4 + (j + u + 1))
                        nc.gpsimd.tensor_tensor(wl[u][:, :], raw[u % 2][:, :], wh[u][:, :].bitcast(F32), ALU.subtract)\
                            .then_inc(w_lo, 1)
                for n in range(j + (end - j) // 4 * 4, end):
                    low(n % 4, n % 2, n, None)

            lows(j, AT["gu0"] + 4)
            for n in range(KT):
                pool.wait_ge(sem("post_x"), n + 1)
                nc.gpsimd.tensor_tensor(tile(h, n), tile(h, n), xt[:, n % 2, :], ALU.add)
                pool.drain().then_inc(h_upd, 1)
            lows(AT["gu0"] + 4, NS)

        @block.scalar
        def _(act):
            act_ = nc.scalar.activation

            def high(j, i=None, per=4):
                act.wait_ge(raw_ready[j % 2], val(16 * (j // 2 + 1), i, 8 * per))
                act_(wh[j % 4][:, :], raw[j % 2][:, :], ACT.Copy).then_inc(w_hi, 1)

            def step(j, i=None, per=4, last=False):
                if j + 4 < NS and not last:
                    act.wait_ge(strip_done, val(j + 1, i, per))
                    high(j + 4, i, per)

            def square(src, t, k, w=S):
                act.wait_ge(h_upd, k + 1)
                act_(sq[:, t % 2, 0:w], src, ACT.Square).then_inc(sq_done, 1)

            def high_tile(src, g, t, k, w=S):
                act.wait_ge(h_upd, k + 1)
                act_(tile(XA[0], t, w), src, ACT.Identity, scale=g).then_inc(hi_done, 1)
                act_(sq[:, t % 2, 0:w], src, ACT.Square).then_inc(sq_done, 1)

            def root(k, scale=1.0 / D, eps=EPS, dst=std, w=S):
                ps = wait_full(act, ("norm", k))
                free(act_(dst[:, 0:w], ps[:, 0:w], ACT.Sqrt, bias=eps_ap(eps), scale=scale), ("norm", k))

            def eps_ap(e):
                return cst[:, COFF["eps"] + (0 if e == EPS else 1):COFF["eps"] + (0 if e == EPS else 1) + 1]

            act.wait_ge(sem("vec_loaded"), 16)
            for t in range(KT):
                if t % 4 == 0:
                    act.wait_ge(sem(f"h_in{t // 4}"), 16)
                high_tile(tile(h, t), V("mix_g", t), t, SQN["in"] + t)
                if t % 2:
                    high(t // 2)
            act.wait_ge(loaded, 16)
            act_(ident_bf[:, :], ident, ACT.Copy)
            act_(neg_bf[:, :], C("neg"), ACT.Copy).then_inc(const_rdy, 1)
            root(NORM["in"])
            act.wait_ge(sem("lb_sub"), 1)
            act_(s_tmp[:, 4:12], s_tmp[:, 4:12], ACT.Exp).then_inc(sem("lb_exp"), 1)
            def turned_values(t):
                ps = wait_full(act, ("gi", t))
                free(act_(hgi[:, :, t * P:(t + 1) * P], blocks(ps[:, :]), ACT.Copy), ("gi", t))

            for n in range(3 * HG):
                step(AT["hgrn"] + n)
                t = n % 4
                if n < 4:
                    act.wait_ge(sem("hg_raw"), n + 1)
                    act_(tile(hb, t), tile(hkk, t), ACT.Sigmoid)
                    act_(tile(hkk, t), tile(hkk, t), ACT.Sigmoid, scale=-1.0).then_inc(sem("hg_sig"), 1)
                elif n < 8:
                    act.wait_ge(sem("hg_raw"), n + 1)
                    act_(tile(hqq, t), tile(hqq, t), ACT.Silu).then_inc(sem("hg_sig"), 1)
                if n >= 9:
                    turned_values(n - 9)
            step(AT["fox", 0])
            turned_values(HG - 1)
            for t in range(HG):
                act.wait_ge(sem("hg_f"), t + 1)
                act_(tile(hb, t), tile(hb, t), ACT.Ln).then_inc(sem("hg_ln"), 1)

            def out_root(t):
                ps = wait_full(act, ("hn", t))
                free(act_(std[:, :], ps[:, :], ACT.Sqrt, bias=eps_ap(EPS), scale=1.0 / P), ("hn", t))

            def fox_step(n):
                step(AT["fox", n])
                if 3 <= n <= 6:
                    ps = wait_full(act, ("fv", n - 3))
                    free(act_(fv[:, :, (n - 3) * P:(n - 2) * P], blocks(ps[:, :]), ACT.Copy), ("fv", n - 3))

            def level_exps(t, l):
                half = 1 << (l - 1)
                e = hE[:, l % 2, :].rearrange("p (n c) -> p n c", c=2 * half)
                act.wait_ge(sem("h_d"), 7 * t + l)
                act_(e[:, :, 0:half], e[:, :, 0:half], ACT.Exp, scale=-1.0)
                act_(e[:, :, half:], e[:, :, half:], ACT.Exp).then_inc(sem("h_e"), 1)

            for t in range(HG):
                if t == 0:
                    level_exps(t, 1)
                for l in range(1, LEVELS):
                    if l + 1 < LEVELS:
                        level_exps(t, l + 1)
                    if l == 2:
                        step(AT["gg", t])
                    if (t, l) in FILL:
                        fox_step(FILL[t, l])
                        act.wait_ge(sem("gg_raw"), t + 1)
                        act_(tile(hgg, t), tile(hgg, t), ACT.Silu).then_inc(sem("gg_s"), 1)
                    if l == 3 and t:
                        out_root(t - 1)
                    if t == 2 and l == 5:
                        act.wait_ge(sem("f_abs"), 1)
                        act_(xt[0:FH, 0, :], xt[0:FH, 0, :], ACT.Exp, scale=-1.0).then_inc(sem("f_exp"), 1)
                    if t == 2 and l == 7:
                        act.wait_ge(sem("f_one"), 1)
                        act_(xt[0:FH, 1, :], xt[0:FH, 1, :], ACT.Ln).then_inc(sem("f_exp"), 1)
                act.wait_ge(sem("h_end"), t + 1)
                act_(hE[:, 0, :], hE[:, 0, :], ACT.Exp).then_inc(sem("h_eb"), 1)
                act.wait_ge(sem("h_z"), 7 * t + LEVELS - 1)
                act_(hE[:, 1, :], tile(hb, t), ACT.Exp).then_inc(sem("h_eb"), 1)
                ps = wait_full(act, ("kt", t))
                free(act_(hkt[:, :, :], blocks(ps[:, 0:3 * P]), ACT.Copy), ("kt", t))
                fox_step(FILL[t, "hs"])
                if t + 1 < HG:
                    level_exps(t + 1, 1)
                fox_step(FILL[t, "ho"])
                ps = wait_full(act, ("ho", t))
                act_(tile(hb, t), ps[:, :], ACT.Copy)
                free(act_(sq[:, t % 2, :], ps[:, :], ACT.Square), ("ho", t))
            out_root(HG - 1)

            act.wait_ge(sem("mem_loaded"), 16)
            for t in range(KT):
                high_tile(mem_in[:, t * NMEM:(t + 1) * NMEM], V("mem_g", t), t, SQN["mem"] + t, NMEM)

            def nf(hd):
                ps = wait_full(act, ("nf", hd))
                free(act_(nfb[:, hd % 2, :], ps[:, :], ACT.Copy), ("nf", hd))

            def fox_exp(u):
                n = (u % TT + 1) * P
                act.wait_ge(sem("f_s"), u + 1)
                act_(fS[:, u % 4, 0:n], fS[:, u % 4, 0:n], ACT.Exp, bias=s_nm[:, u % 4:u % 4 + 1], scale=-1.0,
                     accum_out=s_rs[:, u % 4:u % 4 + 1]).then_inc(sem("f_e"), 1)

            def mem_turned(t):
                ps = wait_full(act, ("mv", t))
                free(act_(memv[:, :, t * P:(t + 1) * P], blocks(ps[:, 0:NMEM]), ACT.Copy), ("mv", t))

            nf(0)
            root(NORM["mem"], dst=memrstd, w=NMEM)
            fox_exp(0)
            for u in range(FH * TT):
                if u + 1 < FH * TT:
                    fox_exp(u + 1)
                if u % 2 == 0:
                    n = u // 2
                    step(AT["mem"] + n)
                    if n > KT:
                        mem_turned(n - KT - 1)
                if (u + 2) % TT == 0 and u + 2 < FH * TT:
                    nf((u + 2) // TT)
                n = (u % TT + 1) * P
                ps = wait_full(act, ("ft", u))
                free(act_(fPT[:, u % 2, 0:n], ps[:, 0:n], ACT.Copy), ("ft", u))
            mem_turned(KT - 1)

            for n in range(KT):
                step(AT["w_out"] + n)
                high_tile(tile(h, n), V("x_g", n), n, SQN["w_out"] + n)
            root(NORM["w_out"])
            with act.Fori(0, KT // 4) as i:
                for u in range(4):
                    step(AT["xq"] + u, i)
            def x_exp(u):
                act.wait_ge(sem("x_m"), u + 1)
                ps = wait_full(act, ("xs", u))
                free(act_(xP[:, u % 4, :], ps[:, 0:NMEM], ACT.Exp, bias=s_nm[:, u % 4:u % 4 + 1],
                          accum_out=s_rs[:, u % 4:u % 4 + 1]), ("xs", u))

            x_exp(0)
            for u in range(XH * TT):
                a, i = u // TT, u % TT
                if u + 1 < XH * TT:
                    x_exp(u + 1)
                ps = wait_full(act, ("xt", u))
                free(act_(xPT[:, a % 2, :, i * P:(i + 1) * P], blocks(ps[:, 0:NMEM]), ACT.Copy), ("xt", u))
            for n in range(KT):
                step(AT["xo"] + n)
                high_tile(tile(h, n), V("ff_g", n), n, SQN["xo"] + n)
            root(NORM["xo"])
            with act.Fori(0, FF1 // D - 1) as i:
                for u in range(16):
                    step(AT["ffn1"] + u, i, 16)
            for u in range(16):
                step(AT["ffn1"] + 48 + u)
                if u >= KT:
                    square(tile(h, u - KT), u, SQN["final"] + u - KT)
            root(NORM["final"])

            for t in range(KT):
                square(tile(h, t), t, SQN["pre"] + t)
            root(NORM["pre"])
            for t in range(KT):
                act.wait_ge(sem("pre_x"), t + 1)
                act_(tile(XA[0], t), xt[:, t % 2, :], ACT.Copy).then_inc(hi_done, 1)
            step(AT["dt"])
            act.wait_ge(sem("s_abs"), 1)
            act_(xt[0:NSH, 0, :], xt[0:NSH, 0, :], ACT.Exp, scale=-1.0)
            act_(s_nea[0:NSH, :], V("a_log")[0:NSH, :], ACT.Exp).then_inc(sem("s_exp"), 1)
            act.wait_ge(sem("s_one"), 1)
            act_(xt[0:NSH, 1, :], xt[0:NSH, 1, :], ACT.Ln).then_inc(sem("s_exp"), 1)
            act.wait_ge(sem("s_acs"), 1)
            act.dma_start(scratch, acs[0:NSH, :]).then_inc(sem("acs_out"), 16)
            for n in range(2 * KT):
                j, t = AT["glu"] + n, n // 2
                step(j)
                if n % 2:
                    if t > 1:
                        act.wait_ge(sem("glu_v"), t - 1)
                    act.wait_ge(strip_done, j + 1)
                    act_(sq[:, t % 2, :], bank[j % 4][:, :], ACT.Sigmoid, bias=V("glu_b", KT + t))
                    act.drain().then_inc(bank_free[j % 4], 1)
            ps = wait_full(act, "dacs")
            free(act_(dacs.rearrange("p a b c -> p (a b c)"), ps[:, 0:2 * TT * NSH], ACT.Copy), "dacs")

            def spread(n):
                if n:
                    act.wait_ge(wk_done[1], uses[("y", (n - 1) // 2, (n - 1) % 2)][1] + 1)
                act.dma_start(Ab[:, :, :], scratch[2 * n:2 * n + 2, :].partition_broadcast(P))\
                    .then_inc(sem("spread"), 16)

            def leave(ins, j):
                ins.then_inc(bank_free[j % 4], 1)

            def group_in(g, k):
                j = AT["ssd", g, k]
                step(j)
                act.wait_ge(strip_done, j + 1)
                ps = bank[j % 4]
                if k < 4:
                    c, x = 4 * g + k, xt[:, k % 2, :]
                    if c >= 2:
                        act.wait_ge(sem("g_raw"), c - 1)
                    r = rawp[:, k % 2, :]
                    leave(act_(r[:, SK - 1:], ps[:, :], ACT.Copy), j)
                    act.drain()
                    ct = [2 * g, 2 * g + 1, 16 + g, 24 + g][k]
                    act_(x, r[:, 0:S], ACT.Identity, bias=V("sc_b", ct), scale=V("sc_w", ct * SK))
                    act.drain().then_inc(sem("g_tap"), 1)
                else:
                    if g >= 2:
                        act.wait_ge(x_ready, x_of_group(g - 2) + 2)
                    leave(act_(zs2[:, g % 2, k - 4, :], ps[:, :], ACT.Silu), j)
                    act.drain().then_inc(sem("g_z"), 1)
                if 1 <= k <= 4:
                    act.wait_ge(sem("g_raw"), 4 * g + k)
                    if g >= 2:
                        act.wait_ge(sem("g_y"), 2 * g - 2)
                    act_(xfs[g % 2][k - 1], xt[:, (k - 1) % 2, :], ACT.Silu).then_inc(sem("g_xf"), 1)

            def x_of_group(g):
                return XN["y0" if g < 4 else "y1"] + 2 * (g % 4)

            def exps(g, q):
                n = 2 * g + q
                act.wait_ge(sem("g_dte"), n + 1)
                act_(s_dte, s_dte, ACT.Exp).then_inc(sem("g_exp"), 1)
                act.wait_ge(sem("g_seg"), n + 1)
                act_(Mm[:, :, :], Mm[:, :, :], ACT.Exp).then_inc(sem("g_exp"), 1)
                a4 = Ab.rearrange("p h (c l) -> p h c l", c=TT)
                act_(s_dl.rearrange("p (h c o) -> p h c o", h=2, o=1), a4[:, :, :, P - 1:P], ACT.Exp)
                act.drain()
                act_(Ab[:, :, :], Ab[:, :, :], ACT.Exp)
                act.drain().then_inc(sem("g_exp"), 1)

            def y_square(g, q):
                act.wait_ge(sem("g_y"), 2 * g + q + 1)
                ins = act_(sq[:, q, :], zs2[:, g % 2, q, :], ACT.Square)
                if q:
                    ins.then_inc(sem("g_sq"), 1)

            def group_root(g):
                ps = wait_full(act, ("gn", g))
                free(act_(std[:, :], ps[:, :], ACT.Sqrt, bias=eps_ap(EPS), scale=1.0 / (2 * P)), ("gn", g))

            def gate(name, col, t, after=None):
                j = AT[name] + t
                step(j)
                act.wait_ge(strip_done, j + 1)
                if after:
                    act.wait_ge(*after)
                leave(act_(gates[t], bank[j % 4][:, :], ACT.Sigmoid, bias=V("gate_b", col + t)), j)

            act.wait_ge(sem("acs_out"), 16)
            spread(0)
            for g in range(-1, GROUPS):
                for k in range(6):
                    if k == 3 and g >= 0:
                        exps(g, 1)
                    if g + 1 < GROUPS:
                        group_in(g + 1, k)
                        for t in OUT0_AT.get(k, []) if g == 4 else []:
                            j = AT["out0", t]
                            step(j)
                            act.wait_ge(strip_done, j + 1)
                            if t:
                                act.wait_ge(sem("out0"), 16 * t)
                            leave(act_(staged, bank[j % 4][:, :], ACT.Copy), j)
                            act.drain().then_inc(sem("staged"), 1)
                            act.wait_ge(sem("staged"), t + 1)
                            act.dma_start(spill[:, t, :], staged).then_inc(sem("out0"), 16)
                    else:
                        gate("gssm", KT, k, (sem("g_y"), 13 + k) if k < 2 else (x_ready, x_of_group(6) + 2))
                    if g < 0:
                        continue
                    if k == 0:
                        if g:
                            y_square(g - 1, 1)
                        exps(g, 0)
                        ps = wait_full(act, ("b", g))
                        free(act_(btok[:, :, :], blocks(ps[:, 0:3 * P]), ACT.Copy), ("b", g))
                    elif k == 1 and g:
                        group_root(g - 1)
                    elif k == 2:
                        spread(2 * g + 1)
                    elif k == 4:
                        y_square(g, 0)
                    elif k == 5 and g + 1 < GROUPS:
                        spread(2 * g + 2)
            y_square(GROUPS - 1, 1)
            act.wait_ge(sem("out0"), 16 * KT)
            act.dma_start(acc.rearrange("p (a b) -> p a b", a=KT), spill).then_inc(sem("acc_in"), 16)
            gate("gssm", KT, 6)
            group_root(GROUPS - 1)
            gate("gssm", KT, 7)
            act.drain().then_inc(sem("gates_s"), 1)
            for n in range(KT):
                step(AT["ssmout1"] + n)
                if n == 2:
                    ps = wait_full(act, ("norm", NORM["conv"]))
                    free(act_(mu, ps[:, :], ACT.Copy, scale=1.0 / D), ("norm", NORM["conv"]))
                    for t in range(KT):
                        square(cv(t), t, SQN["conv"] + t)
                if n == 5:
                    root(NORM["conv"] + 1, eps=LN_EPS)
            for t in range(KT):
                act.wait_ge(sem("ln_x"), t + 1)
                act_(cv(t), cv(t), ACT.Silu, bias=V("ln_b", t))
            act.drain()
            for t in range(KT):
                act.wait_ge(strip_done, AT["ssmout1"] + KT)
                act_(tile(XB[0], t), cv(t), ACT.Copy)
                act.drain().then_inc(hi_done, 1)
            for t in range(KT):
                gate("gconv", 0, t, (sem("acc_g"), KT))
            act.drain().then_inc(sem("gates_s"), 1)
            for t in range(KT):
                step(AT["pw"] + t)
                act.wait_ge(sem("mixed"), t + 1)
                act_(tile(XA[0], t), tile(acc, t), ACT.Copy).then_inc(hi_done, 1)
            for n in range(KT):
                j = AT["w_out2"] + n
                step(j)
                act.wait_ge(strip_done, j + 1)
                if n == 0:
                    act.wait_ge(x_ready, XN["mix"] + KT)
                act_(cv(n), bank[j % 4][:, :], ACT.Copy)
                act.wait_ge(h_upd, SQN["post"] + n + 1)
                leave(act_(sq[:, n % 2, :], bank[j % 4][:, :], ACT.Square), j)
                act.drain().then_inc(sq_done, 1)
            root(NORM["post"])
            for n in range(KT):
                high_tile(tile(h, n), V("ffn_g", n), n, SQN["ffn"] + n)
            root(NORM["ffn"])
            k = 0
            for c, nt in enumerate(CHUNK2):
                turns = nt // 2
                with act.Fori(0, turns) as i:
                    for u in range(4):
                        step(AT[f"gu{c}"] + u, i)
                        if u % 2 == 0:
                            act.wait_ge(sem("ff_g"), i * 2 + (k + u // 2 + 1))
                            act_(sq[:, u // 2, :], xt[:, u // 2, :], ACT.Sigmoid).then_inc(sem("ff_s"), 1)
                k += nt
                for n in range(KT):
                    step(AT[f"down{c}"] + n)
                    if c == 2:
                        square(tile(acc, n), n, SQN["ffpost"] + n)
            root(NORM["ffpost"])

        @block.vector
        def _(dve):
            TTop, STT, TS = nc.vector.tensor_tensor, nc.vector.scalar_tensor_tensor, nc.vector.tensor_scalar
            copy = nc.vector.tensor_copy

            def taken(j, i=None, per=4):
                dve.wait_ge(strip_done, val(j + 1, i, per))
                return bank[j % 4]

            def leave(ins, j):
                ins.then_inc(bank_free[j % 4], 1)

            def split(src, X, k, w=S):
                copy(tile(X[0], k, w), src)
                dve.drain()
                TTop(tile(X[1], k, w), src, tile(X[0], k, w).bitcast(F32), ALU.subtract).then_inc(x_ready, 1)

            def sum_square(t, k, w=S):
                dve.wait_ge(sq_done, k + 1)
                if t == 0:
                    copy(ssum[:, 0:w], sq[:, 0, 0:w])
                else:
                    TTop(ssum[:, 0:w], ssum[:, 0:w], sq[:, t % 2, 0:w], ALU.add)
                dve.drain()

            def low_tile(src, g, t, name, w=S):
                dve.wait_ge(hi_done, HI[name] + t + 1)
                STT(tile(XA[1], t, w), src, g, tile(XA[0], t, w).bitcast(F32), ALU.mult, ALU.subtract)\
                    .then_inc(x_ready, 1)
                sum_square(t, SQN[name] + t, w)

            def prep(src, g, name, w=S):
                for t in range(KT):
                    dve.drain().then_inc(h_upd, 1)
                    if t:
                        low_tile(src(t - 1), V(g, t - 1), t - 1, name, w)
                low_tile(src(KT - 1), V(g, KT - 1), KT - 1, name, w)

            def invert(k, dst, w=S):
                dve.drain().then_inc(ssum_rdy, 1)
                wait_read(dve, ("norm", k))
                nc.vector.reciprocal(dst[:, 0:w], std[:, 0:w])
                dve.drain()

            def residual(n, name, j, g=None):
                ps = taken(j)
                leave(TTop(tile(h, n), tile(h, n), ps[:, :], ALU.add), j)
                dve.drain().then_inc(h_upd, 1)
                for t in ([n - 1] if n else []) + ([n] if n == KT - 1 else []):
                    if g is None:
                        sum_square(t, SQN[name] + t)
                    else:
                        low_tile(tile(h, t), V(g, t), t, name)

            dve.wait_ge(sem("vec_loaded"), 16)
            prep(lambda t: tile(h, t), "mix_g", "in")
            dve.wait_ge(loaded, 16)
            TTop(s_tmp[:, 0:4], V("lb0", 0, 4), V("lb1", 0, 4), ALU.max)
            dve.drain()
            TTop(s_tmp[:, 4:8], V("lb0", 0, 4), s_tmp[:, 0:4], ALU.subtract)
            TTop(s_tmp[:, 8:12], V("lb1", 0, 4), s_tmp[:, 0:4], ALU.subtract)
            dve.drain().then_inc(sem("lb_sub"), 1)
            invert(NORM["in"], rstd)
            for n in range(3 * HG):
                j, t = AT["hgrn"] + n, n % 4
                ps = taken(j)
                dst = [tile(hkk, t), tile(hqq, t), xt[:, t % 2, :]][n // 4]
                if 10 <= n <= 11:
                    dve.wait_ge(wk_done[t % 2], uses[("gi", t - 2)][1] + 1)
                leave(TTop(dst, ps[:, :], rstd[:, :], ALU.mult), j)
                dve.drain().then_inc(sem("hg_raw"), 1)
                if n < 4:
                    dve.wait_ge(sem("hg_sig"), n + 1)
                    if n == 0:
                        dve.wait_ge(sem("lb_exp"), 1)
                        TTop(s_tmp[:, 0:4], s_tmp[:, 4:8], s_tmp[:, 8:12], ALU.add)
                        dve.drain()
                        nc.vector.reciprocal(s_tmp[:, 12:16], s_tmp[:, 0:4])
                        dve.drain()
                        TTop(s_lb, s_tmp[:, 4:8], s_tmp[:, 12:16], ALU.mult)
                        TTop(s_oml, s_tmp[:, 8:12], s_tmp[:, 12:16], ALU.mult)
                        dve.drain()
                    TS(tile(hb, t), tile(hb, t), s_oml[:, t:t + 1], s_lb[:, t:t + 1], ALU.mult, ALU.add)
                    TS(tile(hkk, t), tile(hkk, t), s_oml[:, t:t + 1], None, ALU.mult)
                    dve.drain().then_inc(sem("hg_f"), 1)

            def fox_in(n):
                j = AT["fox", n]
                name, t = STREAM[j]
                ps = taken(j)
                if name == "ff":
                    leave(TTop(fneg[0:FH, :], ps[0:FH, :], rstd[0:FH, :], ALU.mult), j)
                elif name == "fv":
                    if t >= 2:
                        dve.wait_ge(wk_done[2], uses[("fv", t - 2)][1] + 1)
                    leave(TTop(xt[:, t % 2, :], ps[:, :], rstd[:, :], ALU.mult), j)
                    dve.drain().then_inc(sem("fv_raw"), 1)
                elif name == "fq":
                    leave(STT(tile(fq, t), ps[:, :], FD ** -0.5, rstd[:, :], ALU.mult, ALU.mult), j)
                else:
                    leave(TTop(tile(fk, t), ps[:, :], rstd[:, :], ALU.mult), j)

            fox_in(0)
            for t in (2, 3):
                dve.wait_ge(wk_done[t % 2], uses[("gi", t)][1] + 1)
            dve.wait_ge(sem("hg_sig"), 2 * HG)
            for t in range(HG):
                dve.wait_ge(sem("hg_ln"), t + 1)
                nc.vector.tensor_tensor_scan(tile(hb, t), reset, tile(hb, t), 0.0, ALU.mult, ALU.add)
            dve.drain().then_inc(sem("hg_scan"), 1)

            def out_rstd(t):
                wait_read(dve, ("hn", t))
                nc.vector.reciprocal(std[:, :], std[:, :])
                dve.drain()

            def out_norm(t):
                dve.wait_ge(sem("gg_s"), t + 1)
                TTop(tile(hb, t), tile(hb, t), std[:, :], ALU.mult)
                dve.drain()
                STT(tile(hb, t), tile(hb, t), V("hgrn_g"), tile(hgg, t), ALU.mult, ALU.mult)
                dve.drain()

            def distance(t, l):
                half = 1 << (l - 1)
                b = tile(hb, t).rearrange("p (n c) -> p n c", c=2 * half)
                TTop(hE[:, l % 2, :].rearrange("p (n c) -> p n c", c=2 * half), b,
                     b[:, :, half - 1:half].broadcast_to([P, S // (2 * half), 2 * half]), ALU.subtract)\
                    .then_inc(sem("h_d"), 1)

            def gather(t, l):
                ps = wait_full(dve, ("level", t, l))
                mask = C("lev", l).rearrange("p (a b) -> p a b", a=1).broadcast_to([P, TT, P])
                if l == 0:
                    if t:
                        dve.wait_ge(wk_done[2], uses[("ho", t - 1)][1] + 1)
                    free(TTop(blocks(hattn), blocks(ps[:, :]), mask, ALU.mult), ("level", t, l))
                else:
                    free(nc.vector.copy_predicated(blocks(hattn), mask.bitcast(I32), blocks(ps[:, :])),
                         ("level", t, l))
                dve.drain()

            def one_plus(rows, exp_done, one):
                dve.wait_ge(exp_done, 1)
                TS(xt[0:rows, 1, :], xt[0:rows, 0, :], 1.0, None, ALU.add)
                dve.drain()
                TS(ssum[0:rows, :], xt[0:rows, 1, :], -1.0, None, ALU.add)
                dve.drain()
                TTop(xt[0:rows, 0, :], xt[0:rows, 0, :], ssum[0:rows, :], ALU.subtract)
                dve.drain().then_inc(one, 1)

            def log_one_plus(rows, exp_done):
                dve.wait_ge(exp_done, 2)
                TTop(xt[0:rows, 1, :], xt[0:rows, 1, :], xt[0:rows, 0, :], ALU.add)
                dve.drain()

            def fox_gates(stage):
                if stage == 0:
                    dve.wait_ge(wk_done[2], uses[("fv", 3)][1] + 1)
                    TS(fneg[0:FH, :], fneg[0:FH, :], V("foxb")[0:FH, :], None, ALU.add)
                    dve.drain()
                    STT(xt[0:FH, 0, :], fneg[0:FH, :], -1.0, fneg[0:FH, :], ALU.mult, ALU.max)
                    dve.drain().then_inc(sem("f_abs"), 1)
                elif stage == 1:
                    one_plus(FH, sem("f_exp"), sem("f_one"))
                else:
                    log_one_plus(FH, sem("f_exp"))
                    STT(xt[0:FH, 1, :], fneg[0:FH, :], 0.0, xt[0:FH, 1, :], ALU.min, ALU.subtract)
                    dve.drain()
                    TS(ssum[0:FH, :], xt[0:FH, 1, :], 0.0, 1.0, ALU.mult, ALU.add)
                    dve.drain()
                    nc.vector.tensor_tensor_scan(fneg[0:FH, :], ssum[0:FH, :], xt[0:FH, 1, :], 0.0, ALU.mult,
                                                 ALU.subtract)
                    dve.drain().then_inc(sem("f_neg"), 1)

            for t in range(HG):
                distance(t, 1)
                for l in range(1, LEVELS):
                    if l + 1 < LEVELS:
                        distance(t, l + 1)
                    else:
                        b = blocks(tile(hb, t))
                        TTop(blocks(hE[:, 0, :]), b[:, :, P - 1:P].broadcast_to([P, TT, P]), b, ALU.subtract)\
                            .then_inc(sem("h_end"), 1)
                    half = 1 << (l - 1)

                    def halves(a, k):
                        return a.rearrange("p (n c) -> p n c", c=2 * half)[:, :, k * half:(k + 1) * half]

                    dve.wait_ge(sem("h_e"), 7 * t + l)
                    if l == 2 and t:
                        wait_read(dve, ("kt", t - 1))
                    e, z = hE[:, l % 2, :], hZ[:, l % 2, :]
                    TTop(halves(z, 0), halves(tile(hkk, t), 0), halves(e, 0), ALU.mult)
                    TTop(halves(z, 1), halves(tile(hqq, t), 1), halves(e, 1), ALU.mult)
                    dve.drain().then_inc(sem("h_z"), 1)
                    if l == 1 and t:
                        fox_in(FILL[t - 1, "ho"])
                    gather(t, l - 1)
                    if l == 3:
                        j = AT["gg", t]
                        leave(TTop(tile(hgg, t), taken(j)[:, :], rstd[:, :], ALU.mult), j)
                        dve.drain().then_inc(sem("gg_raw"), 1)
                    if (t, l - 1) in FILL:
                        fox_in(FILL[t, l - 1])
                    if l == 4 and t:
                        out_rstd(t - 1)
                        out_norm(t - 1)
                    if (t, l) in ((2, 4), (2, 6), (3, 2)):
                        fox_gates(((2, 4), (2, 6), (3, 2)).index((t, l)))
                dve.wait_ge(sem("h_eb"), 2 * t + 1)
                TTop(hZ[:, 0, :], tile(hkk, t), hE[:, 0, :], ALU.mult)
                dve.drain().then_inc(sem("h_qk"), 1)
                gather(t, LEVELS - 1)
                dve.wait_ge(sem("h_eb"), 2 * t + 2)
                TTop(hZ[:, 2, :], tile(hqq, t), hE[:, 1, :], ALU.mult)
                copy(s_eb, hE[:, 1, P - 1::P])
                dve.drain()
                fox_in(FILL[t, "hs"])
                ps = wait_full(dve, ("hs", t))
                copy(hS[:, 0, :], ps[:, 0:P])
                dve.drain()
                STT(hS[:, 1, :], hS[:, 0, :], s_eb[:, 1:2], ps[:, P:2 * P], ALU.mult, ALU.add)
                dve.drain()
                free(STT(hS[:, 2, :], hS[:, 1, :], s_eb[:, 2:3], ps[:, 2 * P:3 * P], ALU.mult, ALU.add), ("hs", t))
                dve.drain().then_inc(sem("h_s"), 1)
            fox_in(FILL[HG - 1, "ho"])

            dve.wait_ge(strip_done, AT["mem"])
            prep(lambda t: mem_in[:, t * NMEM:(t + 1) * NMEM], "mem_g", "mem", NMEM)
            dve.drain().then_inc(ssum_rdy, 1)
            def fox_logits(u):
                hd, n = u // TT, (u % TT + 1) * P
                if u % TT == 0:
                    wait_read(dve, ("nf", hd))
                ps = wait_full(dve, ("fs", u))
                if u >= 4:
                    dve.wait_ge(wk_done[2], uses[("ft", u - 4)][1] + 1)
                free(nc.vector.tensor_tensor_reduce(
                    out=fS[:, u % 4, 0:n], in0=ps[:, 0:n], in1=nfb[:, hd % 2, 0:n], scale=-1.0, scalar=3.0e38,
                    op0=ALU.add, op1=ALU.min, accum_out=s_nm[:, u % 4:u % 4 + 1]), ("fs", u))
                dve.drain().then_inc(sem("f_s"), 1)

            def mem_in_strip(n):
                j = AT["mem"] + n
                ps = taken(j)
                if n < KT:
                    leave(TTop(memk[:, n * NMEM:(n + 1) * NMEM], ps[:, 0:NMEM], memrstd, ALU.mult), j)
                else:
                    t = n - KT
                    if t >= 2:
                        dve.wait_ge(wk_done[2], uses[("mv", t - 2)][1] + 1)
                    leave(TTop(xt[:, t % 2, 0:NMEM], ps[:, 0:NMEM], memrstd, ALU.mult), j)
                    dve.drain().then_inc(sem("mv_raw"), 1)

            def normalise(sums_ready, n, a, u, done):
                if sums_ready is not None:
                    dve.wait_ge(sums_ready, u + 1)
                nc.vector.reciprocal(s_ri[:, u % 4:u % 4 + 1], s_rs[:, u % 4:u % 4 + 1])
                dve.drain()
                TS(a[:, u % 4, 0:n], a[:, u % 4, 0:n], s_ri[:, u % 4:u % 4 + 1], None, ALU.mult)
                dve.drain().then_inc(done, 1)

            def split_work(key, k):
                ps = wait_full(dve, key)
                copy(tile(XB[0], k), ps[:, :])
                dve.drain()
                free(TTop(tile(XB[1], k), ps[:, :], tile(XB[0], k).bitcast(F32), ALU.subtract), key)
                dve.drain().then_inc(x_ready, 1)

            fox_logits(0)
            fox_logits(1)
            wait_read(dve, ("norm", NORM["mem"]))
            nc.vector.reciprocal(memrstd, memrstd)
            dve.drain()
            for u in range(FH * TT):
                normalise(sem("f_e"), (u % TT + 1) * P, fS, u, sem("f_p"))
                if u % 8 == 1 and u > 8:
                    split_work(("fo", u // 8 - 1), u // 8 - 1)
                if u % 2 == 0:
                    mem_in_strip(u // 2)
                if u + 2 < FH * TT:
                    fox_logits(u + 2)
                if u == 0:
                    out_rstd(HG - 1)
                if u == 1:
                    out_norm(HG - 1)
                if 2 <= u <= HG + 1:
                    split(tile(hb, u - 2), XB, 2 + u)
            split_work(("fo", 3), 3)

            for n in range(KT):
                residual(n, "w_out", AT["w_out"] + n, "x_g")
            invert(NORM["w_out"], rstd)
            with dve.Fori(0, KT // 4) as i:
                for u in range(4):
                    ps = taken(AT["xq"] + u, i)
                    leave(STT(tile(xqf, i * 4 + u), ps[:, :], XD ** -0.5, rstd[:, :], ALU.mult, ALU.mult), AT["xq"] + u)
            dve.drain().then_inc(sem("xq_rdy"), 1)

            def x_max(u):
                ps = wait_full(dve, ("xs", u))
                nc.vector.tensor_reduce(s_nm[:, u % 4:u % 4 + 1], ps[:, 0:NMEM], AX_X, ALU.max, negate=True)\
                    .then_inc(sem("x_m"), 1)

            x_max(0)
            x_max(1)
            for u in range(XH * TT):
                wait_read(dve, ("xs", u))
                normalise(None, NMEM, xP, u, sem("x_p"))
                if u % 2 and u > 5:
                    split_work(("xo", (u - 7) // 2), (u - 7) // 2)
                if u + 2 < XH * TT:
                    if u > 1:
                        dve.wait_ge(wk_done[2], uses[("xt", u - 2)][1] + 1)
                    x_max(u + 2)
            for k in range(KT - 3, KT):
                split_work(("xo", k), k)
            for n in range(KT):
                residual(n, "xo", AT["xo"] + n, "ff_g")
            invert(NORM["xo"], rstd)

            def hidden(j, u, i):
                ps = taken(j, i, 16)
                leave(STT(xt[:, u % 2, :], ps[:, :], 0.0, rstd[:, :], ALU.max, ALU.mult), j)
                dve.drain()
                TTop(xt[:, u % 2, :], xt[:, u % 2, :], xt[:, u % 2, :], ALU.mult)
                dve.drain()
                split(xt[:, u % 2, :], XB, u)

            with dve.Fori(0, FF1 // D - 1) as i:
                for u in range(KT):
                    hidden(AT["ffn1"] + u, u, i)
                for u in range(KT):
                    j = AT["ffn1"] + KT + u
                    ps = taken(j, i, 16)
                    leave(TTop(tile(h, u), tile(h, u), ps[:, :], ALU.add), j)
                dve.drain()
            for u in range(KT):
                hidden(AT["ffn1"] + 48 + u, u, None)
            for u in range(KT):
                residual(u, "final", AT["ffn1"] + 56 + u)
            invert(NORM["final"], rstd)

            def scale_tile(n, g):
                STT(tile(h, n), tile(h, n), g, rstd[:, :], ALU.mult, ALU.mult)

            for n in range(KT):
                scale_tile(n, V("final_g", n))
                dve.drain().then_inc(h_upd, 1)
                if n:
                    sum_square(n - 1, SQN["pre"] + n - 1)
            sum_square(KT - 1, SQN["pre"] + KT - 1)
            nc.vector.memset(vpad[:, :, 0:CONV_K - 1], 0.0)
            nc.vector.memset(rawp[:, :, 0:SK - 1], 0.0)
            invert(NORM["pre"], rstd)

            def pre_low(t):
                dve.wait_ge(hi_done, HI["pre"] + t + 1)
                TTop(tile(XA[1], t), xt[:, t % 2, :], tile(XA[0], t).bitcast(F32), ALU.subtract).then_inc(x_ready, 1)

            for t in range(KT):
                STT(xt[:, t % 2, :], tile(h, t), V("pre_g", t), rstd[:, :], ALU.mult, ALU.mult)
                dve.drain().then_inc(sem("pre_x"), 1)
                if t:
                    pre_low(t - 1)
                    dve.drain()
            pre_low(KT - 1)
            dve.drain()
            ps = taken(AT["dt"])
            leave(TS(acs[0:NSH, :], ps[0:NSH, :], V("dt_b")[0:NSH, :], None, ALU.add), AT["dt"])
            dve.drain()
            STT(xt[0:NSH, 0, :], acs[0:NSH, :], -1.0, acs[0:NSH, :], ALU.mult, ALU.max)
            dve.drain().then_inc(sem("s_abs"), 1)
            one_plus(NSH, sem("s_exp"), sem("s_one"))
            log_one_plus(NSH, sem("s_exp"))
            STT(xt[0:NSH, 1, :], acs[0:NSH, :], 0.0, xt[0:NSH, 1, :], ALU.max, ALU.add)
            dve.drain()
            TS(acs[0:NSH, :], xt[0:NSH, 1, :], s_nea[0:NSH, :], -1.0, ALU.mult, ALU.mult)
            dve.drain()
            nc.vector.tensor_tensor_scan(acs[0:NSH, :], reset[0:NSH, :], acs[0:NSH, :], 0.0, ALU.mult, ALU.add)
            dve.drain().then_inc(sem("s_acs"), 1)
            def depthwise(part):
                t, first = part // 4, CONV_K - 1 - part % 4 * 8
                v, c = vpad[:, t, :], ssum[:, :]
                if part % 4 == 0:
                    TS(c, v[:, CONV_K - 1:], V("dw_w", t * CONV_K + CONV_K - 1), V("dw_b", t), ALU.mult, ALU.add)
                for k in range(min(first, CONV_K - 2), max(first - 8, -1), -1):
                    dve.drain()
                    STT(v[:, 0:S] if k == 0 else c, v[:, k:k + S], V("dw_w", t * CONV_K + k), c, ALU.mult, ALU.add)
                dve.drain()

            parts = iter(range(4 * KT))
            glu_parts = [0, 2, 1, 2, 1, 2, 1, 1]
            dw_slots = {(g, k): 1 for g in range(GROUPS) for k in (3, 5)}
            dw_slots |= {(4, 2): 1, (4, 3): 2, (4, 4): 1, (4, 5): 4}
            assert sum(glu_parts) + sum(dw_slots.values()) == 4 * KT
            for t in range(KT):
                j = AT["glu"] + 2 * t
                dve.wait_ge(bank_free[(j + 1) % 4], (j + 1) // 4 + 1)
                ps = taken(j)
                v = vpad[:, t, CONV_K - 1:]
                leave(STT(v, ps[:, :], V("glu_b", t), sq[:, t % 2, :], ALU.add, ALU.mult), j)
                dve.drain().then_inc(sem("glu_v"), 1)
                for _ in range(glu_parts[t]):
                    depthwise(next(parts))
            def convolve(g, k):
                ct = [2 * g, 2 * g + 1, 16 + g, 24 + g][k]
                x = xt[:, k % 2, :]
                dve.wait_ge(sem("g_tap"), 4 * g + k + 1)
                for tap in range(1, SK):
                    STT(x, rawp[:, k % 2, tap:tap + S], V("sc_w", ct * SK + tap), x, ALU.mult, ALU.add)
                    if tap < SK - 1:
                        dve.drain()
                dve.drain().then_inc(sem("g_raw"), 1)

            def heads(a):
                return a.rearrange("p c (h v) -> p c h v", h=2)

            def group_tokens(g):
                for q in range(2):
                    ps = wait_full(dve, ("x", g, q))
                    dt = dacs[:, 0, :, 4 * g + 2 * q:4 * g + 2 * q + 2].rearrange("p c (h o) -> p c h o", o=1)
                    if g == 0:
                        wait_read(dve, "dacs")
                    free(TTop(heads(xdt[:, :, q * P:(q + 1) * P]), ps[:, :].rearrange("p (c h v) -> p c h v", c=TT, h=2),
                              dt.broadcast_to([P, TT, 2, 64]), ALU.mult), ("x", g, q))
                ps = wait_full(dve, ("cb", g))
                free(TTop(blocks(cbm), blocks(ps[:, :]),
                          tri.rearrange("p (a b) -> p a b", a=1).broadcast_to([P, TT, P]), ALU.mult), ("cb", g))
                dve.drain()

            def to_end(g, q):
                dve.wait_ge(sem("g_exp"), 3 * (2 * g + q) + 1)
                TTop(heads(xde[:, :, q * P:(q + 1) * P]), heads(xdt[:, 0:3, q * P:(q + 1) * P]),
                     s_dte.rearrange("p (h c o) -> p c h o", h=2, o=1)[:, 0:3].broadcast_to([P, 3, 2, 64]), ALU.mult)
                dve.drain().then_inc(sem("g_xde"), 1)

            def products(g, q):
                n = 2 * g + q
                dve.wait_ge(sem("g_exp"), 3 * n + 2)
                TTop(Mm[:, :, :], Mm[:, :, :], cbm.rearrange("p (a b) -> p a b", a=1).broadcast_to([P, 2, S]), ALU.mult)
                ps = wait_full(dve, ("st", g, q))
                dve.wait_ge(sem("g_exp"), 3 * n + 3)
                copy(Ss[:, 0, :], ps[:, 0:P])
                for c in (1, 2):
                    dve.drain()
                    dl = s_dl.rearrange("p (h c) -> p h c", h=2)[:, :, c:c + 1].broadcast_to([P, 2, 64])
                    TTop(Ss[:, c, :].rearrange("p (h v) -> p h v", h=2),
                         Ss[:, c - 1, :].rearrange("p (h v) -> p h v", h=2), dl, ALU.mult)
                    dve.drain()
                    ins = TTop(Ss[:, c, :], Ss[:, c, :], ps[:, c * P:(c + 1) * P], ALU.add)
                free(ins, ("st", g, q))
                dve.drain().then_inc(sem("g_cp"), 1)

            def pair_out(g, q):
                ps = wait_full(dve, ("y", g, q))
                y = std[:, :]
                free(STT(y, xfs[g % 2][q], V("dskip", 2 * g + q), ps[:, :], ALU.mult, ALU.add), ("y", g, q))
                dve.wait_ge(sem("g_z"), 2 * g + q + 1)
                dve.drain()
                z = zs2[:, g % 2, q, :]
                TTop(z, y, z, ALU.mult)
                dve.drain().then_inc(sem("g_y"), 1)

            def group_out(g):
                wait_read(dve, ("gn", g))
                nc.vector.reciprocal(std[:, :], std[:, :])
                dve.drain()
                for q in range(2):
                    z = zs2[:, g % 2, q, :]
                    STT(z, z, V("ssm_g", 2 * g + q), std[:, :], ALU.mult, ALU.mult)
                dve.drain()
                if g == 4:
                    dve.wait_ge(strip_done, AT["out0", KT - 1] + 1)
                for q in range(2):
                    copy(tile(XB[0], 2 * (g % 4) + q), zs2[:, g % 2, q, :])
                dve.drain()
                for q in range(2):
                    k = 2 * (g % 4) + q
                    TTop(tile(XB[1], k), zs2[:, g % 2, q, :], tile(XB[0], k).bitcast(F32), ALU.subtract)\
                        .then_inc(x_ready, 1)

            for g in range(-1, GROUPS):
                for k in range(6):
                    if g >= 0:
                        if k == 0:
                            if g:
                                pair_out(g - 1, 1)
                            group_tokens(g)
                            to_end(g, 0)
                        elif k == 1:
                            products(g, 0)
                        elif k == 2:
                            if g:
                                group_out(g - 1)
                            to_end(g, 1)
                        elif k == 3:
                            pair_out(g, 0)
                        elif k == 4:
                            products(g, 1)
                        for _ in range(dw_slots.get((g, k), 0)):
                            depthwise(next(parts))
                    if g + 1 < GROUPS and (k < 3 or k == 4):
                        convolve(g + 1, min(k, 3))
            pair_out(GROUPS - 1, 1)
            group_out(GROUPS - 1)
            copy(ssum[:, :], cv(0))
            for n in range(1, KT):
                dve.drain()
                TTop(ssum[:, :], ssum[:, :], cv(n), ALU.add)
            dve.drain().then_inc(ssum_rdy, 1)
            dve.wait_ge(sem("gates_s"), 1)
            dve.wait_ge(sem("acc_in"), 16)

            def out1(n):
                j = AT["ssmout1"] + n
                ps = taken(j)
                leave(TTop(tile(acc, n), tile(acc, n), ps[:, :], ALU.add), j)
                dve.drain()
                TTop(tile(acc, n), tile(acc, n), gates[n], ALU.mult)
                dve.drain().then_inc(sem("acc_g"), 1)

            for n in range(3):
                out1(n)
            wait_read(dve, ("norm", NORM["conv"]))
            for n in range(KT):
                TTop(cv(n), cv(n), mu, ALU.subtract)
                dve.drain().then_inc(h_upd, 1)
                if n:
                    sum_square(n - 1, SQN["conv"] + n - 1)
                if n in (3, 6):
                    out1(n // 3 + 2)
            sum_square(KT - 1, SQN["conv"] + KT - 1)
            dve.drain().then_inc(ssum_rdy, 1)
            out1(5)
            wait_read(dve, ("norm", NORM["conv"] + 1))
            nc.vector.reciprocal(rs2, std[:, :])
            dve.drain()
            out1(6)
            for n in range(KT):
                STT(cv(n), cv(n), V("ln_g", n), rs2, ALU.mult, ALU.mult)
                dve.drain().then_inc(sem("ln_x"), 1)
            out1(7)
            for n in range(KT):
                dve.wait_ge(hi_done, HI["conv"] + n + 1)
                TTop(tile(XB[1], n), cv(n), tile(XB[0], n).bitcast(F32), ALU.subtract).then_inc(x_ready, 1)
            dve.wait_ge(sem("gates_s"), 2)

            def mix_low(n):
                dve.wait_ge(hi_done, HI["mix"] + n + 1)
                TTop(tile(XA[1], n), tile(acc, n), tile(XA[0], n).bitcast(F32), ALU.subtract).then_inc(x_ready, 1)

            for n in range(KT):
                j = AT["pw"] + n
                ps = taken(j)
                leave(STT(cv(n), ps[:, :], V("pw_b", n), gates[n], ALU.add, ALU.mult), j)
                dve.drain()
                TTop(tile(acc, n), tile(acc, n), cv(n), ALU.add)
                dve.drain().then_inc(sem("mixed"), 1)
                if n:
                    mix_low(n - 1)
            mix_low(KT - 1)
            for n in range(KT):
                dve.drain().then_inc(h_upd, 1)
                if n:
                    sum_square(n - 1, SQN["post"] + n - 1)
            sum_square(KT - 1, SQN["post"] + KT - 1)
            invert(NORM["post"], rstd)
            for n in range(KT):
                if n > 1:
                    dve.wait_ge(h_upd, SQN["ffn"] + n - 1)
                STT(xt[:, n % 2, :], cv(n), V("post_g", n), rstd[:, :], ALU.mult, ALU.mult)
                dve.drain().then_inc(sem("post_x"), 1)
                if n:
                    low_tile(tile(h, n - 1), V("ffn_g", n - 1), n - 1, "ffn")
            low_tile(tile(h, KT - 1), V("ffn_g", KT - 1), KT - 1, "ffn")
            invert(NORM["ffn"], rstd)
            k = 0
            for c, nt in enumerate(CHUNK2):
                with dve.Fori(0, nt // 2) as i:
                    for u in range(0, 4, 2):
                        j, x = AT[f"gu{c}"] + u, xt[:, u // 2, :]
                        ps = taken(j, i)
                        leave(TTop(x, ps[:, :], rstd[:, :], ALU.mult), j)
                        dve.drain().then_inc(sem("ff_g"), 1)
                        dve.wait_ge(sem("ff_s"), i * 2 + (k + u // 2 + 1))
                        TTop(x, x, sq[:, u // 2, :], ALU.mult)
                        dve.drain()
                        TTop(x, x, rstd[:, :], ALU.mult)
                        dve.drain()
                        ps = taken(j + 1, i)
                        leave(TTop(x, x, ps[:, :], ALU.mult), j + 1)
                        dve.drain()
                        split(x, XB, i * 2 + u // 2)
                        dve.drain()
                k += nt
                for n in range(KT):
                    j = AT[f"down{c}"] + n
                    ps = taken(j)
                    if c == 0:
                        leave(copy(tile(acc, n), ps[:, :]), j)
                        continue
                    leave(TTop(tile(acc, n), tile(acc, n), ps[:, :], ALU.add), j)
                    if c == 2:
                        dve.drain().then_inc(h_upd, 1)
                        sum_square(n, SQN["ffpost"] + n)
                dve.drain()
            invert(NORM["ffpost"], rstd)
            for n in range(KT):
                STT(xt[:, n % 2, :], tile(acc, n), V("ffpost_g", n), rstd[:, :], ALU.mult, ALU.mult)
                dve.drain()
                TTop(tile(h, n), tile(h, n), xt[:, n % 2, :], ALU.add)
                dve.drain().then_inc(sem("result"), 1)


def by_features(a):
    t, f = a.shape
    return np.ascontiguousarray(a.T.reshape(f // P, P, t).transpose(1, 0, 2).reshape(P, -1))


def strip_of(w, n, k0=0, kn=KT):
    part = w[k0 * P:(k0 + kn) * P, n * P:(n + 1) * P]
    if part.shape[1] < P:
        part = np.pad(part, ((0, 0), (0, P - part.shape[1])))
    return part.reshape(kn, P, P).transpose(1, 0, 2).reshape(P, kn * P)


def columns(v):
    v = np.asarray(v).reshape(-1)
    n = -(-v.size // P)
    return np.pad(v, (0, n * P - v.size)).reshape(n, P).T


def lay_out(x):
    g = {k: np.asarray(v) for k, v in x.items()}
    w_in, w_in2, wkv, gu = g["w_in"][0], g["w_in_2"][0], g["w_xkv"][0], g["w_gate_up_2"][0]
    fox, hg = 512, 512
    o = np.cumsum([0, fox, fox, fox, FH, hg, hg, hg, hg])
    part = {n: w_in[:, o[i]:o[i + 1]] for i, n in enumerate(["fq", "fk", "fv", "ff", "gq", "gf", "gi", "gg"])}
    o = np.cumsum([0, D, D, 2 * D, 2 * D, D, D, NSH, D, D])
    part |= {n: w_in2[:, o[i]:o[i + 1]] for i, n in
             enumerate(["val", "glu", "z", "xs", "bm", "cm", "dt", "gconv", "gssm"])}
    part |= {"memk": wkv[:, :D], "memv": wkv[:, D:], "w_out": g["w_out"][0], "xq": g["w_xq"][0], "xo": g["w_xo"][0],
             "w1": g["w1"][0], "w2": g["w2"][0], "ssmout": g["ssm_out_w_2"][0], "pw": g["conv_pw_w_2"][0],
             "w_out2": g["w_out_2"][0], "gate": gu[:, :FF2], "up": gu[:, FF2:], "down": g["w_down_2"][0]}
    full = np.stack([strip_of(part[s[0]], s[1], KT * (s[2] if len(s) > 2 else 0)) for s in STREAM[:NS_FULL]])
    six = np.stack([strip_of(part[s[0]], s[1], KT * s[2], CHUNK2[2]) for s in STREAM[NS_FULL:]])
    lb = g["hgrn_lb_logits"]
    taps = lambda w: w.reshape(w.shape[0], -1, P).transpose(2, 1, 0).reshape(P, -1)
    cols = {"mix_g": g["norm_mix_g"], "mem_g": g["norm_mem_g"], "x_g": g["norm_x_g"], "ff_g": g["norm_ff_g"],
            "final_g": g["final_norm_g"], "pre_g": g["mix_pre_g_2"], "ffn_g": g["ffn_pre_g_2"],
            "post_g": g["mix_post_g_2"], "ffpost_g": g["ffn_post_g_2"], "hgrn_g": g["hgrn_norm_g"], "lb0": lb[0],
            "lb1": lb[1], "foxb": g["fox_f_bias"], "gate_b": g["gate_b_2"], "glu_b": g["glu_b_2"],
            "dw_b": g["conv_dw_b_2"], "ln_g": g["conv_ln_g_2"], "ln_b": g["conv_ln_b_2"], "pw_b": g["conv_pw_b_2"],
            "sc_b": g["ssm_conv_b_2"], "dt_b": g["dt_bias_2"], "a_log": g["a_log_2"],
            "dskip": np.repeat(g["d_skip_2"][0], 64), "ssm_g": g["ssm_norm_g_2"]}
    cols = {k: columns(v) for k, v in cols.items()}
    cols["dw_w"], cols["sc_w"] = taps(g["conv_dw_w_2"][0]), taps(g["ssm_conv_w_2"][0])
    return {"xT": by_features(g["x"][0]), "memT": by_features(g["mem"][0]), "weights": full, "weights6": six,
            "vectors": np.ascontiguousarray(np.concatenate([cols[n] for n, _ in VEC], 1)), "consts": constants()}


def kernel(**inputs):
    import concourse.bacc as _bacc
    from concourse.bass_utils import run_bass_kernel_spmd as _run

    nc = _bacc.Bacc("TRN2", target_bir_lowering=False, num_devices=1)
    arrays, args = {}, []
    for name, a in lay_out(inputs).items():
        arrays[f"in_{name}"] = a
        args.append(nc.dram_tensor(f"in_{name}", a.shape, mybir.dt.from_np(a.dtype), kind="ExternalInput").ap())
    args.append(nc.dram_tensor("scratch", (NSH, S), F32, kind="Internal").ap())
    args.append(nc.dram_tensor("spill", (P, KT, S), F32, kind="Internal").ap())
    args.append(nc.dram_tensor("out_0", (P, KT * S), F32, kind="ExternalOutput").ap())
    block_kernel(nc, *args)
    r = _run(nc, [arrays], core_ids=[0])
    out = np.asarray(r.results[0]["out_0"]).reshape(P, KT, S).transpose(2, 1, 0).reshape(1, S, D)
    return np.ascontiguousarray(out)
```
